# Optimizing a Trainium2 kernel written in Bass

```python
import math
import jax, jax.numpy as jnp
from jax import lax
import numpy as np

D_MODEL = 1024
BATCH = 1
SEQ = 512
DEPTH = 2

CHUNK = 64
Q_BLOCK = 128
HEAD_DIM = 64
HEADS_FOX = 6
HEADS_SB = 5
HEADS_DSA = 5
IDX_HEADS = 8
IDX_DIM = 64
DSA_TOPK_MAX = 256
D_FF = 4 * D_MODEL
PLE_DIM = 256
ROPE_THETA = 10000.0
LN_EPS = 1e-5
N_BRANCH = 3
NEG = -1e30
DEEPNORM_ALPHA = (2 * DEPTH) ** 0.25
DEEPNORM_BETA = (8 * DEPTH) ** -0.25

W_FOX = HEADS_FOX * HEAD_DIM
W_SB = HEADS_SB * HEAD_DIM
W_DSA = HEADS_DSA * HEAD_DIM
IN_SPLITS = (W_FOX, W_FOX, W_FOX, HEADS_FOX,
             W_SB, W_SB, W_SB,
             W_DSA, HEAD_DIM, HEAD_DIM,
             IDX_HEADS * IDX_DIM, IDX_DIM, IDX_HEADS,
             N_BRANCH * D_MODEL)
C_IN = sum(IN_SPLITS)


def split_cols(h):
    out = []
    o = 0
    for w in IN_SPLITS:
        out.append(h[..., o:o + w])
        o += w
    return out

def layer_norm(x, g, b):
    xf = x.astype(jnp.float32)
    mu = jnp.mean(xf, axis=-1, keepdims=True)
    var = jnp.mean(jnp.square(xf - mu), axis=-1, keepdims=True)
    y = (xf - mu) * lax.rsqrt(var + LN_EPS) * g.astype(jnp.float32) + b.astype(jnp.float32)
    return y.astype(x.dtype)

def rope(x, pos):
    half = x.shape[-1] // 2
    inv = ROPE_THETA ** (-jnp.arange(half, dtype=jnp.float32) / half)
    ang = pos.astype(jnp.float32)[:, None] * inv[None, :]
    cos = jnp.cos(ang)[None, :, None, :].astype(x.dtype)
    sin = jnp.sin(ang)[None, :, None, :].astype(x.dtype)
    x1, x2 = x[..., :half], x[..., half:]
    return jnp.concatenate([x1 * cos - x2 * sin, x2 * cos + x1 * sin], axis=-1)

def to_blocks(a):
    b, s = a.shape[:2]
    return jnp.moveaxis(a.reshape(b, s // Q_BLOCK, Q_BLOCK, *a.shape[2:]), 1, 0)

def from_blocks(a):
    nb, b, qb = a.shape[:3]
    return jnp.moveaxis(a, 0, 1).reshape(b, nb * qb, *a.shape[3:])

def fox_attention(q, k, v, log_f):
    b, s, h, dh = q.shape
    c = jnp.cumsum(log_f, axis=1)
    c_k = jnp.transpose(c, (0, 2, 1))[:, :, None, :]
    kpos = jnp.arange(s)
    scale = dh ** -0.5

    def block(args):
        qb, cb, bi = args
        qpos = bi * Q_BLOCK + jnp.arange(Q_BLOCK)
        logits = jnp.einsum('bqhd,bkhd->bhqk', qb, k).astype(jnp.float32) * scale
        logits = logits + jnp.transpose(cb, (0, 2, 1))[..., None] - c_k
        causal = kpos[None, :] <= qpos[:, None]
        logits = jnp.where(causal, logits, NEG)
        w = jax.nn.softmax(logits, axis=-1)
        return jnp.einsum('bhqk,bkhd->bqhd', w.astype(v.dtype), v)

    out = lax.map(block, (to_blocks(q), to_blocks(c), jnp.arange(s // Q_BLOCK)))
    return from_blocks(out).reshape(b, s, h * dh)

def stick_breaking_attention(q, k, v):
    b, s, h, dh = q.shape
    kpos = jnp.arange(s)
    scale = dh ** -0.5

    def block(args):
        qb, bi = args
        qpos = bi * Q_BLOCK + jnp.arange(Q_BLOCK)
        z = jnp.einsum('bqhd,bkhd->bhqk', qb, k).astype(jnp.float32) * scale
        strict = kpos[None, :] < qpos[:, None]
        log_not = jnp.where(strict, jax.nn.log_sigmoid(-z), 0.0)
        after = lax.cumsum(log_not, axis=3, reverse=True) - log_not
        a = jnp.where(strict, jnp.exp(jax.nn.log_sigmoid(z) + after), 0.0)
        return jnp.einsum('bhqk,bkhd->bqhd', a.astype(v.dtype), v)

    out = lax.map(block, (to_blocks(q), jnp.arange(s // Q_BLOCK)))
    return from_blocks(out).reshape(b, s, h * dh)

def dsa_attention(q, k, v, iq, ik, iw):
    b, s, h, dh = q.shape
    n_sel = min(DSA_TOPK_MAX, s // 4)
    kchunk = jnp.arange(s) // CHUNK
    bidx = jnp.arange(b)[:, None, None]
    scale = dh ** -0.5

    def block(args):
        qb, iqb, iwb, bi = args
        qchunk = (bi * Q_BLOCK + jnp.arange(Q_BLOCK)) // CHUNK
        admiss = kchunk[None, :] <= qchunk[:, None]
        idx_logits = jnp.einsum('bqhd,bkd->bqhk', iqb, ik).astype(jnp.float32)
        score = jnp.einsum('bqh,bqhk->bqk', iwb.astype(jnp.float32), jax.nn.relu(idx_logits))
        score = jnp.where(admiss[None], score, NEG)
        _, sel = lax.top_k(score, n_sel)
        sel_ok = (sel // CHUNK) <= qchunk[None, :, None]
        ks = k[bidx, sel]
        vs = v[bidx, sel]
        logits = jnp.einsum('bqhd,bqnd->bhqn', qb, ks).astype(jnp.float32) * scale
        logits = jnp.where(sel_ok[:, None], logits, NEG)
        w = jax.nn.softmax(logits, axis=-1)
        return jnp.einsum('bhqn,bqnd->bqhd', w.astype(vs.dtype), vs)

    out = lax.map(block, (to_blocks(q), to_blocks(iq), to_blocks(iw), jnp.arange(s // Q_BLOCK)))
    return from_blocks(out).reshape(b, s, h * dh)

def first_inputs(seed: int = 0) -> dict:
    key = jax.random.key(seed)
    ks = jax.random.split(key, 20)
    n = jax.random.normal
    f32 = jnp.float32
    L = DEPTH
    bt = DEEPNORM_BETA
    return {
        'x': n(ks[0], (BATCH, SEQ, D_MODEL), f32),
        'p': n(ks[1], (DEPTH, BATCH, SEQ, PLE_DIM), f32),
        'w_in': n(ks[2], (L, D_MODEL, C_IN), f32) * D_MODEL ** -0.5,
        'b_forget': 2.0 + 0.5 * n(ks[3], (L, HEADS_FOX), f32),
        'w_up_fox': n(ks[4], (L, W_FOX, D_MODEL), f32) * W_FOX ** -0.5 * bt,
        'w_up_sb': n(ks[5], (L, W_SB, D_MODEL), f32) * W_SB ** -0.5 * bt,
        'w_up_dsa': n(ks[6], (L, W_DSA, D_MODEL), f32) * W_DSA ** -0.5 * bt,
        'w_out': n(ks[7], (L, D_MODEL, D_MODEL), f32) * D_MODEL ** -0.5 * bt,
        'ln1_g': 1.0 + 0.05 * n(ks[8], (L, D_MODEL), f32),
        'ln1_b': 0.02 * n(ks[9], (L, D_MODEL), f32),
        'w_ff_in': n(ks[10], (L, D_MODEL, D_FF), f32) * D_MODEL ** -0.5,
        'w_ff_out': n(ks[11], (L, D_FF, D_MODEL), f32) * D_FF ** -0.5 * bt,
        'w_ple': n(ks[12], (L, PLE_DIM, D_MODEL), f32) * PLE_DIM ** -0.5 * bt,
        'w_ple_gate': n(ks[13], (L, D_MODEL, D_MODEL), f32) * D_MODEL ** -0.5,
        'ln2_g': 1.0 + 0.05 * n(ks[14], (L, D_MODEL), f32),
        'ln2_b': 0.02 * n(ks[15], (L, D_MODEL), f32),
    }

def first_block(x, p, w_in, b_forget, w_up_fox, w_up_sb, w_up_dsa, w_out, ln1_g, ln1_b,
              w_ff_in, w_ff_out, w_ple, w_ple_gate, ln2_g, ln2_b):
    b, s, _ = x.shape
    pos = jnp.arange(s)
    for i in range(DEPTH):
        h = x @ w_in[i]
        (fq, fk, fv, ff_logit, sq, sk, sv, dq, dk, dv, iq, ik, iw, g) = split_cols(h)
        fq = fq.reshape(b, s, HEADS_FOX, HEAD_DIM)
        fk = fk.reshape(b, s, HEADS_FOX, HEAD_DIM)
        fv = fv.reshape(b, s, HEADS_FOX, HEAD_DIM)
        log_f = jax.nn.log_sigmoid(ff_logit.astype(jnp.float32) + b_forget[i].astype(jnp.float32))
        o_fox = fox_attention(fq, fk, fv, log_f)

        o_sb = stick_breaking_attention(sq.reshape(b, s, HEADS_SB, HEAD_DIM),
                                        sk.reshape(b, s, HEADS_SB, HEAD_DIM),
                                        sv.reshape(b, s, HEADS_SB, HEAD_DIM))

        dq = rope(dq.reshape(b, s, HEADS_DSA, HEAD_DIM), pos)
        dk = rope(dk[:, :, None, :], pos)[:, :, 0, :]
        iq = rope(iq.reshape(b, s, IDX_HEADS, IDX_DIM), pos)
        ik = rope(ik[:, :, None, :], pos)[:, :, 0, :]
        o_dsa = dsa_attention(dq, dk, dv, iq, ik, iw)

        gates = jax.nn.sigmoid(g.reshape(b, s, N_BRANCH, D_MODEL))
        merged = (gates[:, :, 0] * (o_fox @ w_up_fox[i])
                  + gates[:, :, 1] * (o_sb @ w_up_sb[i])
                  + gates[:, :, 2] * (o_dsa @ w_up_dsa[i]))
        x = layer_norm(DEEPNORM_ALPHA * x + merged @ w_out[i], ln1_g[i], ln1_b[i])

        ffn = jnp.square(jax.nn.relu(x @ w_ff_in[i])) @ w_ff_out[i]
        ple = jax.nn.sigmoid(x @ w_ple_gate[i]) * (p[i] @ w_ple[i])
        x = layer_norm(DEEPNORM_ALPHA * x + ffn + ple, ln2_g[i], ln2_b[i])
    return x


D_NSA = 512
D_LRU = 512
D_CONV = 512
D_MIX = D_NSA + D_LRU + D_CONV
N_HEADS = D_NSA // HEAD_DIM
N_KV = 2
N_REP = N_HEADS // N_KV
KV_W = N_KV * HEAD_DIM
L_CMP = 32
S_CMP = 16
CMP_HIDDEN = 256
L_SLC = 64
K_SEL = 16
WINDOW = 512
LRU_BLOCKS = 8
LRU_BLOCK_W = D_LRU // LRU_BLOCKS
LRU_CONV = 4
LRU_C = 8.0
CONV_K = 31
EPS = 1e-6
NEG_2 = -1e30
FORCE = 1e4
COL_SIZES = (D_NSA, KV_W, KV_W, KV_W, KV_W, KV_W, KV_W, N_HEADS * N_BRANCH,
             D_NSA, D_LRU, D_LRU, D_CONV, D_CONV, D_CONV)
N_IN = D_NSA * 2 + KV_W * 6 + N_HEADS * N_BRANCH + D_LRU * 2 + D_CONV * 3


def split_points():
    return [int(v) for v in np.cumsum(COL_SIZES)[:-1]]

def rms_norm(x, g):
    xf = x.astype(jnp.float32)
    y = xf * lax.rsqrt(jnp.mean(xf * xf, axis=-1, keepdims=True) + EPS)
    return (y * g.astype(jnp.float32)).astype(x.dtype)

def rope_tables(positions):
    inv_freq = ROPE_THETA ** (-jnp.arange(0, HEAD_DIM, 2, dtype=jnp.float32) / HEAD_DIM)
    ang = positions.astype(jnp.float32)[..., None] * inv_freq
    return jnp.cos(ang)[:, :, None, :], jnp.sin(ang)[:, :, None, :]

def apply_rope(u, cos, sin):
    uf = u.astype(jnp.float32)
    u1, u2 = jnp.split(uf, 2, axis=-1)
    out = jnp.concatenate([u1 * cos - u2 * sin, u2 * cos + u1 * sin], axis=-1)
    return out.astype(u.dtype)

def causal_dwconv(u, w, b):
    k = w.shape[0]
    c = u.shape[-1]
    y = lax.conv_general_dilated(u, w[:, None, :].astype(u.dtype), window_strides=(1,),
                                 padding=[(k - 1, 0)], dimension_numbers=('NWC', 'WIO', 'NWC'),
                                 feature_group_count=c)
    return y + b

def nsa_attention(q, k_c, v_c, k_s, v_s, k_w, v_w, gates, cmp_pos, cmp_w1, cmp_w2):
    B, T = q.shape[0], q.shape[1]
    qg = q.reshape(B, T, N_KV, N_REP, HEAD_DIM).transpose(0, 2, 3, 1, 4)
    tr = lambda a: a.transpose(0, 2, 1, 3)
    k_c, v_c, k_s, v_s, k_w, v_w = tr(k_c), tr(v_c), tr(k_s), tr(v_s), tr(k_w), tr(v_w)

    n_cmp = (T - L_CMP) // S_CMP + 1
    cmp_start = jnp.arange(n_cmp) * S_CMP
    idx = cmp_start[:, None] + jnp.arange(L_CMP)[None, :]

    def compress(kv, pos, w1, w2):
        blk = (kv[:, :, idx] + pos).reshape(B, N_KV, n_cmp, L_CMP * HEAD_DIM)
        return jax.nn.silu(blk @ w1) @ w2

    kc = compress(k_c, cmp_pos[0], cmp_w1[0], cmp_w2[0])
    vc = compress(v_c, cmp_pos[1], cmp_w1[1], cmp_w2[1])
    cmp_end = cmp_start + L_CMP - 1

    n_sel = T // L_SLC
    k_sel = min(K_SEL, n_sel)
    sel_start = jnp.arange(n_sel) * L_SLC
    overlap = ((cmp_start[:, None] < sel_start[None, :] + L_SLC) &
               (cmp_start[:, None] + L_CMP > sel_start[None, :])).astype(jnp.float32)
    ks_blk = k_s.reshape(B, N_KV, n_sel, L_SLC, HEAD_DIM)
    vs_blk = v_s.reshape(B, N_KV, n_sel, L_SLC, HEAD_DIM)
    bi = jnp.arange(B)[:, None, None, None]
    gi = jnp.arange(N_KV)[None, :, None, None]
    sel_j = jnp.arange(n_sel)

    pad = ((0, 0), (0, 0), (WINDOW, 0), (0, 0))
    kw_pad = jnp.pad(k_w, pad)
    vw_pad = jnp.pad(v_w, pad)
    scale = HEAD_DIM ** -0.5

    def block(i):
        s = i * Q_BLOCK
        qb = lax.dynamic_slice_in_dim(qg, s, Q_BLOCK, axis=3)
        t = s + jnp.arange(Q_BLOCK)
        sc = jnp.einsum('bgrqd,bgnd->bgrqn', qb, kc).astype(jnp.float32) * scale
        mc = cmp_end[None, :] <= t[:, None]
        pc = jnp.where(mc, jax.nn.softmax(jnp.where(mc, sc, NEG_2), axis=-1), 0.0)
        o_c = jnp.einsum('bgrqn,bgnd->bgrqd', pc.astype(vc.dtype), vc)
        imp = jnp.einsum('bgrqn,ns->bgqs', pc, overlap)
        cur = t // L_SLC
        forced = ((sel_j[None, :] == 0) | (sel_j[None, :] == cur[:, None]) |
                  (sel_j[None, :] == cur[:, None] - 1))
        valid = sel_start[None, :] <= t[:, None]
        score = jnp.where(forced, FORCE, jnp.where(valid, imp, -1.0))
        top_v, top_i = lax.top_k(score, k_sel)
        ok = top_v >= 0.0
        kg = ks_blk[bi, gi, top_i]
        vg = vs_blk[bi, gi, top_i]
        ss = jnp.einsum('bgrqd,bgqkld->bgrqkl', qb, kg).astype(jnp.float32) * scale
        tok = top_i[..., None] * L_SLC + jnp.arange(L_SLC)
        ms = (ok[..., None] & (tok <= t[None, None, :, None, None]))[:, :, None]
        ss = jnp.where(ms, ss, NEG_2).reshape(B, N_KV, N_REP, Q_BLOCK, k_sel * L_SLC)
        ps = jax.nn.softmax(ss, axis=-1).reshape(B, N_KV, N_REP, Q_BLOCK, k_sel, L_SLC)
        o_s = jnp.einsum('bgrqkl,bgqkld->bgrqd', ps.astype(vg.dtype), vg)
        kw = lax.dynamic_slice_in_dim(kw_pad, s, WINDOW + Q_BLOCK, axis=2)
        vw = lax.dynamic_slice_in_dim(vw_pad, s, WINDOW + Q_BLOCK, axis=2)
        pos = s - WINDOW + jnp.arange(WINDOW + Q_BLOCK)
        mw = ((pos[None, :] <= t[:, None]) & (pos[None, :] > t[:, None] - WINDOW) &
              (pos[None, :] >= 0))
        sw = jnp.einsum('bgrqd,bgkd->bgrqk', qb, kw).astype(jnp.float32) * scale
        pw = jax.nn.softmax(jnp.where(mw, sw, NEG_2), axis=-1)
        o_w = jnp.einsum('bgrqk,bgkd->bgrqd', pw.astype(vw.dtype), vw)
        return o_c, o_s, o_w

    o_c, o_s, o_w = lax.map(block, jnp.arange(T // Q_BLOCK))

    def unblock(o):
        return o.transpose(1, 0, 4, 2, 3, 5).reshape(B, T, N_KV, N_REP, HEAD_DIM)

    g = gates.reshape(B, T, N_KV, N_REP, N_BRANCH)
    out = g[..., 0:1] * unblock(o_c) + g[..., 1:2] * unblock(o_s) + g[..., 2:3] * unblock(o_w)
    return out.reshape(B, T, D_NSA)

def rg_lru(u, conv_w, conv_b, w_a, b_a, w_i, b_i, lam):
    B, T, C = u.shape
    xc = causal_dwconv(u, conv_w, conv_b)
    xh = xc.reshape(B, T, LRU_BLOCKS, LRU_BLOCK_W)
    r = jax.nn.sigmoid(jnp.einsum('bthi,hij->bthj', xh, w_a).reshape(B, T, C) + b_a)
    ig = jax.nn.sigmoid(jnp.einsum('bthi,hij->bthj', xh, w_i).reshape(B, T, C) + b_i)
    log_a = -LRU_C * r.astype(jnp.float32) * jax.nn.softplus(-lam.astype(jnp.float32))
    a = jnp.exp(log_a)
    bterm = jnp.sqrt(-jnp.expm1(2.0 * log_a)) * (ig * xc).astype(jnp.float32)

    def combine(left, right):
        a1, b1 = left
        a2, b2 = right
        return a1 * a2, a2 * b1 + b2

    _, h = lax.associative_scan(combine, (a, bterm), axis=1)
    return h.astype(u.dtype)

def conformer_conv(ga, gb, dw_w, dw_b, ln_g, ln_b, w_pw2):
    u = ga * jax.nn.sigmoid(gb)
    u = causal_dwconv(u, dw_w, dw_b)
    uf = u.astype(jnp.float32)
    mu = jnp.mean(uf, axis=-1, keepdims=True)
    var = jnp.mean(jnp.square(uf - mu), axis=-1, keepdims=True)
    un = (uf - mu) * lax.rsqrt(var + EPS) * ln_g.astype(jnp.float32) + ln_b.astype(jnp.float32)
    return jax.nn.silu(un).astype(u.dtype) @ w_pw2

def second_inputs(seed: int = 0) -> dict:
    key = jax.random.key(seed)
    ks = jax.random.split(key, 24)
    f32 = jnp.float32
    nrm = lambda k, shape, s: jax.random.normal(k, shape, f32) * s
    u = jax.random.uniform(ks[13], (DEPTH, D_LRU), f32, 0.9, 0.999)
    sg = u ** (1.0 / LRU_C)
    lam = jnp.log(sg / (1.0 - sg))
    return {
        "x": jax.random.normal(ks[0], (BATCH, SEQ, D_MODEL), f32),
        "positions": jnp.broadcast_to(jnp.arange(SEQ, dtype=jnp.int32), (BATCH, SEQ)),
        "norm_g": 1.0 + nrm(ks[1], (DEPTH, D_MODEL), 0.02),
        "w_in": nrm(ks[2], (DEPTH, D_MODEL, N_IN), D_MODEL ** -0.5),
        "b_gate": nrm(ks[3], (DEPTH, N_HEADS * N_BRANCH), 0.02),
        "cmp_pos": nrm(ks[4], (DEPTH, 2, L_CMP, HEAD_DIM), 0.02),
        "cmp_w1": nrm(ks[5], (DEPTH, 2, L_CMP * HEAD_DIM, CMP_HIDDEN), (L_CMP * HEAD_DIM) ** -0.5),
        "cmp_w2": nrm(ks[6], (DEPTH, 2, CMP_HIDDEN, HEAD_DIM), CMP_HIDDEN ** -0.5),
        "lru_conv_w": nrm(ks[7], (DEPTH, LRU_CONV, D_LRU), LRU_CONV ** -0.5),
        "lru_conv_b": nrm(ks[8], (DEPTH, D_LRU), 0.02),
        "lru_w_a": nrm(ks[9], (DEPTH, LRU_BLOCKS, LRU_BLOCK_W, LRU_BLOCK_W), LRU_BLOCK_W ** -0.5),
        "lru_b_a": nrm(ks[10], (DEPTH, D_LRU), 0.02),
        "lru_w_i": nrm(ks[11], (DEPTH, LRU_BLOCKS, LRU_BLOCK_W, LRU_BLOCK_W), LRU_BLOCK_W ** -0.5),
        "lru_b_i": nrm(ks[12], (DEPTH, D_LRU), 0.02),
        "lru_lam": lam,
        "conv_dw_w": nrm(ks[14], (DEPTH, CONV_K, D_CONV), CONV_K ** -0.5),
        "conv_dw_b": nrm(ks[15], (DEPTH, D_CONV), 0.02),
        "conv_ln_g": 1.0 + nrm(ks[16], (DEPTH, D_CONV), 0.02),
        "conv_ln_b": nrm(ks[17], (DEPTH, D_CONV), 0.02),
        "conv_w_pw2": nrm(ks[18], (DEPTH, D_CONV, D_CONV), D_CONV ** -0.5),
        "w_out": nrm(ks[19], (DEPTH, D_MIX, D_MODEL), D_MIX ** -0.5),
        "final_g": 1.0 + nrm(ks[20], (D_MODEL,), 0.02),
    }

def second_block(x, positions, norm_g, w_in, b_gate, cmp_pos, cmp_w1, cmp_w2, lru_conv_w, lru_conv_b,
              lru_w_a, lru_b_a, lru_w_i, lru_b_i, lru_lam, conv_dw_w, conv_dw_b, conv_ln_g, conv_ln_b,
              conv_w_pw2, w_out, final_g):
    B, T = x.shape[0], x.shape[1]
    cos, sin = rope_tables(positions)
    for l in range(DEPTH):
        h = rms_norm(x, norm_g[l])
        proj = h @ w_in[l]
        (q, k_c, v_c, k_s, v_s, k_w, v_w, g_lin, z_nsa, u_lru, z_lru, glu_a, glu_b,
         z_conv) = jnp.split(proj, split_points(), axis=-1)
        kvr = lambda a: a.reshape(B, T, N_KV, HEAD_DIM)
        q = apply_rope(q.reshape(B, T, N_HEADS, HEAD_DIM), cos, sin)
        k_c = apply_rope(kvr(k_c), cos, sin)
        k_s = apply_rope(kvr(k_s), cos, sin)
        k_w = apply_rope(kvr(k_w), cos, sin)
        gates = jax.nn.sigmoid(g_lin + b_gate[l]).reshape(B, T, N_HEADS, N_BRANCH)
        y_nsa = nsa_attention(q, k_c, kvr(v_c), k_s, kvr(v_s), k_w, kvr(v_w), gates,
                              cmp_pos[l], cmp_w1[l], cmp_w2[l])
        y_lru = rg_lru(u_lru, lru_conv_w[l], lru_conv_b[l], lru_w_a[l], lru_b_a[l],
                       lru_w_i[l], lru_b_i[l], lru_lam[l])
        y_conv = conformer_conv(glu_a, glu_b, conv_dw_w[l], conv_dw_b[l], conv_ln_g[l],
                                conv_ln_b[l], conv_w_pw2[l])
        mixed = jnp.concatenate([y_nsa * jax.nn.silu(z_nsa), y_lru * jax.nn.silu(z_lru),
                                 y_conv * jax.nn.silu(z_conv)], axis=-1)
        x = x + mixed @ w_out[l]
    return rms_norm(x, final_g)


def setup_inputs(seed=0):
    out = dict(first_inputs(seed))
    for name, value in second_inputs(seed + 1).items():
        if name != "x":
            out[name + "_2"] = value
    return out


def reference(
    x, p, w_in, b_forget, w_up_fox, w_up_sb, w_up_dsa, w_out, ln1_g, ln1_b, w_ff_in, w_ff_out,
    w_ple, w_ple_gate, ln2_g, ln2_b, positions_2, norm_g_2, w_in_2, b_gate_2, cmp_pos_2,
    cmp_w1_2, cmp_w2_2, lru_conv_w_2, lru_conv_b_2, lru_w_a_2, lru_b_a_2, lru_w_i_2, lru_b_i_2,
    lru_lam_2, conv_dw_w_2, conv_dw_b_2, conv_ln_g_2, conv_ln_b_2, conv_w_pw2_2, w_out_2,
    final_g_2,
):
    x = first_block(
        x, p, w_in, b_forget, w_up_fox, w_up_sb, w_up_dsa, w_out, ln1_g, ln1_b, w_ff_in,
        w_ff_out, w_ple, w_ple_gate, ln2_g, ln2_b,
    )
    return second_block(
        x, positions_2, norm_g_2, w_in_2, b_gate_2, cmp_pos_2, cmp_w1_2, cmp_w2_2, lru_conv_w_2,
        lru_conv_b_2, lru_w_a_2, lru_b_a_2, lru_w_i_2, lru_b_i_2, lru_lam_2, conv_dw_w_2,
        conv_dw_b_2, conv_ln_g_2, conv_ln_b_2, conv_w_pw2_2, w_out_2, final_g_2,
    )


_drawn_inputs = setup_inputs


def setup_inputs(seed=0):
    import zlib

    import numpy as np

    out = dict(_drawn_inputs(seed))
    spreads = {}
    factors = {'b_forget': 2.748,
     'norm_g_2': 3.154,
     'b_gate_2': 22.011,
     'cmp_pos_2': 8.0,
     'lru_b_a_2': 25.983,
     'lru_b_i_2': 8.0,
     'conv_dw_b_2': 5.063,
     'conv_ln_g_2': 8.0,
     'conv_ln_b_2': 8.0,
     'final_g_2': 8.051,
     'lru_conv_b_2': 2.795}
    for name, (base, spread) in spreads.items():
        noise = np.random.default_rng([zlib.crc32(name.encode()), seed]).standard_normal(out[name].shape)
        drawn = base * np.exp(spread * noise) if base else spread * noise
        out[name] = __import__('jax').numpy.asarray(drawn.astype(out[name].dtype))
    for name, factor in factors.items():
        out[name] = (out[name] * factor).astype(out[name].dtype)
    return out
```

```python
from contextlib import ExitStack
import math

import numpy as np

import concourse.bass as bass
from concourse import mybir

F32 = mybir.dt.float32
F32R = mybir.dt.float32r
BF16 = mybir.dt.bfloat16
I32 = mybir.dt.int32
ALU = mybir.AluOpType
ACT = mybir.ActivationFunctionType
AX = mybir.AxisListType.X

P = 128
SEQ = 512
D = 1024
KT = D // P
QB = SEQ // P
HD = 64
SLOTS = 4
DEPTH = 2
NEG = -1e30
MARK = -3e38
ALPHA = (2 * DEPTH) ** 0.25
LN_EPS = 1e-5
TOPK = 128
IDX_HEADS = 8

A_FQ, A_SQ, A_FK, A_SK, A_FV, A_SV, A_SDV = 0, 3, 5, 8, 10, 13, 15
A_IKF, A_S4D4Q, A_S4KDK, A_DKIK, A_DQ, A_IQ = 16, 17, 18, 19, 20, 22
A_NPROJ = 26
A_GFOX = A_NPROJ
A_MIX = A_GFOX + KT
A_OUT = A_MIX + 3 * KT
A_FFN = A_OUT + KT
A_PLE = A_FFN + 64
A_PG = A_PLE + 2
A_UNITS = A_PG + KT
assert A_UNITS % SLOTS == 0
A_GROUPS = A_UNITS // SLOTS
A_VT = 10
A_NVT = 7
V_FOX, V_SB, V_S4, V_DSA, V_IW = 0, 384, 640, 704, 6 * P + 72

C_ID, C_ROT, C_TRI, C_CAUS, C_STRICT, C_ST01, C_CHUNK = (P * n for n in range(7))
C_QA = 7 * P
C_QB = C_QA + 6
C_KA = C_QB + 6
C_KB = C_KA + 1
C_N = C_KB + 1

PA_G1, PA_B1, PA_G2, PA_B2, PA_BF, PA_N = 0, 8, 16, 24, 32, 33

B_GA, B_GB, B_U, B_ZL, B_ZC, B_ZN, B_Q, B_KV, B_G = 0, 4, 8, 12, 16, 20, 24, 28, 34
B_BD = 35
B_CMP1 = 36
B_CMP2 = 44
B_PW2 = 46
B_OUTL, B_OUTC, B_OUTN = 48, 52, 56
B_UNITS = 60
B_GROUPS = B_UNITS // SLOTS
B_HEADS, B_REP = 8, 4
CONV_K, LRU_K = 31, 4
UC_W, UP_W = CONV_K - 1 + SEQ, LRU_K - 1 + SEQ
NBLK = 31
NB2 = 2 * NBLK
RMS_EPS = 1e-6
PB_G, PB_BG, PB_BA, PB_BI, PB_LAM, PB_LCW, PB_LCB = 0, 8, 9, 13, 17, 21, 37
PB_DW, PB_DWB, PB_LNG, PB_LNB, PB_POS, PB_N = 41, 165, 169, 173, 177, 209
PB_FINAL, PB_INV = DEPTH * PB_N, DEPTH * PB_N + KT


class Plan:
    pass


def plan(nc, ctx):
    S = Plan()
    S.nc = nc
    base = -(-nc.sbuf_base // 64) * 64

    def at(name, shape, dt, kb):
        return nc.alloc_sbuf_tensor_at(name, shape, dt, offset=base + int(kb * 1024))

    W = KT * P
    WK = 187.75
    S.raw = [at(f"w_raw{s}", [P, W], F32, 4 * s) for s in range(SLOTS)]
    S.wh = [at(f"w_hi{s}", [P, W], F32R, 16 + 4 * s) for s in range(SLOTS)]
    S.wl = [at(f"w_lo{s}", [P, W], F32R, 32 + 4 * s) for s in range(SLOTS)]
    S.xh = at("x_hi", [P, KT * SEQ], F32R, 48)
    S.xl = at("x_lo", [P, KT * SEQ], F32R, 64)
    S.gfox = at("gate_fox", [P, KT * SEQ], F32, 80)
    S.t = at("ln_in", [P, KT * SEQ], F32, 80)
    S.plep = at("ple_proj", [P, KT * SEQ], F32, 80)
    S.qkv = at("proj", [P, A_NPROJ * SEQ], F32, 96)
    S.rh = at("rhs_hi", [P, KT * SEQ], F32R, 96)
    S.rl = at("rhs_lo", [P, KT * SEQ], F32R, 112)
    S.ml = at("merged_lo", [P, KT * SEQ], F32R, 128)
    S.yacc = at("ffn_sum", [P, KT * SEQ], F32, 128)
    S.r = [at(f"idx_relu{e}", [P, SEQ], F32, 116 + 2 * e) for e in range(2)]
    S.score = at("idx_score", [P, 9 * P], F32, 120)
    S.sp = at("softplus_sum", [P, 10 * P], F32, 116)
    S.nz0 = at("neg_abs", [P, SEQ], F32, 121)
    S.dmask = at("sparse_mask", [P, 9 * P], BF16, 124.5)
    S.vt = at("v_tok", [P, QB * A_NVT * P], F32, 148)
    S.praw = at("p_raw", [P, 2 * SEQ], F32, 148)
    S.ph = at("p_hi", [P, 2 * SEQ], F32R, 152)
    S.pl = at("p_lo", [P, 2 * SEQ], F32R, 156)
    S.otok = at("o_tok", [P, QB * D], F32, 162)
    S.mh = at("merged_hi", [P, KT * SEQ], F32R, 162)
    S.cos = at("cos", [P, SEQ], F32, 178)
    S.sin = at("sin", [P, SEQ], F32, 180)
    S.con = at("constants", [P, C_N], F32, 182)
    S.ones = at("ones", [P, P], F32, 185.75)
    S.negones = at("neg_ones", [P, P], F32, 186.25)
    S.idb = at("ident_bf", [P, P], BF16, 186.75)
    S.causb = at("causal_bf", [P, P], BF16, 187)
    S.strictb = at("strict_bf", [P, P], BF16, 187.25)
    S.chunkb = at("chunk_bf", [P, P], BF16, 187.5)
    S.wk = [at(f"work{n}", [P, SEQ], F32, WK + 2 * n) for n in range(8)]
    S.stk_w = at("stick_weights", [P, 10 * P], F32, WK + 8)
    S.c = at("log_f_sum", [P, SEQ], F32, WK + 16)
    o = [(WK + 18) * 1024]

    def small(name, n, dt=F32):
        o[0] += 4 * n
        return nc.alloc_sbuf_tensor_at(name, [P, n], dt, offset=base + int(o[0] - 4 * n), align_bytes=4)

    S.prmA = small("params_a", DEPTH * PA_N)
    S.cur = small("params_cur", PA_N)
    S.nm = [small(f"neg_max{e}", 1) for e in range(2)]
    S.rs = [small(f"row_sum{e}", 1) for e in range(2)]
    S.rinv = [small(f"row_inv{e}", 1) for e in range(2)]
    S.top = [small(f"top8_{b}", 8) for b in range(3)]
    S.tick = small("tick", 32)
    S.eps = small("ln_eps", 1)
    S.res = at("residual", [P, KT * SEQ], F32, 80)
    S.q = at("b_q", [P, 4 * SEQ], F32, 96)
    S.kv = {n: at(f"b_{n}", [P, SEQ], F32, 104 + 2 * i) for i, n in enumerate(("kc", "ks", "kw", "vc", "vs", "vw", "gl"))}
    S.vbd = at("cmp_values", [P, 2 * 4 * HD], F32, 104)
    S.vtok = {"s": at("b_vs_tok", [P, SEQ], F32, 174.75), "w": at("b_vw_tok", [P, SEQ], F32, 112)}
    S.gate = at("b_gate_tok", [P, QB * 3 * B_HEADS], F32, 116)
    S.cmx, S.csum = (at(f"cmp_{n}", [P, QB * B_HEADS], F32, 116.5 + d) for n, d in (("max", 0), ("sum", 0.25)))
    S.mnh, S.mnl = at("nsa_hi", [P, 4 * SEQ], F32R, 96), at("nsa_lo", [P, 4 * SEQ], F32R, 104)
    S.zl, S.zc, S.zn = (at(f"silu_z_{n}", [P, 4 * SEQ], F32, 118 + 8 * i) for i, n in enumerate(("lru", "conv", "nsa")))
    S.uc = at("glu_out", [P, 4 * UC_W], F32, 142)
    S.ls = at("lru_tanh", [P, 4 * SEQ], F32, 142)
    S.ot2 = at("b_o_tok", [P, QB * 512], F32, 142)
    S.cacc = at("conv_sum", [P, 4 * SEQ], F32, 150.5)
    S.up = at("lru_in", [P, 4 * UP_W], F32, 158.5)
    S.la = at("lru_log_a", [P, 4 * SEQ], F32, 158.5)
    S.mch = at("conv_hi", [P, 4 * SEQ], F32R, 158.5)
    S.xc = at("lru_conv", [P, 4 * SEQ], F32, 166.75)
    S.mcl = at("conv_lo", [P, 4 * SEQ], F32R, 166.75)
    S.hkh, S.hkl = (at(f"cmp_hid_k_{n}", [P, 2 * NB2], F32R, 176.75 + d) for n, d in (("hi", 0), ("lo", 0.5)))
    S.kcb = at("cmp_keys", [P, HD], F32, 177.75)
    S.blk = [at(f"cmp_blocks_{n}", [P, 16 * NB2], F32, WK + 4 * i) for i, n in enumerate("kv")]
    S.lri, S.lrt = at("lru_i", [P, 4 * SEQ], F32, WK), at("lru_tmp", [P, 4 * SEQ], F32, WK + 8)
    S.hvh, S.hvl = (at(f"cmp_hid_v_{n}", [P, SEQ], F32R, WK + 2 * i) for i, n in ((1, "hi"), (2, "lo")))
    S.pos = at("positions", [P, SEQ], I32, WK + 8)
    S.prmB = at("params_b", [P, SEQ], F32, WK + 16)
    S.cmask = small("cmp_mask", QB * 32)
    S.curB = small("params_b_cur", PB_N)
    S.lam = [small(f"lam{n}", 4) for n in range(5)]
    S.rg = [small(f"gate_inv{e}", 1) for e in range(2)]
    S.eps2, S.halfpi = small("rms_eps", 1), small("half_pi", 1)

    S.ps = [nc.alloc_psum_tensor(f"bank{n}", [P, SEQ], F32) for n in range(8)]
    S.X = S.ps[4:]

    def sem(name):
        return ctx.enter_context(nc.semaphore(name))

    def ring(name):
        return [sem(f"{name}{s}") for s in range(SLOTS)]

    S.raw_landed, S.hi_ready, S.lo_ready = ring("raw_landed"), ring("hi_ready"), ring("lo_ready")
    S.unit_done, S.bank_free = ring("unit_done"), ring("bank_free")
    S.sem = sem
    S.con_landed = sem("con_landed")
    S.x_ready = sem("x_ready")
    S.scaled = sem("scaled")
    S.rot_ready = sem("rot_ready")
    S.rope_done = sem("rope_done")
    S.vt_ready = sem("vt_ready")
    S.vt_done = sem("vt_done")
    S.logf_in = sem("logf_in")
    S.logf_out = sem("logf_out")
    S.idx_ready = sem("idx_ready")
    S.relu_done = sem("relu_done")
    S.idx_acc = sem("idx_acc")
    S.mask_ready = sem("mask_ready")
    S.fox_staged = sem("fox_staged")
    S.fox_aug = sem("fox_aug")
    S.s_staged = sem("s_staged")
    S.d_staged = sem("d_staged")
    S.stk_z = sem("stk_z")
    S.stk_na = sem("stk_na")
    S.stk_ln = sem("stk_ln")
    S.stk_sp = sem("stk_sp")
    S.stk_c = sem("stk_c")
    S.stk_a = sem("stk_a")
    S.stk_o = sem("stk_o")
    S.stk_oev = sem("stk_oev")
    S.ot_ready = sem("ot_ready")
    S.ot_hi = sem("ot_hi")
    S.ot_done = sem("ot_done")
    S.merge_x = sem("merge_x")
    S.merge_done = sem("merge_done")
    S.t_ready = sem("t_ready")
    S.ln_mean = sem("ln_mean")
    S.ln_d = sem("ln_d")
    S.ln_sq = sem("ln_sq")
    S.ln_var = sem("ln_var")
    S.ln_std = sem("ln_std")
    S.ln_y = sem("ln_y")
    S.ln_hi = sem("ln_hi")
    S.ffn_act = sem("ffn_act")
    S.ffn_h = sem("ffn_h")
    S.p_landed = sem("p_landed")
    S.p_ready = sem("p_ready")
    S.y_ready = sem("y_ready")
    S.out_done = sem("out_done")
    S.pb_landed = sem("pb_landed")
    S.ang_ready = sem("ang_ready")
    S.tab_ready = sem("tab_ready")
    S.res_ready = sem("res_ready")
    S.rms_sq = sem("rms_sq")
    S.rms_var = sem("rms_var")
    S.rms_std = sem("rms_std")
    S.rms_y = sem("rms_y")
    S.rms_hi = sem("rms_hi")
    S.lam_in = sem("lam_in")
    S.lam_out = sem("lam_out")
    S.glu_done = sem("glu_done")
    S.bvt_ready = sem("bvt_ready")
    S.bvt_done = sem("bvt_done")
    S.gl_done = sem("gl_done")
    S.b_rot_ready = sem("b_rot_ready")
    S.b_rope_done = sem("b_rope_done")
    S.xc_split = sem("xc_split")
    S.lru_ready = sem("lru_ready")
    S.lru_gate = sem("lru_gate")
    S.nla_ready = sem("nla_ready")
    S.s_ready = sem("s_ready")
    S.a_ready = sem("a_ready")
    S.b2_ready = sem("b2_ready")
    S.beta_ready = sem("beta_ready")
    S.lru_done = sem("lru_done")
    S.blk_raw = sem("blk_raw")
    S.blk_ready = sem("blk_ready")
    S.hid_act = sem("hid_act")
    S.hid_split = sem("hid_split")
    S.kcb_ready = sem("kcb_ready")
    S.vbd_ready = sem("vbd_ready")
    S.cs_ready = sem("cs_ready")
    S.cexp_in = sem("cexp_in")
    S.cexp_out = sem("cexp_out")
    S.cp_ready = sem("cp_ready")
    S.cpt_ready = sem("cpt_ready")
    S.cpt_copied = sem("cpt_copied")
    S.oc_ready = sem("oc_ready")
    S.oc_done = sem("oc_done")
    S.dw_done = sem("dw_done")
    S.cl_mean = sem("cl_mean")
    S.cl_d = sem("cl_d")
    S.cl_sq = sem("cl_sq")
    S.cl_var = sem("cl_var")
    S.cl_std = sem("cl_std")
    S.cl_y = sem("cl_y")
    S.cl_hi = sem("cl_hi")
    S.un_ready = sem("un_ready")
    S.mc_y = sem("mc_y")
    S.mc_hi = sem("mc_hi")
    S.mc_ready = sem("mc_ready")
    S.q_staged = sem("q_staged")
    S.bt_ready = sem("bt_ready")
    S.mn_y = sem("mn_y")
    S.mn_hi = sem("mn_hi")
    S.mn_ready = sem("mn_ready")
    S.y_done = sem("y_done")
    S.nsa = SoftmaxSems(sem, "nsa")
    S.fox = SoftmaxSems(sem, "fox")
    S.dsa = SoftmaxSems(sem, "dsa")
    return S


class SoftmaxSems:

    def __init__(self, sem, stage):
        self.s = sem(f"{stage}_scores")
        self.max = sem(f"{stage}_max")
        self.p = sem(f"{stage}_probs")
        self.pt = sem(f"{stage}_turned")
        self.ptc = sem(f"{stage}_turned_copied")
        self.o = sem(f"{stage}_out_ready")
        self.out = sem(f"{stage}_out_used")


class Step:

    def __init__(self, b, qk, v, norm, scale=None):
        self.b = b
        self.qk = qk
        self.v = v
        self.norm = norm
        self.scale = scale


def cols(t, j, n=SEQ, w=None):
    w = n if w is None else w
    return t[:, j * n:j * n + w] if isinstance(j, int) else t[:, bass.ds(j * n, w)]


def pe_unit(S, pe, u, g, out, rh, rl):
    s = u % SLOTS
    pe.wait_ge(S.lo_ready[s], g + 1)
    pe.wait_ge(S.bank_free[s], g + 1)
    for k in range(KT):
        pe_tile(S, s, k, out, rh, rl, k, k == 0, k == KT - 1)
    return S.last


def pe_tile(S, s, w, out, rh, rl, k, first, last, lo=0, hi=P):
    nc = S.nc
    wh, wl = (t[s][lo:hi, w * P:(w + 1) * P] for t in (S.wh, S.wl))
    xh, xl = (t[lo:hi, k * SEQ:(k + 1) * SEQ] for t in (rh, rl))
    nc.tensor.matmul(out, wh, xh, start=first, stop=False)
    nc.tensor.matmul(out, wh, xl, start=False, stop=False)
    S.last = nc.tensor.matmul(out, wl, xh, start=False, stop=last)


def act_split(S, act, u, g):
    s = u % SLOTS
    act.wait_ge(S.raw_landed[s], 16 * (g + 2))
    S.nc.scalar.activation(S.wh[s][:, :], S.raw[s][:, :], ACT.Copy).then_inc(S.hi_ready[s], 1)


def sp_stream(S, sp, w_dram, groups):
    for s in range(SLOTS):
        sp.dma_start(S.raw[s][:, :], w_dram[s]).then_inc(S.raw_landed[s], 16)
    with sp.Fori(1, groups) as g:
        for s in range(SLOTS):
            sp.wait_ge(S.lo_ready[s], g)
            src = w_dram[bass.ds(g * SLOTS + s, 1), :, :].rearrange("a p n -> (a p) n")
            sp.dma_start(S.raw[s][:, :], src).then_inc(S.raw_landed[s], 16)


def pool_split(S, pool, groups):
    with pool.Fori(0, groups) as g:
        for s in range(SLOTS):
            pool.wait_ge(S.hi_ready[s], g + 1)
            S.nc.gpsimd.tensor_tensor(S.wl[s][:, :], S.raw[s][:, :], S.wh[s][:, :].bitcast(F32),
                                      ALU.subtract).then_inc(S.lo_ready[s], 1)


def attn_pe(S, pe, Z, n0, steps, ident):
    nc = S.nc
    N = len(steps)

    def scores(n):
        if n >= 2:
            pe.wait_ge(Z.p, n0 + n - 1)
        for i, (lhsT, rhs, c, w) in enumerate(steps[n].qk):
            m = nc.tensor.matmul(S.X[n % 2][:, c:c + w], lhsT, rhs, start=(i == 0), stop=(i == len(steps[n].qk) - 1),
                                 skip_group_check=True)
        m.then_inc(Z.s, 1)

    def turn(n):
        pe.wait_ge(Z.p, n0 + n + 1)
        if n >= 1:
            pe.wait_ge(Z.ptc, n0 + n)
        for k in range(steps[n].b + 1):
            m = nc.tensor.transpose(S.X[2][:, k * P:(k + 1) * P], S.wk[4 + n % 2][:, k * P:(k + 1) * P], ident)
        m.then_inc(Z.pt, 1)

    scores(0)
    scores(1)
    turn(0)
    for n in range(N):
        if n + 2 < N:
            scores(n + 2)
        if n + 1 < N:
            turn(n + 1)
        pe.wait_ge(Z.ptc, n0 + n + 1)
        pe.wait_ge(Z.out, n0 + n + 2)
        b = steps[n].b
        for k in range(b + 1):
            m = nc.tensor.matmul(S.X[3][:, 0:HD], S.wk[6 + n % 2][:, k * P:(k + 1) * P], steps[n].v(k),
                                 start=(k == 0), stop=(k == b))
        m.then_inc(Z.o, 1)


def attn_copy_turned(S, Z, eng, op, n0, n, steps):
    eng.wait_ge(Z.pt, n0 + n + 1)
    if n >= 2:
        eng.wait_ge(Z.o, n0 + n - 1)
    w = (steps[n].b + 1) * P
    op(S.wk[6 + n % 2][:, 0:w], S.X[2][:, 0:w]).then_inc(Z.ptc, 1)


def attn_act(S, act, Z, n0, steps):
    nc = S.nc
    N = len(steps)

    def exps(n):
        act.wait_ge(Z.max, n0 + n + 1)
        act.wait_ge(Z.out, n0 + n + 1)
        w = (steps[n].b + 1) * P
        nc.scalar.activation(S.wk[4 + n % 2][:, 0:w], S.X[n % 2][:, 0:w], ACT.Exp, bias=S.nm[n % 2][:, :],
                             accum_out=S.rs[n % 2][:, :]).then_inc(Z.p, 1)

    exps(0)
    for n in range(N):
        if n + 1 < N:
            exps(n + 1)
        if n % 2:
            attn_copy_turned(S, Z, act, lambda o, i: nc.scalar.activation(o, i, ACT.Copy), n0, n, steps)


def attn_dve(S, dve, Z, n0, steps):
    nc = S.nc
    N = len(steps)

    def rowmax(n):
        dve.wait_ge(Z.s, n0 + n + 1)
        if n >= 2:
            dve.wait_ge(Z.p, n0 + n - 1)
        w = (steps[n].b + 1) * P
        nc.vector.tensor_reduce(S.nm[n % 2][:, :], S.X[n % 2][:, 0:w], AX, ALU.max, negate=True).then_inc(Z.max, 1)

    rowmax(0)
    for n in range(N):
        if n + 1 < N:
            rowmax(n + 1)
        if n % 2 == 0:
            attn_copy_turned(S, Z, dve, nc.vector.tensor_copy, n0, n, steps)
        nc.vector.reciprocal(S.rinv[n % 2][:, :], S.rs[n % 2][:, :])
        dve.drain()
        if steps[n].scale:
            steps[n].scale(n)
            dve.drain()
        dve.wait_ge(Z.o, n0 + n + 1)
        steps[n].norm(n)


def fox_steps(S, i):
    steps = []
    for e in range(2):
        for b in range(QB):
            w = (b + 1) * P
            qk = [(S.wk[e][:, b * P:w], S.wk[2 + e][:, 0:w], 0, w), (S.idb[:, :], S.causb[:, :], b * P, P)]

            def v(k, e=e):
                return cols2(S.vt, k * A_NVT * P + V_FOX + e * HD, i, 2 * HD, HD)

            def norm(n, b=b, e=e):
                S.nc.vector.tensor_scalar(cols2(S.otok, b * D + e * HD, i, 2 * HD, HD), S.X[3][:, 0:HD],
                                          S.rinv[n % 2][:, :], None, ALU.mult).then_inc(S.fox.out, 1)
            steps.append(Step(b, qk, v, norm))
    return steps


def cols2(t, c0, i, stride, w):
    return t[:, c0 + i * stride:c0 + i * stride + w] if isinstance(i, int) else t[:, bass.ds(i * stride + c0, w)]


def dsa_steps(S, heads):
    steps = []
    for h0, i, q, k in heads:
        for b in range(QB):
            w = (b + 1) * P
            qk = [(q[:, b * P:w], k[:, 0:w], 0, w)]
            if b == 0:
                qk.append((S.idb[:, :], S.chunkb[:, :], 0, P))
            else:
                m0 = (b * (b + 1) // 2 - 1) * P
                qk.append((S.idb[:, :], S.dmask[:, m0:m0 + w], 0, w))

            def v(kt):
                return S.vt[:, kt * A_NVT * P + V_DSA:kt * A_NVT * P + V_DSA + HD]

            def norm(n, b=b, h0=h0, i=i):
                S.nc.vector.tensor_scalar(cols2(S.otok, b * D + (11 + h0) * HD, i, 2 * HD, HD), S.X[3][:, 0:HD],
                                          S.rinv[n % 2][:, :], None, ALU.mult).then_inc(S.dsa.out, 1)
            steps.append(Step(b, qk, v, norm))
    return steps


def tile_rows(S, u, half):
    return S.qkv[64 * half:64 * half + 64, u * SEQ:(u + 1) * SEQ]


def dsa_pair(S, i):
    return dsa_steps(S, [(0, i, S.wk[0][0:64, :], tile_rows(S, A_DKIK, 0)),
                         (1, i, S.wk[0][64:128, :], tile_rows(S, A_S4KDK, 1))])


def dsa_last(S):
    return dsa_steps(S, [(4, 0, tile_rows(S, A_S4D4Q, 1), tile_rows(S, A_S4KDK, 1))])


SB0 = [0, 4 * P, 7 * P, 9 * P]


def stk_pe(S, pe, n0, q, k, v):
    nc = S.nc

    def z(n):
        i = QB - 1 - n
        if n >= 2:
            pe.wait_ge(S.stk_a, n0 + n - 1)
        nc.tensor.matmul(S.X[n % 2][:, 0:SEQ - i * P], k[:, i * P:(i + 1) * P], q[:, i * P:SEQ], start=True, stop=True,
                         skip_group_check=True).then_inc(S.stk_z, 1)

    z(0)
    for n, i in enumerate(reversed(range(QB))):
        w = SEQ - i * P
        bank = S.X[n % 2]
        if n + 1 < QB:
            z(n + 1)
        pe.wait_ge(S.stk_sp, n0 + n + 1)
        nc.tensor.matmul(bank[:, 0:w], S.con[:, C_TRI:C_TRI + P], S.sp[:, SB0[i]:SB0[i] + w], start=False, stop=False,
                         skip_group_check=True)
        for j in range(i + 1, QB):
            wj = SEQ - j * P
            nc.tensor.matmul(bank[:, w - wj:w], S.negones[:, :], S.sp[:, SB0[j]:SB0[j] + wj], start=False, stop=False,
                             skip_group_check=True)
        nc.tensor.matmul(bank[:, 0:P], S.idb[:, :], S.strictb[:, :], start=False, stop=True,
                         skip_group_check=True).then_inc(S.stk_c, 1)
    pe.wait_ge(S.stk_a, n0 + QB)
    for b in range(QB):
        for kt in range(b + 1):
            c = SB0[kt] + (b - kt) * P
            m = nc.tensor.matmul(S.X[2][:, b * HD:(b + 1) * HD], S.stk_w[:, c:c + P], v(kt),
                                 start=(kt == 0), stop=(kt == b), skip_group_check=True)
    m.then_inc(S.stk_o, 1)


def stk_act(S, act, n0):
    nc = S.nc
    for n, i in enumerate(reversed(range(QB))):
        w = SEQ - i * P
        t = S.nz0[:, 0:w]
        act.wait_ge(S.stk_na, n0 + n + 1)
        nc.scalar.activation(t, t, ACT.Exp)
        act.drain()
        nc.scalar.activation(t, t, ACT.Ln, bias=1.0).then_inc(S.stk_ln, 1)
        act.wait_ge(S.stk_c, n0 + n + 1)
        nc.scalar.activation(S.stk_w[:, SB0[i]:SB0[i] + w], S.X[n % 2][:, 0:w], ACT.Exp).then_inc(S.stk_a, 1)


def stk_dve(S, dve, n0, h0, out):
    nc = S.nc
    for n, i in enumerate(reversed(range(QB))):
        w = SEQ - i * P
        t, sp = S.nz0[:, 0:w], S.sp[:, SB0[i]:SB0[i] + w]
        dve.wait_ge(S.stk_z, n0 + n + 1)
        z = S.X[n % 2][:, 0:w]
        nc.vector.tensor_scalar(sp, z, 0.0, None, ALU.max)
        dve.drain()
        nc.vector.scalar_tensor_tensor(out=t, in0=sp, scalar=-2.0, in1=z, op0=ALU.mult, op1=ALU.add).then_inc(S.stk_na, 1)
        dve.wait_ge(S.stk_ln, n0 + n + 1)
        nc.vector.tensor_tensor(sp, sp, t, ALU.add)
        dve.drain()
        nc.vector.tensor_tensor(sp[:, 0:P], sp[:, 0:P], S.con[:, C_ST01:C_ST01 + P], ALU.mult).then_inc(S.stk_sp, 1)
    dve.wait_ge(S.stk_o, h0 + 1)
    nc.vector.tensor_copy(out, S.X[2][:, 0:QB * HD].rearrange("p (b d) -> p b d", b=QB)).then_inc(S.stk_oev, 1)


def otok_head(S, h0, i):
    v = S.otok[:, :].rearrange("p (b d) -> p b d", b=QB)
    c = h0 * HD
    return v[:, :, c:c + HD] if isinstance(i, int) else v[:, :, bass.ds(i * 2 * HD + c, HD)]


def stk_v(S, col, i):
    return lambda kt: cols2(S.vt, kt * A_NVT * P + col, i, 2 * HD, HD)


def ln_pe(S, pe, n0, t_sem, t0, t):
    nc = S.nc
    for j in range(KT):
        pe.wait_ge(t_sem, t0 + j + 1)
        m = nc.tensor.matmul(S.X[0][:, :], S.ones[:, :], t[:, j * SEQ:(j + 1) * SEQ], start=(j == 0), stop=(j == KT - 1))
    m.then_inc(S.ln_mean, 1)
    for j in range(KT):
        pe.wait_ge(S.ln_sq, n0 * KT + j + 1)
        nc.tensor.matmul(S.X[1][:, :], S.ones[:, :], S.wk[j % 2][:, :], start=(j == 0),
                         stop=(j == KT - 1)).then_inc(S.ln_var, 1)


def ln_act(S, act, n0, t, g, b):
    nc = S.nc
    for j in range(KT):
        act.wait_ge(S.ln_d, n0 * KT + j + 1)
        if j >= 2:
            act.wait_ge(S.ln_var, n0 * KT + j - 1)
        nc.scalar.activation(S.wk[j % 2][:, :], t[:, j * SEQ:(j + 1) * SEQ], ACT.Square).then_inc(S.ln_sq, 1)
    act.wait_ge(S.ln_var, n0 * KT + KT)
    nc.scalar.activation(S.wk[2][:, :], S.X[1][:, :], ACT.Sqrt, bias=S.eps[:, :]).then_inc(S.ln_std, 1)
    for j in range(KT):
        act.wait_ge(S.ln_y, n0 * KT + j + 1)
        nc.scalar.activation(S.xh[:, j * SEQ:(j + 1) * SEQ], t[:, j * SEQ:(j + 1) * SEQ],
                             ACT.Copy).then_inc(S.ln_hi, 1)


def ln_dve(S, dve, n0, t, g, b):
    nc = S.nc
    tiles = [t[:, j * SEQ:(j + 1) * SEQ] for j in range(KT)]
    dve.wait_ge(S.ln_mean, n0 + 1)
    for j in range(KT):
        nc.vector.tensor_tensor(tiles[j], tiles[j], S.X[0][:, :], ALU.subtract).then_inc(S.ln_d, 1)
    dve.wait_ge(S.ln_std, n0 + 1)
    nc.vector.reciprocal(S.wk[3][:, :], S.wk[2][:, :])
    dve.drain()
    for j in range(KT + 2):
        if j < KT:
            nc.vector.tensor_tensor(tiles[j], tiles[j], S.wk[3][:, :], ALU.mult)
            dve.drain()
            nc.vector.tensor_scalar(tiles[j], tiles[j], S.cur[:, g + j:g + j + 1], S.cur[:, b + j:b + j + 1],
                                    ALU.mult, ALU.add).then_inc(S.ln_y, 1)
        if j == 0:
            dve.drain()
        if j >= 2:
            q = j - 2
            dve.wait_ge(S.ln_hi, n0 * KT + q + 1)
            nc.vector.tensor_tensor(S.xl[:, q * SEQ:(q + 1) * SEQ], tiles[q],
                                    S.xh[:, q * SEQ:(q + 1) * SEQ].bitcast(F32),
                                    ALU.subtract).then_inc(S.x_ready, 1)


ROPE = [(A_IKF, 0, 64), (A_S4D4Q, 64, 128), (A_S4KDK, 64, 128)] + [(u, 0, P) for u in range(A_DKIK, A_NPROJ)]


def idx_steps():
    return [(b, h) for b in range(1, QB) for h in range(IDX_HEADS)]


SC0 = [None, 0, 2 * P, 5 * P]


def a_tensor(S, pe):
    nc = S.nc
    ident = S.con[:, C_ID:C_ID + P]
    with pe.Fori(0, DEPTH) as L:
        G = lambda u, i=0: L * A_GROUPS + u // SLOTS + i
        with pe.Fori(0, 6) as i:
            pe.wait_ge(S.x_ready, L * 2 * KT + KT)
            for u in range(SLOTS):
                pe_unit(S, pe, u, G(u, i), S.ps[u][:, :], S.xh, S.xl).then_inc(S.unit_done[u], 1)
        for u in (24, 25):
            pe_unit(S, pe, u, G(u), S.ps[u % SLOTS][:, :], S.xh, S.xl).then_inc(S.unit_done[u % SLOTS], 1)
        pe.wait_ge(S.bank_free[25 % SLOTS], G(25) + 2)
        for v in range(A_NVT):
            if v >= 2:
                pe.wait_ge(S.vt_done, L * A_NVT + v - 1)
            for t in range(QB):
                m = nc.tensor.transpose(S.X[2 + v % 2][:, t * P:(t + 1) * P],
                                        S.qkv[:, (A_VT + v) * SEQ + t * P:(A_VT + v) * SEQ + (t + 1) * P], ident)
            m.then_inc(S.vt_ready, 1)
        pe.wait_ge(S.scaled, L + 1)
        for n, (u, _, _) in enumerate(ROPE):
            if n >= 2:
                pe.wait_ge(S.rope_done, L * len(ROPE) + n - 1)
            nc.tensor.matmul(S.X[n % 2][:, :], S.con[:, C_ROT:C_ROT + P], S.qkv[:, u * SEQ:(u + 1) * SEQ],
                             start=True, stop=True).then_inc(S.rot_ready, 1)
        pe.wait_ge(S.vt_done, (L + 1) * A_NVT)
        pe.wait_ge(S.rope_done, (L + 1) * len(ROPE))
        for n, (b, h) in enumerate(idx_steps()):
            if n >= 4:
                pe.wait_ge(S.relu_done, L * 24 + n - 3)
            k = tile_rows(S, A_IKF, 0) if h % 2 == 0 else tile_rows(S, A_DKIK, 1)
            q = tile_rows(S, A_IQ + h // 2, h % 2)
            w = (b + 1) * P
            nc.tensor.matmul(S.X[n % 4][:, 0:w], q[:, b * P:w], k[:, 0:w], start=True,
                             stop=True).then_inc(S.idx_ready, 1)
        with pe.Fori(0, 2) as i:
            for u in range(A_GFOX, A_GFOX + SLOTS):
                pe_unit(S, pe, u, G(u, i), S.ps[u % SLOTS][:, :], S.xh, S.xl).then_inc(S.unit_done[u % SLOTS], 1)
        with pe.Fori(0, 3) as i:
            pe.wait_ge(S.relu_done, (L + 1) * 24)
            pe.wait_ge(S.fox_staged, (L * 3 + i) * 4 + 4)
            pe.wait_ge(S.fox_aug, (L * 3 + i) * 2 + 2)
            attn_pe(S, pe, S.fox, (L * 3 + i) * 8, fox_steps(S, i), ident)
        with pe.Fori(0, 2) as i:
            pe.wait_ge(S.fox.out, (L + 1) * 24 + 2)
            pe.wait_ge(S.s_staged, (L * 2 + i) * 2 + 2)
            for e in range(2):
                h0 = L * 5 + i * 2 + e
                pe.wait_ge(S.stk_oev, h0 + 1)
                stk_pe(S, pe, h0 * QB, S.wk[0][64 * e:64 * e + 64, :], S.wk[1][64 * e:64 * e + 64, :],
                       stk_v(S, V_SB + e * HD, i))
        pe.wait_ge(S.stk_oev, L * 5 + 5)
        stk_pe(S, pe, (L * 5 + 4) * QB, tile_rows(S, A_S4D4Q, 0), tile_rows(S, A_S4KDK, 0), stk_v(S, V_S4, 0))
        with pe.Fori(0, 2) as i:
            pe.wait_ge(S.stk_oev, L * 5 + 6)
            pe.wait_ge(S.mask_ready, L + 1)
            pe.wait_ge(S.d_staged, L * 2 + i + 1)
            attn_pe(S, pe, S.dsa, L * 20 + i * 8, dsa_pair(S, i), ident)
        attn_pe(S, pe, S.dsa, L * 20 + 16, dsa_last(S), ident)
        pe.wait_ge(S.dsa.out, (L + 1) * 20 + 2)
        for k in range(KT):
            if k >= 4:
                pe.wait_ge(S.ot_done, L * KT + k - 3)
            for b in range(QB):
                m = nc.tensor.transpose(S.X[k % 4][:, b * P:(b + 1) * P],
                                        S.otok[:, b * D + k * P:b * D + (k + 1) * P], ident)
            m.then_inc(S.ot_ready, 1)
        with pe.Fori(0, 2) as i:
            pe.wait_ge(S.ot_done, (L + 1) * KT)
            for jj in range(4):
                u = A_MIX + 3 * jj
                for d in range(2):
                    pe_unit(S, pe, u + d, G(u + d, 3 * i), S.ps[(u + d) % SLOTS][:, :], S.xh,
                            S.xl).then_inc(S.unit_done[(u + d) % SLOTS], 1)
                u += 2
                s = u % SLOTS
                pe.wait_ge(S.lo_ready[s], G(u, 3 * i) + 1)
                pe.wait_ge(S.bank_free[s], G(u, 3 * i) + 1)
                pe.wait_ge(S.merge_x, L * KT + i * 4 + jj + 1)
                XS, XD = S.X[2 * (jj % 2)][:, :], S.X[2 * (jj % 2) + 1][:, :]
                for k in range(3):
                    pe_tile(S, s, k, S.ps[s][:, :], S.rh, S.rl, k, k == 0, k == 2)
                pe_tile(S, s, 3, XS, S.rh, S.rl, 3, True, False)
                pe_tile(S, s, 4, XS, S.rh, S.rl, 4, False, False)
                pe_tile(S, s, 5, XS, S.rh, S.rl, 5, False, True, 0, 64)
                pe_tile(S, s, 6, XD, S.rh, S.rl, 6, True, False)
                pe_tile(S, s, 5, XD, S.rh, S.rl, 5, False, False, 64, 128)
                pe_tile(S, s, 7, XD, S.rh, S.rl, 7, False, True)
                S.last.then_inc(S.unit_done[s], 1)
        with pe.Fori(0, 2) as i:
            pe.wait_ge(S.merge_done, (L + 1) * KT)
            for u in range(A_OUT, A_OUT + SLOTS):
                pe_unit(S, pe, u, G(u, i), S.ps[u % SLOTS][:, :], S.mh, S.ml).then_inc(S.unit_done[u % SLOTS], 1)
        ln_pe(S, pe, L * 2, S.t_ready, L * KT, S.t)
        with pe.Fori(0, 4) as q:
            with pe.Fori(0, 2) as i:
                pe.wait_ge(S.x_ready, L * 2 * KT + 2 * KT)
                for u in range(A_FFN, A_FFN + SLOTS):
                    pe_unit(S, pe, u, G(u, q * 4 + i), S.ps[u % SLOTS][:, :], S.xh,
                            S.xl).then_inc(S.unit_done[u % SLOTS], 1)
            with pe.Fori(0, 2) as i:
                pe.wait_ge(S.ffn_h, (L * 4 + q) * KT + KT + 2)
                for u in range(A_FFN, A_FFN + SLOTS):
                    pe_unit(S, pe, u, G(u, q * 4 + i + 2), S.ps[u % SLOTS][:, :], S.rh,
                            S.rl).then_inc(S.unit_done[u % SLOTS], 1)
        pe.wait_ge(S.p_ready, L + 1)
        for d in range(2):
            u = A_PLE + d
            s = u % SLOTS
            pe.wait_ge(S.lo_ready[s], G(u) + 1)
            pe.wait_ge(S.bank_free[s], G(u) + 1)
            if d:
                pe.wait_ge(S.bank_free[(u - 1) % SLOTS], G(u - 1) + 2)
            for o in range(4):
                for k in range(2):
                    pe_tile(S, s, 2 * o + k, S.X[o][:, :], S.ph, S.pl, k, k == 0, k == 1)
            S.last.then_inc(S.unit_done[s], 1)
        with pe.Fori(0, 2) as i:
            for u in range(A_PG, A_PG + SLOTS):
                pe_unit(S, pe, u, G(u, i), S.ps[u % SLOTS][:, :], S.xh, S.xl).then_inc(S.unit_done[u % SLOTS], 1)
        ln_pe(S, pe, L * 2 + 1, S.y_ready, L * KT + 2, S.yacc)


def a_scalar(S, act, p_dram):
    nc = S.nc

    def take(u, g, out, func, **kw):
        s = u % SLOTS
        act.wait_ge(S.unit_done[s], g + 1)
        nc.scalar.activation(out, S.ps[s][:, :], func, **kw).then_inc(S.bank_free[s], 1)
        act_split(S, act, u, g)

    for s in range(SLOTS):
        act.wait_ge(S.raw_landed[s], 16)
        nc.scalar.activation(S.wh[s][:, :], S.raw[s][:, :], ACT.Copy).then_inc(S.hi_ready[s], 1)
    with act.Fori(0, DEPTH) as L:
        G = lambda u, i=0: L * A_GROUPS + u // SLOTS + i
        with act.Fori(0, 6) as i:
            for u in range(SLOTS):
                take(u, G(u, i), cols(S.qkv, i * SLOTS + u), ACT.Copy)
        for u in (24, 25):
            take(u, G(u), cols(S.qkv, u), ACT.Copy)
        vt = S.vt[:, :].rearrange("p (t c) -> p t c", t=QB)
        for v in range(A_NVT):
            act.wait_ge(S.vt_ready, L * A_NVT + v + 1)
            nc.scalar.activation(vt[:, :, v * P:(v + 1) * P], S.X[2 + v % 2][:, :].rearrange("p (t c) -> p t c", t=QB),
                                 ACT.Copy).then_inc(S.vt_done, 1)
        nc.scalar.preload_act_table_set("natural_log_exp_and_others")
        act.wait_ge(S.logf_in, L + 1)
        lf = S.wk[5][64:128, :]
        nc.scalar.activation(lf, lf, ACT.Exp)
        act.drain()
        nc.scalar.activation(lf, lf, ACT.Ln, bias=1.0).then_inc(S.logf_out, 1)
        for n, (b, h) in enumerate(idx_steps()):
            act.wait_ge(S.idx_ready, L * 24 + n + 1)
            if n >= 2:
                act.wait_ge(S.idx_acc, L * 24 + n - 1)
            w = (b + 1) * P
            nc.scalar.activation(S.r[n % 2][:, 0:w], S.X[n % 4][:, 0:w], ACT.Relu).then_inc(S.relu_done, 1)
        with act.Fori(0, 2) as i:
            for j in range(SLOTS):
                take(A_GFOX + j, G(A_GFOX + j, i), cols(S.gfox, i * SLOTS + j), ACT.Tanh, scale=0.5)
        with act.Fori(0, 3) as i:
            for e in range(2):
                src = S.qkv[64 * e:64 * e + 64, :]
                for t, u in ((e, A_FQ), (2 + e, A_FK)):
                    nc.scalar.activation(S.wk[t][0:64, :], cols2(src, u * SEQ, i, SEQ, SEQ), ACT.Copy).then_inc(S.fox_staged, 1)
            attn_act(S, act, S.fox, (L * 3 + i) * 8, fox_steps(S, i))
        nc.scalar.preload_act_table_set("natural_log_exp_and_others")
        act.wait_ge(S.fox.out, (L + 1) * 24 + 2)
        with act.Fori(0, 2) as i:
            act.wait_ge(S.stk_oev, L * 5 + i * 2 + 1)
            for t, u in ((0, A_SQ), (1, A_SK)):
                nc.scalar.activation(S.wk[t][:, :], cols(S.qkv, i + u), ACT.Copy).then_inc(S.s_staged, 1)
            for e in range(2):
                stk_act(S, act, (L * 5 + i * 2 + e) * QB)
        stk_act(S, act, (L * 5 + 4) * QB)
        with act.Fori(0, 2) as i:
            act.wait_ge(S.stk_oev, L * 5 + 6)
            nc.scalar.activation(S.wk[0][:, :], cols(S.qkv, i + A_DQ), ACT.Copy).then_inc(S.d_staged, 1)
            attn_act(S, act, S.dsa, L * 20 + i * 8, dsa_pair(S, i))
        attn_act(S, act, S.dsa, L * 20 + 16, dsa_last(S))
        for k in range(KT):
            act.wait_ge(S.ot_ready, L * KT + k + 1)
            nc.scalar.activation(S.rh[:, k * SEQ:(k + 1) * SEQ], S.X[k % 4][:, :], ACT.Copy).then_inc(S.ot_hi, 1)
        act.dma_start(S.praw[:, :], p_dram[bass.ds(L, 1), :, :].rearrange("a p n -> (a p) n")).then_inc(S.p_landed, 16)
        with act.Fori(0, 2) as i:
            for jj in range(4):
                u = A_MIX + 3 * jj
                for d in range(2):
                    s, g = (u + d) % SLOTS, G(u + d, 3 * i)
                    act.wait_ge(S.unit_done[s], g + 1)
                    if d == 0:
                        act.wait_ge(S.merge_x, L * KT + i * 4 + jj + 1)
                    nc.scalar.activation(S.wk[4 + 2 * (jj % 2) + d][:, :], S.ps[s][:, :], ACT.Tanh,
                                         scale=0.5).then_inc(S.bank_free[s], 1)
                    act_split(S, act, u + d, g)
                act.wait_ge(S.unit_done[(u + 2) % SLOTS], G(u + 2, 3 * i) + 1)
                act_split(S, act, u + 2, G(u + 2, 3 * i))
        with act.Fori(0, 2) as i:
            for u in range(A_OUT, A_OUT + SLOTS):
                act.wait_ge(S.unit_done[u % SLOTS], G(u, i) + 1)
                act_split(S, act, u, G(u, i))
        ln_act(S, act, L * 2, S.t, PA_G1, PA_B1)
        with act.Fori(0, 4) as q:
            with act.Fori(0, 2) as i:
                for j in range(SLOTS):
                    u = A_FFN + j
                    s, g = u % SLOTS, G(u, q * 4 + i)
                    act.wait_ge(S.unit_done[s], g + 1)
                    act.wait_ge(S.ffn_h, (L * 4 + q) * KT + i * SLOTS + j + 1)
                    nc.scalar.activation(S.wk[j % 2][:, :], S.ps[s][:, :], ACT.Relu).then_inc(S.bank_free[s], 1)
                    act.drain()
                    nc.scalar.activation(cols(S.rh, i * SLOTS + j), S.wk[j % 2][:, :], ACT.Square).then_inc(S.ffn_act, 1)
                    act_split(S, act, u, g)
            with act.Fori(0, 2) as i:
                for u in range(A_FFN, A_FFN + SLOTS):
                    g = G(u, q * 4 + i + 2)
                    act.wait_ge(S.unit_done[u % SLOTS], g + 1)
                    act_split(S, act, u, g)
        for d in range(2):
            u = A_PLE + d
            s = u % SLOTS
            act.wait_ge(S.unit_done[s], G(u) + 1)
            for o in range(4):
                m = nc.scalar.activation(cols(S.plep, 4 * d + o), S.X[o][:, :], ACT.Copy)
            m.then_inc(S.bank_free[s], 1)
            act_split(S, act, u, G(u))
        with act.Fori(0, 2) as i:
            for j in range(SLOTS):
                u = A_PG + j
                s, g = u % SLOTS, G(u, i)
                act.wait_ge(S.unit_done[s], g + 1)
                act.wait_ge(S.y_ready, L * KT + i * SLOTS + j + 1)
                nc.scalar.activation(S.wk[4 + j % 2][:, :], S.ps[s][:, :], ACT.Tanh, scale=0.5).then_inc(S.bank_free[s], 1)
                act_split(S, act, u, g)
        ln_act(S, act, L * 2 + 1, S.yacc, PA_G2, PA_B2)


def a_vector(S, dve):
    nc = S.nc
    with dve.Fori(0, DEPTH) as L:
        G = lambda u, i=0: L * A_GROUPS + u // SLOTS + i
        nc.vector.tensor_copy(S.cur[:, :], cols(S.prmA, L, PA_N))
        dve.drain()
        dve.wait_ge(S.bank_free[25 % SLOTS], G(25) + 2)
        for u, n in ((A_FQ, 5), (A_S4D4Q, 1), (A_DQ, 2)):
            t = S.qkv[:, u * SEQ:(u + n) * SEQ]
            m = nc.vector.tensor_scalar(t, t, HD ** -0.5, None, ALU.mult)
        m.then_inc(S.scaled, 1)
        f, na = S.c[64:128, :], S.wk[5][64:128, :]
        nc.vector.tensor_scalar(f, S.qkv[64:128, A_IKF * SEQ:(A_IKF + 1) * SEQ], S.cur[64:128, PA_BF:PA_BF + 1], None, ALU.add)
        dve.drain()
        nc.vector.scalar_tensor_tensor(out=na, in0=f, scalar=-1.0, in1=f, op0=ALU.mult, op1=ALU.min).then_inc(S.logf_in, 1)
        for n, (u, lo, hi) in enumerate(ROPE):
            t = S.qkv[lo:hi, u * SEQ:(u + 1) * SEQ]
            a, b = S.wk[n % 2][lo:hi, :], S.wk[2 + n % 2][lo:hi, :]
            nc.vector.tensor_tensor(a, t, S.cos[lo:hi, :], ALU.mult)
            dve.wait_ge(S.rot_ready, L * len(ROPE) + n + 1)
            nc.vector.tensor_tensor(b, S.X[n % 2][lo:hi, :], S.sin[lo:hi, :], ALU.mult)
            dve.drain()
            nc.vector.tensor_tensor(t, a, b, ALU.add).then_inc(S.rope_done, 1)
        nc.vector.memset(S.wk[4][64:128, :], 1.0)
        dve.wait_ge(S.logf_out, L + 1)
        nc.vector.scalar_tensor_tensor(out=f, in0=f, scalar=0.0, in1=na, op0=ALU.min, op1=ALU.subtract)
        dve.drain()
        nc.vector.tensor_tensor_scan(na, S.wk[4][64:128, :], f, 0.0, ALU.mult, ALU.add)
        dve.drain()
        nc.vector.tensor_copy(f, na)
        for e in range(2):
            nc.vector.tensor_scalar(S.wk[2 + e][64:128, :], na, S.con[64:128, C_KA:C_KA + 1], S.con[64:128, C_KB:C_KB + 1],
                                    ALU.mult, ALU.add)
        dve.wait_ge(S.vt_done, (L + 1) * A_NVT)
        for n, (b, h) in enumerate(idx_steps()):
            dve.wait_ge(S.relu_done, L * 24 + n + 1)
            w = (b + 1) * P
            acc = S.score[:, SC0[b]:SC0[b] + w]
            iw = S.vt[:, b * A_NVT * P + V_IW + h:b * A_NVT * P + V_IW + h + 1]
            if h == 0:
                nc.vector.tensor_scalar(acc, S.r[n % 2][:, 0:w], iw, None, ALU.mult).then_inc(S.idx_acc, 1)
            else:
                nc.vector.scalar_tensor_tensor(out=acc, in0=S.r[n % 2][:, 0:w], scalar=iw, in1=acc, op0=ALU.mult,
                                               op1=ALU.add).then_inc(S.idx_acc, 1)
            dve.drain()
        for b in range(1, QB):
            nc.vector.memset(S.score[0:64, SC0[b] + b * P + 64:SC0[b] + (b + 1) * P], NEG)
        dve.drain()
        with dve.Fori(0, TOPK // 8) as _:
            for b in range(1, QB):
                nc.vector.max(S.top[b - 1][:, :], S.score[:, SC0[b]:SC0[b] + (b + 1) * P])
            dve.drain()
            for b in range(1, QB):
                sc = S.score[:, SC0[b]:SC0[b] + (b + 1) * P]
                nc.vector.match_replace(sc, S.top[b - 1][:, :], sc, MARK)
            dve.drain()
        nc.vector.tensor_scalar(S.dmask[:, :], S.score[:, :], MARK / 2, NEG, ALU.is_gt, ALU.mult).then_inc(S.mask_ready, 1)
        with dve.Fori(0, 3) as i:
            for e in range(2):
                qa = S.con[64:128, bass.ds(i * 2 + C_QA + e, 1)]
                qb = S.con[64:128, bass.ds(i * 2 + C_QB + e, 1)]
                nc.vector.tensor_scalar(S.wk[e][64:128, :], f, qa, qb, ALU.mult, ALU.add).then_inc(S.fox_aug, 1)
            attn_dve(S, dve, S.fox, (L * 3 + i) * 8, fox_steps(S, i))
        with dve.Fori(0, 2) as i:
            for e in range(2):
                h0 = L * 5 + i * 2 + e
                stk_dve(S, dve, h0 * QB, h0, otok_head(S, 6 + e, i))
        stk_dve(S, dve, (L * 5 + 4) * QB, L * 5 + 4, otok_head(S, 10, 0))
        with dve.Fori(0, 2) as i:
            attn_dve(S, dve, S.dsa, L * 20 + i * 8, dsa_pair(S, i))
        attn_dve(S, dve, S.dsa, L * 20 + 16, dsa_last(S))
        for k in range(KT):
            dve.wait_ge(S.ot_hi, L * KT + k + 1)
            nc.vector.tensor_tensor(S.rl[:, k * SEQ:(k + 1) * SEQ], S.X[k % 4][:, :],
                                    S.rh[:, k * SEQ:(k + 1) * SEQ].bitcast(F32), ALU.subtract).then_inc(S.ot_done, 1)
        dve.wait_ge(S.p_landed, 16 * (L + 1))
        nc.vector.tensor_copy(S.ph[:, :], S.praw[:, :])
        dve.drain()
        nc.vector.tensor_tensor(S.pl[:, :], S.praw[:, :], S.ph[:, :].bitcast(F32), ALU.subtract).then_inc(S.p_ready, 1)
        with dve.Fori(0, 2) as i:
            for jj in range(4):
                u = A_MIX + 3 * jj
                s, s1 = (u + 2) % SLOTS, (u + 1) % SLOTS
                dve.wait_ge(S.unit_done[s], G(u + 2, 3 * i) + 1)
                dve.wait_ge(S.bank_free[s1], G(u + 1, 3 * i) + 2)
                a, b, c = S.wk[3 * (jj % 2)][:, :], S.wk[1][:, :], S.wk[2][:, :]
                nc.vector.scalar_tensor_tensor(out=a, in0=cols(S.gfox, i * 4 + jj), scalar=1.0, in1=S.ps[s][:, :],
                                               op0=ALU.add, op1=ALU.mult).then_inc(S.bank_free[s], 1)
                for d, o in ((0, b), (1, c)):
                    m = nc.vector.scalar_tensor_tensor(out=o, in0=S.wk[4 + 2 * (jj % 2) + d][:, :], scalar=1.0,
                                                       in1=S.X[2 * (jj % 2) + d][:, :], op0=ALU.add, op1=ALU.mult)
                m.then_inc(S.merge_x, 1)
                dve.drain()
                nc.vector.tensor_tensor(a, a, b, ALU.add)
                dve.drain()
                nc.vector.tensor_tensor(a, a, c, ALU.add)
                dve.drain()
                mh, ml = cols(S.mh, i * 4 + jj), cols(S.ml, i * 4 + jj)
                nc.vector.tensor_scalar(mh, a, 0.5, None, ALU.mult)
                dve.drain()
                nc.vector.scalar_tensor_tensor(out=ml, in0=a, scalar=0.5, in1=mh.bitcast(F32), op0=ALU.mult,
                                               op1=ALU.subtract).then_inc(S.merge_done, 1)
        with dve.Fori(0, 2) as i:
            for j in range(SLOTS):
                u = A_OUT + j
                s = u % SLOTS
                dve.wait_ge(S.unit_done[s], G(u, i) + 1)
                t = cols(S.t, i * SLOTS + j)
                nc.vector.scalar_tensor_tensor(out=t, in0=cols(S.xh, i * SLOTS + j).bitcast(F32), scalar=ALPHA,
                                               in1=S.ps[s][:, :], op0=ALU.mult, op1=ALU.add).then_inc(S.bank_free[s], 1)
                dve.drain()
                nc.vector.scalar_tensor_tensor(out=t, in0=cols(S.xl, i * SLOTS + j).bitcast(F32), scalar=ALPHA,
                                               in1=t, op0=ALU.mult, op1=ALU.add).then_inc(S.t_ready, 1)
        ln_dve(S, dve, L * 2, S.t, PA_G1, PA_B1)
        dve.drain()
        nc.vector.tensor_scalar(S.yacc[:, :], S.xh[:, :].bitcast(F32), ALPHA, None, ALU.mult)
        dve.drain()
        nc.vector.scalar_tensor_tensor(out=S.yacc[:, :], in0=S.xl[:, :].bitcast(F32), scalar=ALPHA, in1=S.yacc[:, :],
                                       op0=ALU.mult, op1=ALU.add)
        with dve.Fori(0, 4) as q:
            with dve.Fori(0, 2) as i:
                for j in range(SLOTS):
                    dve.wait_ge(S.ffn_act, (L * 4 + q) * KT + i * SLOTS + j + 1)
                    h = S.wk[2 + j % 2][:, :]
                    nc.vector.tensor_tensor(h, S.wk[j % 2][:, :], S.wk[j % 2][:, :], ALU.mult)
                    dve.drain()
                    nc.vector.tensor_tensor(cols(S.rl, i * SLOTS + j), h, cols(S.rh, i * SLOTS + j).bitcast(F32),
                                            ALU.subtract).then_inc(S.ffn_h, 1)
            with dve.Fori(0, 2) as i:
                for j in range(SLOTS):
                    u = A_FFN + j
                    s = u % SLOTS
                    dve.wait_ge(S.unit_done[s], G(u, q * 4 + i + 2) + 1)
                    y = cols(S.yacc, i * SLOTS + j)
                    nc.vector.tensor_tensor(y, y, S.ps[s][:, :], ALU.add).then_inc(S.bank_free[s], 1)
        with dve.Fori(0, 2) as i:
            for j in range(SLOTS):
                u = A_PG + j
                s = u % SLOTS
                dve.wait_ge(S.bank_free[s], G(u, i) + 2)
                a, y = S.wk[6 + j % 2][:, :], cols(S.yacc, i * SLOTS + j)
                nc.vector.scalar_tensor_tensor(out=a, in0=S.wk[4 + j % 2][:, :], scalar=1.0, in1=cols(S.plep, i * SLOTS + j),
                                               op0=ALU.add, op1=ALU.mult)
                dve.drain()
                nc.vector.scalar_tensor_tensor(out=y, in0=a, scalar=0.5, in1=y, op0=ALU.mult,
                                               op1=ALU.add).then_inc(S.y_ready, 1)
        ln_dve(S, dve, L * 2 + 1, S.yacc, PA_G2, PA_B2)


def GB(L, u, i=0):
    return DEPTH * A_GROUPS + L * B_GROUPS + u // SLOTS + i


def seq(t, j):
    return t[:, j * SEQ:(j + 1) * SEQ]


def rms_pe(S, pe, n0):
    for j in range(KT):
        pe.wait_ge(S.rms_sq, n0 * KT + j + 1)
        S.nc.tensor.matmul(S.X[1][:, :], S.ones[:, :], S.wk[j % 2][:, :], start=(j == 0),
                           stop=(j == KT - 1)).then_inc(S.rms_var, 1)


def rms_act(S, act, n0, split):
    nc = S.nc
    act.wait_ge(S.res_ready, n0 + 1)
    for j in range(KT):
        if j >= 2:
            act.wait_ge(S.rms_var, n0 * KT + j - 1)
        nc.scalar.activation(S.wk[j % 2][:, :], seq(S.res, j), ACT.Square).then_inc(S.rms_sq, 1)
    act.wait_ge(S.rms_var, n0 * KT + KT)
    nc.scalar.activation(S.wk[2][:, :], S.X[1][:, :], ACT.Sqrt, bias=S.eps2[:, :]).then_inc(S.rms_std, 1)
    for j in range(KT if split else 0):
        act.wait_ge(S.rms_y, n0 * KT + j + 1)
        nc.scalar.activation(seq(S.xh, j), S.wk[4 + j % 4][:, :], ACT.Copy).then_inc(S.rms_hi, 1)


def rms_dve(S, dve, n0):
    nc = S.nc
    dve.wait_ge(S.rms_std, n0 + 1)
    nc.vector.reciprocal(S.wk[3][:, :], S.wk[2][:, :])
    dve.drain()
    for j in range(KT + 2):
        if j < KT:
            nc.vector.scalar_tensor_tensor(out=S.wk[4 + j % 4][:, :], in0=seq(S.res, j), scalar=S.curB[:, PB_G + j:PB_G + j + 1],
                                           in1=S.wk[3][:, :], op0=ALU.mult, op1=ALU.mult).then_inc(S.rms_y, 1)
        if j >= 2:
            q = j - 2
            dve.wait_ge(S.rms_hi, n0 * KT + q + 1)
            nc.vector.tensor_tensor(seq(S.xl, q), S.wk[4 + q % 4][:, :], seq(S.xh, q).bitcast(F32),
                                    ALU.subtract).then_inc(S.x_ready, 1)
            dve.drain()


def pairs_pe(S, pe, L, u, rh, rl, k0):
    s = u % SLOTS
    pe.wait_ge(S.lo_ready[s], GB(L, u) + 1)
    pe.wait_ge(S.bank_free[s], GB(L, u) + 1)
    for o, bank in ((0, S.ps[s]), (1, S.X[s])):
        for k in range(4):
            pe_tile(S, s, 4 * o + k, bank[:, :], rh, rl, k0 + k, k == 0, k == 3)
    S.last.then_inc(S.unit_done[s], 1)


def nsa_steps(S, t):
    steps = []
    for src, k, br in (("s", S.kv["ks"], 1), ("w", S.kv["kw"], 2)):
        for e in range(2):
            for b in range(QB):
                w = (b + 1) * P
                qk = [(S.wk[0][64 * e:64 * e + 64, b * P:w], k[64 * e:64 * e + 64, 0:w], 0, w),
                      (S.idb[:, :], S.causb[:, :], b * P, P)]

                def v(kt, src=src, e=e):
                    return S.vtok[src][:, kt * P + e * HD:kt * P + (e + 1) * HD]

                def scale(n, b=b, e=e, br=br):
                    gate = cols2(S.gate, b * 3 * B_HEADS + e * 12 + br, t, 3, 1)
                    S.nc.vector.tensor_scalar(S.rg[n % 2][:, :], S.rinv[n % 2][:, :], gate, None, ALU.mult)

                def norm(n, b=b, e=e):
                    o = cols2(S.ot2, b * 512 + e * 256, t, HD, HD)
                    S.nc.vector.scalar_tensor_tensor(out=o, in0=S.X[3][:, 0:HD], scalar=S.rg[n % 2][:, :], in1=o,
                                                     op0=ALU.mult, op1=ALU.add).then_inc(S.nsa.out, 1)
                steps.append(Step(b, qk, v, norm, scale))
    return steps


def rope_tiles(S):
    return [S.kv[n][:, :] for n in ("kc", "ks", "kw")] + [seq(S.q, t) for t in range(4)]


NROPE = 7


def b_tensor(S, pe):
    nc = S.nc
    ident = S.con[:, C_ID:C_ID + P]
    with pe.Fori(0, DEPTH) as L:
        rms_pe(S, pe, L)
        with pe.Fori(0, 8) as i:
            pe.wait_ge(S.x_ready, KT * (1 + 2 * DEPTH) + L * KT + KT)
            for u in range(SLOTS):
                pe_unit(S, pe, u, GB(L, u, i), S.ps[u][:, :], S.xh, S.xl).then_inc(S.unit_done[u], 1)
        for u in (32, 33, 34):
            pe_unit(S, pe, u, GB(L, u), S.ps[u % SLOTS][:, :], S.xh, S.xl).then_inc(S.unit_done[u % SLOTS], 1)
        pe.wait_ge(S.bank_free[B_G % SLOTS], GB(L, B_G) + 2)
        for v, name in enumerate(("vs", "vw", "gl")):
            if v >= 2:
                pe.wait_ge(S.bvt_done, L * 2 + 1)
            for t in range(QB):
                m = nc.tensor.transpose(S.X[2 + v % 2][:, t * P:(t + 1) * P], S.kv[name][:, t * P:(t + 1) * P], ident)
            m.then_inc(S.bvt_ready, 1)
        for n, t in enumerate(rope_tiles(S)):
            if n >= 2:
                pe.wait_ge(S.b_rope_done, L * NROPE + n - 1)
            nc.tensor.matmul(S.X[n % 2][:, :], S.con[:, C_ROT:C_ROT + P], t, start=True, stop=True).then_inc(S.b_rot_ready, 1)
        s = B_BD % SLOTS
        pe.wait_ge(S.lo_ready[s], GB(L, B_BD) + 1)
        pe.wait_ge(S.xc_split, L + 1)
        pe.wait_ge(S.b_rope_done, (L + 1) * NROPE)
        pe.wait_ge(S.bvt_done, L * 2 + 2)
        pe.wait_ge(S.gl_done, L + 1)
        for t in range(4):
            if t >= 2:
                pe.wait_ge(S.lru_gate, L * 4 + t - 1)
            for d in range(2):
                pe_tile(S, s, 2 * t + d, S.X[2 * (t % 2) + d][:, :], S.xh, S.xl, t, True, True)
            S.last.then_inc(S.lru_ready, 1)
        S.last = nc.tensor.matmul(S.ps[s][:, 0:P], ident, ident, start=True, stop=True)
        S.last.then_inc(S.unit_done[s], 1)
        pe.wait_ge(S.lru_gate, L * 4 + 4)
        for kv in range(2):
            pe.wait_ge(S.blk_ready, L * 2 + kv + 1)
            for m in range(2):
                for half in range(2):
                    u = B_CMP1 + 4 * kv + 2 * m + half
                    s = u % SLOTS
                    pe.wait_ge(S.lo_ready[s], GB(L, u) + 1)
                    out = S.X[kv][:, m * HD:m * HD + NB2]
                    for k in range(KT):
                        lp = half * KT + k
                        c = (4 + 2 * kv) * SEQ + lp * NB2
                        wh, wl = (t[s][:, k * P:(k + 1) * P] for t in (S.wh, S.wl))
                        bh, bl = (t[:, c:c + NB2] for t in (S.xh, S.xl))
                        nc.tensor.matmul(out, wh, bh, start=(lp == 0), stop=False, skip_group_check=True)
                        nc.tensor.matmul(out, wh, bl, start=False, stop=False, skip_group_check=True)
                        mm = nc.tensor.matmul(out, wl, bh, start=False, stop=(lp == 15), skip_group_check=True)
                    mm.then_inc(S.unit_done[s], 1)
        s = B_CMP2 % SLOTS
        pe.wait_ge(S.lo_ready[s], GB(L, B_CMP2) + 1)
        pe.wait_ge(S.hid_split, L * 2 + 1)
        for m in range(2):
            wh, wl = (t[s][:, m * P:(m + 1) * P] for t in (S.wh, S.wl))
            bh, bl = (t[:, m * NB2:(m + 1) * NB2] for t in (S.hkh, S.hkl))
            for i, (a, b) in enumerate(((wh, bh), (wh, bl), (wl, bh))):
                mm = nc.tensor.matmul(S.X[2][:, 0:NB2], a, b, start=(m == 0 and i == 0), stop=(m == 1 and i == 2))
        mm.then_inc(S.unit_done[s], 1)
        s = (B_CMP2 + 1) % SLOTS
        pe.wait_ge(S.lo_ready[s], GB(L, B_CMP2 + 1) + 1)
        pe.wait_ge(S.hid_split, L * 2 + 2)
        for g in range(2):
            for m in range(2):
                wh, wl = (t[s][:, m * P:m * P + HD] for t in (S.wh, S.wl))
                bh, bl = (t[:, (2 * m + g) * P:(2 * m + g + 1) * P] for t in (S.hvh, S.hvl))
                for i, (a, b) in enumerate(((bh, wh), (bh, wl), (bl, wh))):
                    mm = nc.tensor.matmul(S.X[3][:, g * HD:(g + 1) * HD], a, b, start=(m == 0 and i == 0),
                                          stop=(m == 1 and i == 2), skip_group_check=True)
        mm.then_inc(S.unit_done[s], 1)
        pe.wait_ge(S.kcb_ready, L + 1)
        for b in range(QB):
            for t in range(B_REP):
                o = S.X[b // 2][:, (b % 2) * 256:(b % 2 + 1) * 256].rearrange("p (g t n) -> p g t n", g=2, t=B_REP)[:, :, t, :]
                mm = nc.tensor.matmul(o, S.q[:, t * SEQ + b * P:t * SEQ + (b + 1) * P],
                                      S.kcb[:, :].rearrange("p (g n) -> p g n", g=2), start=True, stop=True, skip_group_check=True)
            if b % 2:
                mm.then_inc(S.cs_ready, 1)
        pe.wait_ge(S.vbd_ready, L + 1)
        for h in range(2):
            pe.wait_ge(S.cp_ready, L * 2 + h + 1)
            for k in range(4):
                mm = nc.tensor.transpose(S.X[2 + h][:, k * P:(k + 1) * P], S.wk[4 + h][:, k * P:(k + 1) * P], ident)
            mm.then_inc(S.cpt_ready, 1)
        for b in range(QB):
            pe.wait_ge(S.cpt_copied, L * 2 + b // 2 + 1)
            if b >= 2:
                pe.wait_ge(S.oc_done, L * 4 + b - 1)
            for g in range(2):
                c = ((b % 2) * 2 + g) * P
                mm = nc.tensor.matmul(S.X[b % 2][:, g * 256:(g + 1) * 256], S.wk[6 + b // 2][:, c:c + P],
                                      S.vbd[:, g * 256:(g + 1) * 256], start=True, stop=True, skip_group_check=True)
            mm.then_inc(S.oc_ready, 1)
        pe.wait_ge(S.oc_done, L * 4 + 4)
        pe.wait_ge(S.dw_done, L + 1)
        for t in range(4):
            mm = nc.tensor.matmul(S.X[0][:, :], S.ones[:, :], seq(S.cacc, t), start=(t == 0), stop=(t == 3))
        mm.then_inc(S.cl_mean, 1)
        for t in range(4):
            pe.wait_ge(S.cl_sq, L * 4 + t + 1)
            nc.tensor.matmul(S.X[1][:, :], S.ones[:, :], S.wk[t][:, :], start=(t == 0), stop=(t == 3)).then_inc(S.cl_var, 1)
        pe.wait_ge(S.un_ready, L * 4 + 4)
        for u in (B_PW2, B_PW2 + 1):
            pairs_pe(S, pe, L, u, S.xh, S.xl, 4)
        pe.wait_ge(S.lru_done, L + 1)
        for u in range(B_OUTL, B_OUTL + 4):
            pairs_pe(S, pe, L, u, S.xh, S.xl, 0)
        pe.wait_ge(S.mc_ready, L * 4 + 4)
        for u in range(B_OUTC, B_OUTC + 4):
            pairs_pe(S, pe, L, u, S.mch, S.mcl, 0)
        with pe.Fori(0, B_REP) as t:
            for s in range(SLOTS):
                pe.wait_ge(S.bank_free[s], GB(L, B_OUTC) + 2)
            pe.wait_ge(S.q_staged, L * B_REP + t + 1)
            attn_pe(S, pe, S.nsa, L * 64 + t * 16, nsa_steps(S, t), ident)
        pe.wait_ge(S.nsa.out, (L + 1) * 64 + 2)
        for k in range(4):
            for b in range(QB):
                mm = nc.tensor.transpose(S.X[k][:, b * P:(b + 1) * P], S.ot2[:, b * 512 + k * P:b * 512 + (k + 1) * P], ident)
            mm.then_inc(S.bt_ready, 1)
        pe.wait_ge(S.mn_ready, L * 4 + 4)
        for u in range(B_OUTN, B_OUTN + 4):
            pairs_pe(S, pe, L, u, S.mnh, S.mnl, 0)
    rms_pe(S, pe, DEPTH)


def b_scalar(S, act, T):
    nc = S.nc

    def take(L, u, i, out, func, **kw):
        s = u % SLOTS
        act.wait_ge(S.unit_done[s], GB(L, u, i) + 1)
        nc.scalar.activation(out, S.ps[s][:, :], func, **kw).then_inc(S.bank_free[s], 1)
        act_split(S, act, u, GB(L, u, i))

    def used(L, u):
        act.wait_ge(S.unit_done[u % SLOTS], GB(L, u) + 1)
        act_split(S, act, u, GB(L, u))

    act.wait_ge(S.res_ready, 1)
    act.dma_start(S.prmB[:, :], T["prm_b"]).then_inc(S.pb_landed, 16)
    act.dma_start(S.pos[:, :], T["pos"].to_broadcast([P, SEQ])).then_inc(S.pb_landed, 16)
    act.wait_ge(S.ang_ready, 1)
    nc.scalar.activation(S.sin[:, :], S.wk[0][:, :], ACT.Sin)
    nc.scalar.activation(S.cos[:, :], S.wk[1][:, :], ACT.Sin, scale=-1.0, bias=S.halfpi[:, :]).then_inc(S.tab_ready, 1)
    act.drain()
    with act.Fori(0, DEPTH) as L:
        rms_act(S, act, L, True)
        act.wait_ge(S.lam_in, L + 1)
        nc.scalar.activation(S.lam[0][:, :], S.lam[0][:, :], ACT.Exp).then_inc(S.lam_out, 1)
        for j in range(SLOTS):
            c = j * UC_W + CONV_K - 1
            take(L, B_GA + j, 0, S.uc[:, c:c + SEQ], ACT.Copy, scale=0.5)
        for j in range(SLOTS):
            if j >= 2:
                act.wait_ge(S.glu_done, L * 4 + j - 1)
            take(L, B_GB + j, 0, S.wk[6 + j % 2][:, :], ACT.Tanh, scale=0.5)
        for j in range(SLOTS):
            c = j * UP_W + LRU_K - 1
            take(L, B_U + j, 0, S.up[:, c:c + SEQ], ACT.Copy)
        for u0, z in ((B_ZL, S.zl), (B_ZC, S.zc), (B_ZN, S.zn)):
            for j in range(SLOTS):
                take(L, u0 + j, 0, seq(z, j), ACT.Silu)
        for j in range(SLOTS):
            take(L, B_Q + j, 0, seq(S.q, j), ACT.Copy, scale=HD ** -0.5)
        for j, name in enumerate(("kc", "ks", "kw", "vc", "vs", "vw")):
            take(L, B_KV + j, 0, S.kv[name][:, :], ACT.Copy)
        take(L, B_G, 0, S.kv["gl"][:, :], ACT.Tanh, scale=0.5, bias=S.curB[:, PB_BG:PB_BG + 1])
        for v, name in enumerate("sw"):
            act.wait_ge(S.bvt_ready, L * 3 + v + 1)
            nc.scalar.activation(S.vtok[name][:, :], S.X[2 + v][:, :], ACT.Copy).then_inc(S.bvt_done, 1)
        for kv, name in enumerate(("kc", "vc")):
            if kv == 0:
                act.wait_ge(S.b_rope_done, L * NROPE + 1)
            for g in range(2):
                for l2 in range(2):
                    src = S.kv[name][64 * g:64 * g + 64, :]
                    o = S.blk[kv][64 * l2:64 * l2 + 64, :].rearrange("p (a g n) -> p a g n", a=16, g=2)[:, :, g, :]
                    for half in range(2):
                        i = src[:, 16 * half:16 * half + 16 * NBLK].rearrange("p (n a l) -> p a n l", a=8, l=2)[:, :, :, l2]
                        m = nc.scalar.activation(o[:, 8 * half:8 * half + 8, :], i, ACT.Copy)
            m.then_inc(S.blk_raw, 1)
        act.wait_ge(S.blk_ready, L * 2 + 2)
        for t in range(4):
            act.wait_ge(S.lru_ready, L * 4 + t + 1)
            nc.scalar.activation(seq(S.la, t), S.X[2 * (t % 2)][:, :], ACT.Tanh, scale=0.5, bias=S.curB[:, PB_BA + t:PB_BA + t + 1])
            nc.scalar.activation(seq(S.lri, t), S.X[2 * (t % 2) + 1][:, :], ACT.Tanh, scale=0.5,
                                 bias=S.curB[:, PB_BI + t:PB_BI + t + 1]).then_inc(S.lru_gate, 1)
        used(L, B_BD)
        act.wait_ge(S.nla_ready, L + 1)
        nc.scalar.activation(S.ls[:, :], S.la[:, :], ACT.Tanh).then_inc(S.s_ready, 1)
        act.drain()
        nc.scalar.activation(S.la[:, :], S.la[:, :], ACT.Exp, scale=-1.0).then_inc(S.a_ready, 1)
        act.wait_ge(S.b2_ready, L + 1)
        nc.scalar.activation(S.ls[:, :], S.ls[:, :], ACT.Sqrt).then_inc(S.beta_ready, 1)
        for kv in range(2):
            for u in range(4):
                used(L, B_CMP1 + 4 * kv + u)
            if kv == 0:
                act.wait_ge(S.lru_done, L + 1)
            nc.scalar.activation(S.wk[0][:, kv * 2 * HD:kv * 2 * HD + 2 * NB2].rearrange("p (m n) -> p m n", m=2),
                                 S.X[kv][:, 0:2 * HD].rearrange("p (m n) -> p m n", m=2)[:, :, 0:NB2],
                                 ACT.Silu).then_inc(S.hid_act, 1)
        used(L, B_CMP2)
        used(L, B_CMP2 + 1)
        for h in range(2):
            act.wait_ge(S.cexp_in, L * 2 + h + 1)
            nc.scalar.activation(S.wk[4 + h][:, :], S.wk[4 + h][:, :], ACT.Exp).then_inc(S.cexp_out, 1)
        for h in range(2):
            act.wait_ge(S.cpt_ready, L * 2 + h + 1)
            nc.scalar.activation(S.wk[6 + h][:, :], S.X[2 + h][:, :], ACT.Copy).then_inc(S.cpt_copied, 1)
        for t in range(4):
            act.wait_ge(S.cl_d, L * 4 + t + 1)
            nc.scalar.activation(S.wk[t][:, :], seq(S.cacc, t), ACT.Square).then_inc(S.cl_sq, 1)
        act.wait_ge(S.cl_var, L * 4 + 4)
        nc.scalar.activation(S.wk[4][:, :], S.X[1][:, :], ACT.Sqrt, scale=2.0, bias=S.eps2[:, :]).then_inc(S.cl_std, 1)
        for t in range(4):
            act.wait_ge(S.cl_y, L * 4 + t + 1)
            nc.scalar.activation(seq(S.cacc, t), seq(S.cacc, t), ACT.Silu)
            act.drain()
            nc.scalar.activation(seq(S.xh, 4 + t), seq(S.cacc, t), ACT.Copy).then_inc(S.cl_hi, 1)
        used(L, B_PW2)
        used(L, B_PW2 + 1)
        for t in range(4):
            act.wait_ge(S.mc_y, L * 4 + t + 1)
            nc.scalar.activation(seq(S.mch, t), seq(S.zc, t), ACT.Copy).then_inc(S.mc_hi, 1)
        for u in range(B_OUTL, B_OUTC + 4):
            used(L, u)
        with act.Fori(0, B_REP) as t:
            nc.scalar.activation(S.wk[0][:, :], cols(S.q, t), ACT.Copy).then_inc(S.q_staged, 1)
            attn_act(S, act, S.nsa, L * 64 + t * 16, nsa_steps(S, t))
        for k in range(4):
            act.wait_ge(S.mn_y, L * 4 + k + 1)
            nc.scalar.activation(seq(S.mnh, k), seq(S.zn, k), ACT.Copy).then_inc(S.mn_hi, 1)
        for u in range(B_OUTN, B_OUTN + 4):
            used(L, u)
    rms_act(S, act, DEPTH, False)


def free_bank(S, dve, u):
    s = u % SLOTS
    S.nc.vector.memset(S.tick[:, 24 + s:25 + s], 0.0).then_inc(S.bank_free[s], 1)


def b_rope_tables(S, dve):
    nc = S.nc
    ang, k, r = S.wk[2][:, :], S.wk[3][:, :], S.wk[0][:, :]
    two_pi = (6.25, 0.033203125, 2 * math.pi - 6.25 - 0.033203125)
    magic = 1.5 * 2.0 ** 23
    dve.wait_ge(S.pb_landed, 32)
    nc.vector.tensor_copy(ang, S.pos[:, :])
    dve.drain()
    nc.vector.tensor_scalar(ang, ang, S.prmB[:, PB_INV:PB_INV + 1], None, ALU.mult)
    dve.drain()
    nc.vector.tensor_scalar(k, ang, 1 / (2 * math.pi), magic, ALU.mult, ALU.add)
    dve.drain()
    nc.vector.tensor_scalar(k, k, magic, None, ALU.subtract)
    dve.drain()
    nc.vector.scalar_tensor_tensor(out=r, in0=k, scalar=-two_pi[0], in1=ang, op0=ALU.mult, op1=ALU.add)
    for part in two_pi[1:]:
        dve.drain()
        nc.vector.scalar_tensor_tensor(out=r, in0=k, scalar=-part, in1=r, op0=ALU.mult, op1=ALU.add)
    dve.drain()
    nc.vector.tensor_scalar(r, r, 3.1415925, -3.1415925, ALU.min, ALU.max)
    dve.drain()
    nc.vector.scalar_tensor_tensor(out=S.wk[1][:, :], in0=r, scalar=-1.0, in1=r, op0=ALU.mult, op1=ALU.max).then_inc(S.ang_ready, 1)


def b_softplus(S, dve, L):
    nc = S.nc
    e, y, y2, p, m = (t[:, :] for t in S.lam)
    lam = S.curB[:, PB_LAM:PB_LAM + 4]
    dve.wait_ge(S.lam_out, L + 1)
    nc.vector.tensor_scalar(y, e, 2.0, None, ALU.add)
    dve.drain()
    nc.vector.reciprocal(y, y)
    dve.drain()
    nc.vector.tensor_tensor(y, y, e, ALU.mult)
    dve.drain()
    nc.vector.tensor_tensor(y2, y, y, ALU.mult)
    dve.drain()
    nc.vector.tensor_scalar(p, y2, 1 / 15, None, ALU.mult)
    for k in range(13, 1, -2):
        dve.drain()
        nc.vector.scalar_tensor_tensor(out=p, in0=p, scalar=1 / k, in1=y2, op0=ALU.add, op1=ALU.mult)
    dve.drain()
    nc.vector.scalar_tensor_tensor(out=p, in0=p, scalar=1.0, in1=y, op0=ALU.add, op1=ALU.mult)
    nc.vector.tensor_scalar(m, lam, -4.0, 0.0, ALU.mult, ALU.max)
    dve.drain()
    nc.vector.scalar_tensor_tensor(out=lam, in0=p, scalar=8.0, in1=m, op0=ALU.mult, op1=ALU.add)
    dve.drain()


def b_vector(S, dve):
    nc = S.nc
    col = lambda c: S.curB[:, c:c + 1]
    stt = nc.vector.scalar_tensor_tensor
    dve.drain()
    nc.vector.tensor_tensor(S.res[:, :], S.xh[:, :].bitcast(F32), S.xl[:, :].bitcast(F32), ALU.add).then_inc(S.res_ready, 1)
    b_rope_tables(S, dve)
    with dve.Fori(0, DEPTH) as L:
        nc.vector.tensor_copy(S.curB[:, :], cols(S.prmB, L, PB_N))
        for t, w, pad in ((S.uc, UC_W, CONV_K - 1), (S.up, UP_W, LRU_K - 1)):
            for j in range(4):
                nc.vector.memset(t[:, j * w:j * w + pad], 0.0)
        dve.drain()
        half = S.curB[:, PB_BG:PB_LAM]
        nc.vector.tensor_scalar(half, half, 0.5, None, ALU.mult)
        lam = S.curB[:, PB_LAM:PB_LAM + 4]
        stt(out=S.lam[0][:, :], in0=lam, scalar=-1.0, in1=lam, op0=ALU.mult, op1=ALU.min).then_inc(S.lam_in, 1)
        rms_dve(S, dve, L)
        b_softplus(S, dve, L)
        for j in range(4):
            u = B_GB + j
            dve.wait_ge(S.bank_free[u % SLOTS], GB(L, u) + 2)
            t = S.uc[:, j * UC_W + CONV_K - 1:(j + 1) * UC_W]
            stt(out=t, in0=S.wk[6 + j % 2][:, :], scalar=1.0, in1=t, op0=ALU.add, op1=ALU.mult).then_inc(S.glu_done, 1)
        for k in range(LRU_K):
            for t in range(4):
                src, o, w = S.up[:, t * UP_W + k:t * UP_W + k + SEQ], seq(S.xc, t), col(PB_LCW + t * LRU_K + k)
                if k == 0:
                    dve.wait_ge(S.bank_free[t], GB(L, B_U + t) + 2)
                    nc.vector.tensor_scalar(o, src, w, col(PB_LCB + t), ALU.mult, ALU.add)
                else:
                    stt(out=o, in0=src, scalar=w, in1=o, op0=ALU.mult, op1=ALU.add)
            dve.drain()
        for t in range(4):
            nc.vector.tensor_scalar(seq(S.cacc, t), S.uc[:, t * UC_W:t * UC_W + SEQ], col(PB_DW + t * CONV_K), col(PB_DWB + t),
                                    ALU.mult, ALU.add)
        dve.drain()
        with dve.Fori(1, CONV_K) as k:
            for t in range(4):
                stt(out=seq(S.cacc, t), in0=S.uc[:, bass.ds(k + t * UC_W, SEQ)], scalar=S.curB[:, bass.ds(k + (PB_DW + t * CONV_K), 1)],
                    in1=seq(S.cacc, t), op0=ALU.mult, op1=ALU.add)
            dve.drain()
        x4h, x4l = S.xh[:, 0:4 * SEQ], S.xl[:, 0:4 * SEQ]
        dve.wait_ge(S.unit_done[B_G % SLOTS], GB(L, B_G) + 1)
        nc.vector.tensor_copy(x4h, S.xc[:, :]).then_inc(S.dw_done, 1)
        dve.drain()
        nc.vector.tensor_tensor(x4l, S.xc[:, :], x4h.bitcast(F32), ALU.subtract).then_inc(S.xc_split, 1)
        dve.wait_ge(S.bvt_ready, L * 3 + 3)
        nc.vector.tensor_scalar(S.gate[:, :].rearrange("p (b c) -> p b c", b=QB),
                                S.X[2][:, :].rearrange("p (b c) -> p b c", b=QB)[:, :, 0:3 * B_HEADS], 1.0, 0.5,
                                ALU.add, ALU.mult).then_inc(S.gl_done, 1)
        dve.wait_ge(S.tab_ready, 1)
        for n, t in enumerate(rope_tiles(S)):
            a, b = S.wk[4 + n % 2][:, :], S.wk[6 + n % 2][:, :]
            nc.vector.tensor_tensor(a, t, S.cos[:, :], ALU.mult)
            dve.wait_ge(S.b_rot_ready, L * NROPE + n + 1)
            nc.vector.tensor_tensor(b, S.X[n % 2][:, :], S.sin[:, :], ALU.mult)
            dve.drain()
            nc.vector.tensor_tensor(t, a, b, ALU.add).then_inc(S.b_rope_done, 1)
        for kv in range(2):
            dve.wait_ge(S.blk_raw, L * 2 + kv + 1)
            t = S.blk[kv][:, :].rearrange("p (a n) -> p a n", a=16)
            pos = S.curB[:, PB_POS + 16 * kv:PB_POS + 16 * kv + 16]
            c = (4 + 2 * kv) * SEQ
            bh, bl = S.xh[:, c:c + 16 * NB2], S.xl[:, c:c + 16 * NB2]
            nc.vector.tensor_tensor(t, t, pos.unsqueeze(2).to_broadcast([P, 16, NB2]), ALU.add)
            dve.drain()
            nc.vector.tensor_copy(bh, S.blk[kv][:, :])
            dve.drain()
            nc.vector.tensor_tensor(bl, S.blk[kv][:, :], bh.bitcast(F32), ALU.subtract).then_inc(S.blk_ready, 1)
        dve.wait_ge(S.lru_gate, L * 4 + 4)
        free_bank(S, dve, B_BD)
        for t in range(4):
            m = nc.vector.tensor_scalar(seq(S.la, t), seq(S.la, t), 1.0, col(PB_LAM + t), ALU.add, ALU.mult)
        m.then_inc(S.nla_ready, 1)
        stt(out=S.lri[:, :], in0=S.lri[:, :], scalar=1.0, in1=S.xc[:, :], op0=ALU.add, op1=ALU.mult)
        dve.wait_ge(S.s_ready, L + 1)
        nc.vector.tensor_scalar(S.lrt[:, :], S.ls[:, :], 1.0, None, ALU.add)
        dve.drain()
        nc.vector.reciprocal(S.lrt[:, :], S.lrt[:, :])
        dve.drain()
        stt(out=S.ls[:, :], in0=S.ls[:, :], scalar=2.0, in1=S.lrt[:, :], op0=ALU.mult, op1=ALU.mult).then_inc(S.b2_ready, 1)
        dve.wait_ge(S.beta_ready, L + 1)
        stt(out=S.lri[:, :], in0=S.lri[:, :], scalar=0.5, in1=S.ls[:, :], op0=ALU.mult, op1=ALU.mult)
        dve.drain()
        for t in range(4):
            dve.wait_ge(S.a_ready, L + 1)
            nc.vector.tensor_tensor_scan(seq(S.lrt, t), seq(S.la, t), seq(S.lri, t), 0.0, ALU.mult, ALU.add)
        dve.drain()
        nc.vector.tensor_tensor(S.la[:, :], S.lrt[:, :], S.zl[:, :], ALU.mult)
        dve.drain()
        nc.vector.tensor_copy(x4h, S.la[:, :])
        dve.drain()
        nc.vector.tensor_tensor(x4l, S.la[:, :], x4h.bitcast(F32), ALU.subtract).then_inc(S.lru_done, 1)
        nc.vector.memset(S.kcb[:, :], 0.0)
        nc.vector.memset(S.vbd[:, :], 0.0)
        dve.drain()
        for kv in range(2):
            dve.wait_ge(S.hid_act, L * 2 + kv + 1)
            for u in range(4):
                free_bank(S, dve, B_CMP1 + 4 * kv + u)
            h = S.wk[0][:, kv * 2 * HD:kv * 2 * HD + 2 * NB2]
            if kv == 0:
                nc.vector.tensor_copy(S.hkh[:, :], h)
                dve.drain()
                nc.vector.tensor_tensor(S.hkl[:, :], h, S.hkh[:, :].bitcast(F32), ALU.subtract).then_inc(S.hid_split, 1)
            else:
                nc.vector.memset(S.hvh[:, :].bitcast(F32), 0.0)
                nc.vector.memset(S.hvl[:, :].bitcast(F32), 0.0)
                dve.drain()
                rep = lambda x, i: x[:, i * P:(i + 1) * P].rearrange("p (j n) -> p j n", j=4)[:, :, 0:NBLK]
                one = lambda i: h[:, i * NBLK:(i + 1) * NBLK].unsqueeze(1).to_broadcast([P, 4, NBLK])
                for i in range(4):
                    nc.vector.tensor_copy(rep(S.hvh, i), one(i))
                dve.drain()
                for i in range(4):
                    m = nc.vector.tensor_tensor(rep(S.hvl, i), one(i), rep(S.hvh, i).bitcast(F32), ALU.subtract)
                m.then_inc(S.hid_split, 1)
        dve.wait_ge(S.unit_done[B_CMP2 % SLOTS], GB(L, B_CMP2) + 1)
        for g in range(2):
            m = nc.vector.tensor_copy(S.kcb[64 * g:64 * g + 64, 32 * g:32 * g + NBLK],
                                      S.X[2][64 * g:64 * g + 64, g * NBLK:(g + 1) * NBLK])
        m.then_inc(S.kcb_ready, 1)
        dve.wait_ge(S.unit_done[(B_CMP2 + 1) % SLOTS], GB(L, B_CMP2 + 1) + 1)
        for g in range(2):
            for t in range(4):
                m = nc.vector.tensor_copy(S.vbd[32 * t:32 * t + 32, (4 * g + t) * HD:(4 * g + t + 1) * HD],
                                          S.X[3][32 * t:32 * t + 32, g * HD:(g + 1) * HD])
        m.then_inc(S.vbd_ready, 1)
        free_bank(S, dve, B_CMP2)
        free_bank(S, dve, B_CMP2 + 1)
        for h in range(2):
            dve.wait_ge(S.cs_ready, L * 2 + h + 1)
            p4 = S.wk[4 + h][:, :].rearrange("p (b t n) -> p b t n", b=2, t=B_HEADS)
            p3 = S.wk[4 + h][:, :].rearrange("p (r n) -> p r n", n=32)
            mask = S.cmask[:, 64 * h:64 * h + 64].rearrange("p (b n) -> p b n", b=2).unsqueeze(2).to_broadcast([P, 2, B_HEADS, 32])
            mx = S.cmx[:, 16 * h:16 * h + 16]
            nc.vector.tensor_tensor(p4, S.X[h][:, :].rearrange("p (b t n) -> p b t n", b=2, t=B_HEADS), mask, ALU.add)
            dve.drain()
            nc.vector.tensor_reduce(mx, p3, AX, ALU.max)
            dve.drain()
            nc.vector.tensor_scalar(mx, mx, NEG / 10, None, ALU.max)
            dve.drain()
            nc.vector.tensor_tensor(p3, p3, mx.unsqueeze(2).to_broadcast([P, 16, 32]), ALU.subtract).then_inc(S.cexp_in, 1)
        for h in range(2):
            dve.wait_ge(S.cexp_out, L * 2 + h + 1)
            p3 = S.wk[4 + h][:, :].rearrange("p (r n) -> p r n", n=32)
            sm = S.csum[:, 16 * h:16 * h + 16]
            nc.vector.tensor_reduce(sm, p3, AX, ALU.add)
            dve.drain()
            nc.vector.tensor_scalar(sm, sm, 1e-30, None, ALU.max)
            dve.drain()
            nc.vector.reciprocal(sm, sm)
            dve.drain()
            gate = S.gate[:, 48 * h:48 * h + 48].rearrange("p (r c) -> p r c", c=3)[:, :, 0]
            nc.vector.tensor_tensor(sm, sm, gate, ALU.mult)
            dve.drain()
            nc.vector.tensor_tensor(p3, p3, sm.unsqueeze(2).to_broadcast([P, 16, 32]), ALU.mult).then_inc(S.cp_ready, 1)
        for b in range(QB):
            dve.wait_ge(S.oc_ready, L * 4 + b + 1)
            nc.vector.tensor_copy(S.ot2[:, b * 512:(b + 1) * 512], S.X[b % 2][:, :]).then_inc(S.oc_done, 1)
        dve.wait_ge(S.cl_mean, L + 1)
        for t in range(4):
            stt(out=seq(S.cacc, t), in0=S.X[0][:, :], scalar=-2.0, in1=seq(S.cacc, t), op0=ALU.mult, op1=ALU.add).then_inc(S.cl_d, 1)
        dve.wait_ge(S.cl_std, L + 1)
        nc.vector.reciprocal(S.wk[5][:, :], S.wk[4][:, :])
        dve.drain()
        for t in range(4):
            nc.vector.tensor_tensor(seq(S.cacc, t), seq(S.cacc, t), S.wk[5][:, :], ALU.mult)
        dve.drain()
        for t in range(4):
            nc.vector.tensor_scalar(seq(S.cacc, t), seq(S.cacc, t), col(PB_LNG + t), col(PB_LNB + t),
                                    ALU.mult, ALU.add).then_inc(S.cl_y, 1)
        for t in range(4):
            dve.wait_ge(S.cl_hi, L * 4 + t + 1)
            nc.vector.tensor_tensor(seq(S.xl, 4 + t), seq(S.cacc, t), seq(S.xh, 4 + t).bitcast(F32), ALU.subtract).then_inc(S.un_ready, 1)
        for d in range(2):
            u = B_PW2 + d
            s = u % SLOTS
            dve.wait_ge(S.unit_done[s], GB(L, u) + 1)
            nc.vector.tensor_tensor(seq(S.zc, 2 * d), seq(S.zc, 2 * d), S.ps[s][:, :], ALU.mult).then_inc(S.mc_y, 1)
            nc.vector.tensor_tensor(seq(S.zc, 2 * d + 1), seq(S.zc, 2 * d + 1), S.X[s][:, :], ALU.mult).then_inc(S.mc_y, 1)
            dve.drain()
            free_bank(S, dve, u)
        for t in range(4):
            dve.wait_ge(S.mc_hi, L * 4 + t + 1)
            nc.vector.tensor_tensor(seq(S.mcl, t), seq(S.zc, t), seq(S.mch, t).bitcast(F32), ALU.subtract).then_inc(S.mc_ready, 1)

        def add_out(u0):
            for j in range(4):
                s = (u0 + j) % SLOTS
                dve.wait_ge(S.unit_done[s], GB(L, u0 + j) + 1)
                nc.vector.tensor_tensor(seq(S.res, 2 * j), seq(S.res, 2 * j), S.ps[s][:, :], ALU.add)
                nc.vector.tensor_tensor(seq(S.res, 2 * j + 1), seq(S.res, 2 * j + 1), S.X[s][:, :],
                                        ALU.add).then_inc(S.bank_free[s], 1)
            dve.drain()

        add_out(B_OUTL)
        add_out(B_OUTC)
        with dve.Fori(0, B_REP) as t:
            attn_dve(S, dve, S.nsa, L * 64 + t * 16, nsa_steps(S, t))
        for k in range(4):
            dve.wait_ge(S.bt_ready, L * 4 + k + 1)
            nc.vector.tensor_tensor(seq(S.zn, k), seq(S.zn, k), S.X[k][:, :], ALU.mult).then_inc(S.mn_y, 1)
        for k in range(4):
            dve.wait_ge(S.mn_hi, L * 4 + k + 1)
            nc.vector.tensor_tensor(seq(S.mnl, k), seq(S.zn, k), seq(S.mnh, k).bitcast(F32), ALU.subtract).then_inc(S.mn_ready, 1)
        add_out(B_OUTN)
        nc.vector.memset(S.tick[:, 28:29], 0.0).then_inc(S.res_ready, 1)
    dve.wait_ge(S.rms_std, DEPTH + 1)
    nc.vector.reciprocal(S.wk[3][:, :], S.wk[2][:, :])
    dve.drain()
    for j in range(KT):
        stt(out=seq(S.res, j), in0=seq(S.res, j), scalar=S.prmB[:, PB_FINAL + j:PB_FINAL + j + 1], in1=S.wk[3][:, :],
            op0=ALU.mult, op1=ALU.mult).then_inc(S.y_done, 1)


def prime(S, dve, sems):
    for n, sm in enumerate([sm for sm, times in sems for _ in range(times)]):
        S.nc.vector.memset(S.tick[:, n:n + 1], 0.0).then_inc(sm, 1)


def setup_sync(S, sp, T):
    for dst, src in ((S.con, T["con"]), (S.cos, T["cos"]), (S.sin, T["sin"]), (S.prmA, T["prm_a"]), (S.t, T["x"]), (S.cmask, T["cmask"])):
        sp.dma_start(dst[:, :], src).then_inc(S.con_landed, 16)


def setup_vector(S, dve):
    nc = S.nc
    prime(S, dve, [(b, 1) for b in S.bank_free] + [(S.stk_oev, 1), (S.merge_x, 2), (S.ffn_h, 2), (S.y_ready, 2),
                                                   (S.fox.out, 2), (S.dsa.out, 2), (S.nsa.out, 2)])
    nc.vector.memset(S.ones[:, :], 1.0 / D)
    nc.vector.memset(S.negones[:, :], -1.0)
    nc.vector.memset(S.eps[:, :], LN_EPS)
    nc.vector.memset(S.eps2[:, :], RMS_EPS)
    nc.vector.memset(S.halfpi[:, :], math.pi / 2)
    dve.wait_ge(S.con_landed, 16 * 6)
    for dst, c in ((S.idb, C_ID), (S.causb, C_CAUS), (S.strictb, C_STRICT), (S.chunkb, C_CHUNK)):
        nc.vector.tensor_copy(dst[:, :], S.con[:, c:c + P])
    nc.vector.tensor_copy(S.xh[:, :], S.t[:, :])
    dve.drain()
    for k in range(KT):
        nc.vector.tensor_tensor(S.xl[:, k * SEQ:(k + 1) * SEQ], S.t[:, k * SEQ:(k + 1) * SEQ],
                                S.xh[:, k * SEQ:(k + 1) * SEQ].bitcast(F32), ALU.subtract).then_inc(S.x_ready, 1)


def program(nc, T, out):
    with ExitStack() as ctx:
        S = plan(nc, ctx)
        groups = T["w"].shape[0] // SLOTS
        block = ctx.enter_context(nc.Block())

        @block.sync
        def _(sp):
            setup_sync(S, sp, T)
            sp_stream(S, sp, T["w"], groups)
            for j in range(KT):
                sp.wait_ge(S.y_done, j + 1)
                sp.dma_start(out[:, j * SEQ:(j + 1) * SEQ], seq(S.res, j)).then_inc(S.out_done, 16)
            sp.wait_ge(S.out_done, 16 * KT)

        @block.gpsimd
        def _(pool):
            pool_split(S, pool, groups)

        @block.tensor
        def _(pe):
            a_tensor(S, pe)
            b_tensor(S, pe)

        @block.scalar
        def _(act):
            a_scalar(S, act, T["p"])
            b_scalar(S, act, T)

        @block.vector
        def _(dve):
            setup_vector(S, dve)
            a_vector(S, dve)
            b_vector(S, dve)


def feature_major(a):
    n, f = a.shape
    return np.ascontiguousarray(a.reshape(n, f // P, P).transpose(2, 1, 0).reshape(P, -1))


def unit_of(w):
    return w.reshape(KT, P, P).transpose(1, 0, 2).reshape(P, KT * P)


def units_of(w):
    return [unit_of(w[:, c:c + P]) for c in range(0, w.shape[1], P)]


def units_a(a, l):
    w = np.asarray(a["w_in"][l])
    sizes = (384, 384, 384, 6, 320, 320, 320, 320, 64, 64, 512, 64, 8, 3 * D)
    at = np.cumsum((0,) + sizes)
    fq, fk, fv, ff, sq, sk, sv, dq, dk, dv, iq, ik, iw, g = (w[:, at[n]:at[n + 1]] for n in range(14))
    zero = lambda n: np.zeros((D, n), w.dtype)
    cat = lambda *x: np.concatenate(x, axis=1)
    proj = cat(fq, sq[:, :256], fk, sk[:, :256], fv, sv[:, :256], sv[:, 256:], dv,
               ik, ff, zero(2), iw, zero(16), ff, zero(26), sq[:, 256:], dq[:, 256:], sk[:, 256:], dk, dk, ik,
               dq[:, :256], iq)
    up = np.concatenate([np.asarray(a[k][l]) for k in ("w_up_fox", "w_up_sb", "w_up_dsa")], axis=0)
    g0, g1, g2 = (units_of(g[:, n * D:(n + 1) * D]) for n in range(3))
    mix = [m for three in zip(g1, g2, units_of(up)) for m in three]
    fin, fout = np.asarray(a["w_ff_in"][l]), np.asarray(a["w_ff_out"][l])
    ffn = [m for q in range(4) for m in units_of(fin[:, q * D:(q + 1) * D]) + units_of(fout[q * D:(q + 1) * D])]
    ple = np.asarray(a["w_ple"][l]).reshape(2, P, 2, 4, P).transpose(2, 1, 3, 0, 4).reshape(2, P, KT * P)
    all_ = (units_of(proj) + g0 + mix + units_of(np.asarray(a["w_out"][l])) + ffn + list(ple)
            + units_of(np.asarray(a["w_ple_gate"][l])))
    assert len(all_) == A_UNITS
    return all_


def units_b(a, l):
    w = np.asarray(a["w_in_2"][l])
    sizes = (512, 128, 128, 128, 128, 128, 128, 24, 512, 512, 512, 512, 512, 512)
    at = np.cumsum((0,) + sizes)
    q, kc, vc, ks, vs, kw, vw, gl, zn, ul, zl, ga, gb, zc = (w[:, at[n]:at[n + 1]] for n in range(14))
    q = q.reshape(D, 2, B_REP, HD).transpose(0, 2, 1, 3).reshape(D, 512)
    gl = np.concatenate([gl, np.zeros((D, P - 24), w.dtype)], axis=1)
    plain = units_of(np.concatenate([ga, gb, ul, zl, zc, zn, q, kc, ks, kw, vc, vs, vw, gl], axis=1))
    bd = np.zeros((KT, P, P), w.dtype)
    for t in range(4):
        for d, name in enumerate(("lru_w_a_2", "lru_w_i_2")):
            for e in range(2):
                bd[2 * t + d, 64 * e:64 * e + 64, 64 * e:64 * e + 64] = np.asarray(a[name])[l, 2 * t + e]
    w1, w2 = np.asarray(a["cmp_w1_2"][l]), np.asarray(a["cmp_w2_2"][l])
    c1 = [unit_of(w1[kv, h * D:(h + 1) * D, m * P:(m + 1) * P]) for kv in range(2) for m in range(2) for h in range(2)]
    c2 = np.zeros((2, D, P), w.dtype)
    c2[0, 0:256] = np.concatenate([w2[0], w2[0]], axis=1)
    c2[1, 0:256, 0:HD] = w2[1]

    def pairs(m):
        return [np.concatenate([unit4(m[:, c + o * P:c + (o + 1) * P]) for o in range(2)], axis=1)
                for c in range(0, m.shape[1], 2 * P)]

    def unit4(m):
        return m.reshape(4, P, P).transpose(1, 0, 2).reshape(P, 4 * P)

    wo = np.asarray(a["w_out_2"][l])
    all_ = (plain + [bd.transpose(1, 0, 2).reshape(P, KT * P)] + c1 + [unit_of(c2[0]), unit_of(c2[1])]
            + pairs(np.asarray(a["conv_w_pw2_2"][l])) + pairs(wo[512:1024]) + pairs(wo[1024:]) + pairs(wo[:512]))
    assert len(all_) == B_UNITS
    return all_


def params_b(a):
    out = np.zeros((P, SEQ), np.float32)

    def tiles(v, n):
        return np.asarray(v).reshape(n, P).T

    for l in range(DEPTH):
        c = out[:, l * PB_N:(l + 1) * PB_N]
        c[:, PB_G:PB_G + KT] = tiles(a["norm_g_2"][l], KT)
        c[0:3 * B_HEADS, PB_BG] = np.asarray(a["b_gate_2"][l])
        for at, name in ((PB_BA, "lru_b_a_2"), (PB_BI, "lru_b_i_2"), (PB_LAM, "lru_lam_2"), (PB_LCB, "lru_conv_b_2"),
                         (PB_DWB, "conv_dw_b_2"), (PB_LNG, "conv_ln_g_2"), (PB_LNB, "conv_ln_b_2")):
            c[:, at:at + 4] = tiles(a[name][l], 4)
        c[:, PB_LCW:PB_LCW + 16] = np.asarray(a["lru_conv_w_2"][l]).reshape(LRU_K, 4, P).transpose(2, 1, 0).reshape(P, -1)
        c[:, PB_DW:PB_DW + 4 * CONV_K] = np.asarray(a["conv_dw_w_2"][l]).reshape(CONV_K, 4, P).transpose(2, 1, 0).reshape(P, -1)
        c[:, PB_POS:PB_POS + 32] = np.asarray(a["cmp_pos_2"][l]).reshape(32, P).T
    out[:, PB_FINAL:PB_FINAL + KT] = tiles(a["final_g_2"], KT)
    out[:, PB_INV] = np.tile(np.float32(10000.0) ** (-np.arange(0, HD, 2, dtype=np.float32) / np.float32(HD)), 4)
    return out


def cmp_mask():
    t = np.arange(P)[:, None, None] + P * np.arange(QB)[None, :, None]
    n = np.arange(32)[None, None, :]
    return np.where((16 * n + 31 <= t) & (n < NBLK), 0.0, NEG).astype(np.float32).reshape(P, QB * 32)


def constants():
    c = np.zeros((P, C_N), np.float32)
    i, j = np.arange(P)[:, None], np.arange(P)[None, :]
    c[:, C_ID:C_ID + P] = i == j
    half, same = HD // 2, i // HD == j // HD
    c[:, C_ROT:C_ROT + P] = np.where(same & (i == j + half), -1.0, np.where(same & (i == j - half), 1.0, 0.0))
    c[:, C_TRI:C_TRI + P] = np.where(i >= j, -1.0, 0.0)
    c[:, C_CAUS:C_CAUS + P] = np.where(j > i, NEG, 0.0)
    c[:, C_STRICT:C_STRICT + P] = np.where(i >= j, NEG, 0.0)
    c[:, C_ST01:C_ST01 + P] = i < j
    c[:, C_CHUNK:C_CHUNK + P] = np.where(j // 64 > i // 64, NEG, 0.0)
    for h in range(6):
        c[96 + h, C_QA + h] = 1.0
        c[64 + h, C_QB + h] = 1.0
    c[64:96, C_KA] = -1.0
    c[96:, C_KB] = 1.0
    return c


def rope_constants():
    inv = np.float32(10000.0) ** (-np.arange(32, dtype=np.float32) / np.float32(32))
    ang = (np.arange(SEQ, dtype=np.float32)[:, None] * inv[None, :]).astype(np.float32)
    rep = lambda t: np.ascontiguousarray(np.tile(t.T, (4, 1)).astype(np.float32))
    return rep(np.cos(ang)), rep(np.sin(ang))


def arrays_of(a):
    prm = np.zeros((P, DEPTH, PA_N), np.float32)
    for l in range(DEPTH):
        for c, name in ((PA_G1, "ln1_g"), (PA_B1, "ln1_b"), (PA_G2, "ln2_g"), (PA_B2, "ln2_b")):
            prm[:, l, c:c + KT] = np.asarray(a[name][l]).reshape(KT, P).T
        prm[64:70, l, PA_BF] = np.asarray(a["b_forget"][l])
        prm[96:102, l, PA_BF] = np.asarray(a["b_forget"][l])
    cos, sin = rope_constants()
    units = [u for l in range(DEPTH) for u in units_a(a, l)] + [u for l in range(DEPTH) for u in units_b(a, l)]
    units += [np.zeros((P, KT * P), np.float32)] * SLOTS
    return {
        "x": feature_major(np.asarray(a["x"])[0]),
        "p": np.stack([feature_major(np.asarray(a["p"])[l, 0]) for l in range(DEPTH)]),
        "w": np.stack(units), "con": constants(), "cos": cos, "sin": sin, "prm_a": prm.reshape(P, -1),
        "prm_b": params_b(a), "cmask": cmp_mask(), "pos": np.asarray(a["positions_2"]),
    }


def kernel(**inputs):
    import concourse.bacc as bacc
    from concourse.bass_utils import run_bass_kernel_spmd

    nc = bacc.Bacc("TRN2", target_bir_lowering=False, num_devices=1)
    arrays = arrays_of(inputs)
    T = {k: nc.dram_tensor(k, v.shape, mybir.dt.from_np(v.dtype), kind="ExternalInput").ap() for k, v in arrays.items()}
    out = nc.dram_tensor("out", (P, KT * SEQ), F32, kind="ExternalOutput").ap()
    program(nc, T, out)
    r = run_bass_kernel_spmd(nc, [arrays], core_ids=[0])
    y = np.asarray(r.results[0]["out"]).reshape(P, KT, SEQ)
    return np.ascontiguousarray(y.transpose(2, 1, 0).reshape(1, SEQ, D))
```

```python
from contextlib import ExitStack
import math

import numpy as np

import concourse.bass as bass
from concourse import mybir

F32 = mybir.dt.float32
F32R = mybir.dt.float32r
BF16 = mybir.dt.bfloat16
I32 = mybir.dt.int32
ALU = mybir.AluOpType
ACT = mybir.ActivationFunctionType
AX = mybir.AxisListType.X

P = 128
SEQ = 512
D = 1024
KT = D // P
QB = SEQ // P
HD = 64
SLOTS = 4
DEPTH = 2
NEG = -1e30
MARK = -3e38
ALPHA = (2 * DEPTH) ** 0.25
LN_EPS = 1e-5
TOPK = 128
IDX_HEADS = 8

A_FV, A_SV, A_SDV, A_FQ, A_FK, A_SQ, A_SK = 0, 3, 5, 6, 9, 12, 14
A_IKF, A_S4D4Q, A_S4KDK, A_DKIK, A_DQ, A_IQ = 16, 17, 18, 19, 20, 22
A_NPROJ = 26
A_GATE = A_NPROJ
A_UP = A_GATE + 3 * KT
A_OUT = A_UP + KT
A_PLE = A_OUT + KT
A_FFN = A_PLE + 2
A_PG = A_FFN + 64
A_UNITS = A_PG + KT
assert A_UNITS % SLOTS == 0
A_GROUPS = A_UNITS // SLOTS
A_VT = (0, 1, 2, 3, 4, 5, A_IKF)
A_NVT = len(A_VT)
ROPE_UNITS, FOX_UNITS, STK_UNITS = 0, 4, 16
V_FOX, V_SB, V_S4, V_DSA, V_IW = 0, 384, 640, 704, 6 * P + 72

C_ID, C_ROT, C_TRI, C_CAUS, C_STRICT, C_ST01, C_CHUNK = (P * n for n in range(7))
C_QA = 7 * P
C_QB = C_QA + 6
C_KA = C_QB + 6
C_KB = C_KA + 1
C_N = C_KB + 1

PA_G1, PA_B1, PA_G2, PA_B2, PA_BF, PA_N = 0, 8, 16, 24, 32, 33

B_GA, B_GB, B_U, B_ZL, B_ZC, B_ZN, B_Q, B_KV, B_G = 0, 4, 8, 12, 16, 20, 24, 28, 34
B_BD = 35
B_CMP1 = 36
B_CMP2 = 44
B_PW2 = 46
B_OUTL, B_OUTC, B_OUTN = 48, 52, 56
B_UNITS = 60
B_GROUPS = B_UNITS // SLOTS
B_HEADS, B_REP = 8, 4
CONV_K, LRU_K = 31, 4
UC_W, UP_W = CONV_K - 1 + SEQ, LRU_K - 1 + SEQ
NBLK = 31
NB2 = 2 * NBLK
RMS_EPS = 1e-6
PB_G, PB_BG, PB_BA, PB_BI, PB_LAM, PB_LCW, PB_LCB = 0, 8, 9, 13, 17, 21, 37
PB_DW, PB_DWB, PB_LNG, PB_LNB, PB_POS, PB_N = 41, 165, 169, 173, 177, 209
PB_FINAL, PB_INV = DEPTH * PB_N, DEPTH * PB_N + KT


class Plan:
    pass


def plan(nc, ctx):
    S = Plan()
    S.nc = nc
    base = -(-nc.sbuf_base // 64) * 64

    def at(name, shape, dt, kb):
        return nc.alloc_sbuf_tensor_at(name, shape, dt, offset=base + int(kb * 1024))

    W = KT * P
    WK = 187.75
    S.raw = [at(f"w_raw{s}", [P, W], F32, 4 * s) for s in range(SLOTS)]
    S.wh = [at(f"w_hi{s}", [P, W], F32R, 16 + 4 * s) for s in range(SLOTS)]
    S.wl = [at(f"w_lo{s}", [P, W], F32R, 32 + 4 * s) for s in range(SLOTS)]
    S.xh = at("x_hi", [P, KT * SEQ], F32R, 48)
    S.xl = at("x_lo", [P, KT * SEQ], F32R, 64)
    S.gates = at("gates", [P, 3 * KT * SEQ], F32, 80)
    S.ml = at("merged_lo", [P, KT * SEQ], F32R, 80)
    S.plep = at("ple_proj", [P, KT * SEQ], F32, 80)
    S.qkv = at("proj", [P, A_NPROJ * SEQ], F32, 96)
    S.t = at("ln_in", [P, KT * SEQ], F32, 96)
    S.yacc = at("ffn_sum", [P, KT * SEQ], F32, 96)
    S.praw = at("p_raw", [P, 2 * SEQ], F32, 112)
    S.ph = at("p_hi", [P, 2 * SEQ], F32R, 116)
    S.pl = at("p_lo", [P, 2 * SEQ], F32R, 120)
    S.r = [at(f"idx_relu{e}", [P, SEQ], F32, 96 + 2 * e) for e in range(2)]
    S.sacc = at("idx_sum", [P, 9 * P], F32, 100)
    S.nz0 = at("neg_abs", [P, SEQ], F32, 128)
    S.score = at("idx_score", [P, 9 * P], F32, 140)
    S.dmask = at("sparse_mask", [P, 9 * P], BF16, 144.5)
    S.rh = at("rhs_hi", [P, KT * SEQ], F32R, 130)
    S.rl = at("rhs_lo", [P, KT * SEQ], F32R, 146)
    S.vt = at("v_tok", [P, QB * A_NVT * P], F32, 148)
    S.otok = at("o_tok", [P, QB * D], F32, 162)
    S.mh = at("merged_hi", [P, KT * SEQ], F32R, 162)
    S.cos = at("cos", [P, SEQ], F32, 178)
    S.sin = at("sin", [P, SEQ], F32, 180)
    S.con = at("constants", [P, C_N], F32, 182)
    S.ones = at("ones", [P, P], F32, 185.75)
    S.negones = at("neg_ones", [P, P], F32, 186.25)
    S.idb = at("ident_bf", [P, P], BF16, 186.75)
    S.causb = at("causal_bf", [P, P], BF16, 187)
    S.strictb = at("strict_bf", [P, P], BF16, 187.25)
    S.chunkb = at("chunk_bf", [P, P], BF16, 187.5)
    S.wk = [at(f"work{n}", [P, SEQ], F32, WK + 2 * n) for n in range(8)]
    S.sp = at("softplus_sum", [P, 10 * P], F32, WK + 6)
    S.stk_w = at("stick_weights", [P, 10 * P], F32, WK + 11)
    S.c = at("log_f_sum", [P, SEQ], F32, WK + 16)
    o = [(WK + 18) * 1024]

    def small(name, n, dt=F32):
        o[0] += 4 * n
        return nc.alloc_sbuf_tensor_at(name, [P, n], dt, offset=base + int(o[0] - 4 * n), align_bytes=4)

    S.prmA = small("params_a", DEPTH * PA_N)
    S.cur = small("params_cur", PA_N)
    S.nm = [small(f"neg_max{e}", 1) for e in range(4)]
    S.rs = [small(f"row_sum{e}", 1) for e in range(4)]
    S.rinv = [small(f"row_inv{e}", 1) for e in range(2)]
    S.top = [small(f"top8_{b}", 8) for b in range(3)]
    S.tick = small("tick", 32)
    S.eps = small("ln_eps", 1)
    S.res = at("residual", [P, KT * SEQ], F32, 80)
    S.q = at("b_q", [P, 4 * SEQ], F32, 96)
    S.kv = {n: at(f"b_{n}", [P, SEQ], F32, 104 + 2 * i) for i, n in enumerate(("kc", "ks", "kw", "vc", "vs", "vw", "gl"))}
    S.vbd = at("cmp_values", [P, 2 * 4 * HD], F32, 104)
    S.vtok = {"s": at("b_vs_tok", [P, SEQ], F32, 174.75), "w": at("b_vw_tok", [P, SEQ], F32, 112)}
    S.gate = at("b_gate_tok", [P, QB * 3 * B_HEADS], F32, 116)
    S.cmx, S.csum = (at(f"cmp_{n}", [P, QB * B_HEADS], F32, 116.5 + d) for n, d in (("max", 0), ("sum", 0.25)))
    S.mnh, S.mnl = at("nsa_hi", [P, 4 * SEQ], F32R, 96), at("nsa_lo", [P, 4 * SEQ], F32R, 104)
    S.zl, S.zc, S.zn = (at(f"silu_z_{n}", [P, 4 * SEQ], F32, 118 + 8 * i) for i, n in enumerate(("lru", "conv", "nsa")))
    S.uc = at("glu_out", [P, 4 * UC_W], F32, 142)
    S.ls = at("lru_tanh", [P, 4 * SEQ], F32, 142)
    S.ot2 = at("b_o_tok", [P, QB * 512], F32, 142)
    S.cacc = at("conv_sum", [P, 4 * SEQ], F32, 150.5)
    S.up = at("lru_in", [P, 4 * UP_W], F32, 158.5)
    S.la = at("lru_log_a", [P, 4 * SEQ], F32, 158.5)
    S.xc = at("lru_conv", [P, 4 * SEQ], F32, 166.75)
    S.hkh, S.hkl = (at(f"cmp_hid_k_{n}", [P, 2 * NB2], F32R, 176.75 + d) for n, d in (("hi", 0), ("lo", 0.5)))
    S.kcb = at("cmp_keys", [P, HD], F32, 177.75)
    S.blk = [at(f"cmp_blocks_{n}", [P, 16 * NB2], F32, WK + 4 * i) for i, n in enumerate("kv")]
    S.lri, S.lrt = at("lru_i", [P, 4 * SEQ], F32, WK), at("lru_tmp", [P, 4 * SEQ], F32, WK + 8)
    S.hvh, S.hvl = (at(f"cmp_hid_v_{n}", [P, SEQ], F32R, WK + 2 * i) for i, n in ((1, "hi"), (2, "lo")))
    S.pos = at("positions", [P, SEQ], I32, WK + 8)
    S.prmB = at("params_b", [P, SEQ], F32, WK + 16)
    S.cmask = small("cmp_mask", QB * 32)
    S.curB = small("params_b_cur", PB_N)
    S.lam = [small(f"lam{n}", 4) for n in range(5)]
    S.rg = [small(f"gate_inv{e}", 1) for e in range(2)]
    S.eps2, S.halfpi, S.tiny = small("rms_eps", 1), small("half_pi", 1), small("tiny", 1)

    S.ps = [nc.alloc_psum_tensor(f"bank{n}", [P, SEQ], F32) for n in range(8)]
    S.X = S.ps[4:]

    def sem(name):
        return ctx.enter_context(nc.semaphore(name))

    def ring(name):
        return [sem(f"{name}{s}") for s in range(SLOTS)]

    S.raw_landed, S.hi_ready, S.lo_ready = ring("raw_landed"), ring("hi_ready"), ring("lo_ready")
    S.unit_done, S.bank_free = ring("unit_done"), ring("bank_free")
    S.sem = sem
    S.con_landed = sem("con_landed")
    S.x_ready = sem("x_ready")
    S.scaled = sem("scaled")
    S.rot_ready = sem("rot_ready")
    S.rope_done = sem("rope_done")
    S.vt_ready = sem("vt_ready")
    S.vt_done = sem("vt_done")
    S.logf_in = sem("logf_in")
    S.logf_out = sem("logf_out")
    S.idx_ready = sem("idx_ready")
    S.relu_done = sem("relu_done")
    S.idx_acc = sem("idx_acc")
    S.mask_ready = sem("mask_ready")
    S.fox_staged = sem("fox_staged")
    S.fox_aug = sem("fox_aug")
    S.s_staged = sem("s_staged")
    S.d_staged = sem("d_staged")
    S.stk_z = sem("stk_z")
    S.stk_na = sem("stk_na")
    S.stk_ln = sem("stk_ln")
    S.stk_sp = sem("stk_sp")
    S.stk_c = sem("stk_c")
    S.stk_a = sem("stk_a")
    S.stk_o = sem("stk_o")
    S.stk_oev = sem("stk_oev")
    S.ot_ready = sem("ot_ready")
    S.ot_hi = sem("ot_hi")
    S.ot_done = sem("ot_done")
    S.merge_x = sem("merge_x")
    S.merge_done = sem("merge_done")
    S.t_ready = sem("t_ready")
    S.ln_mean = sem("ln_mean")
    S.ln_d = sem("ln_d")
    S.ln_sq = sem("ln_sq")
    S.ln_var = sem("ln_var")
    S.ln_std = sem("ln_std")
    S.ln_y = sem("ln_y")
    S.ln_hi = sem("ln_hi")
    S.ffn_act = sem("ffn_act")
    S.ffn_h = sem("ffn_h")
    S.p_landed = sem("p_landed")
    S.p_ready = sem("p_ready")
    S.y_ready = sem("y_ready")
    S.out_done = sem("out_done")
    S.pb_landed = sem("pb_landed")
    S.ang_ready = sem("ang_ready")
    S.tab_ready = sem("tab_ready")
    S.res_ready = sem("res_ready")
    S.rms_sq = sem("rms_sq")
    S.rms_var = sem("rms_var")
    S.rms_std = sem("rms_std")
    S.rms_y = sem("rms_y")
    S.rms_hi = sem("rms_hi")
    S.lam_in = sem("lam_in")
    S.lam_out = sem("lam_out")
    S.glu_done = sem("glu_done")
    S.bvt_ready = sem("bvt_ready")
    S.bvt_done = sem("bvt_done")
    S.gl_done = sem("gl_done")
    S.gate_tanh = sem("gate_tanh")
    S.q0_zero = sem("q0_zero")
    S.b_rot_ready = sem("b_rot_ready")
    S.b_rope_done = sem("b_rope_done")
    S.xc_split = sem("xc_split")
    S.lru_ready = sem("lru_ready")
    S.lru_gate = sem("lru_gate")
    S.nla_ready = sem("nla_ready")
    S.s_ready = sem("s_ready")
    S.a_ready = sem("a_ready")
    S.b2_ready = sem("b2_ready")
    S.beta_ready = sem("beta_ready")
    S.lru_done = sem("lru_done")
    S.blk_raw = sem("blk_raw")
    S.blk_ready = sem("blk_ready")
    S.hid_act = sem("hid_act")
    S.hid_split = sem("hid_split")
    S.kcb_ready = sem("kcb_ready")
    S.vbd_ready = sem("vbd_ready")
    S.cs_ready = sem("cs_ready")
    S.cexp_in = sem("cexp_in")
    S.cexp_out = sem("cexp_out")
    S.cp_ready = sem("cp_ready")
    S.cpt_ready = sem("cpt_ready")
    S.cpt_copied = sem("cpt_copied")
    S.oc_ready = sem("oc_ready")
    S.oc_done = sem("oc_done")
    S.dw_done = sem("dw_done")
    S.cl_mean = sem("cl_mean")
    S.cl_d = sem("cl_d")
    S.cl_sq = sem("cl_sq")
    S.cl_var = sem("cl_var")
    S.cl_std = sem("cl_std")
    S.cl_y = sem("cl_y")
    S.cl_hi = sem("cl_hi")
    S.un_ready = sem("un_ready")
    S.mc_y = sem("mc_y")
    S.mc_hi = sem("mc_hi")
    S.mc_ready = sem("mc_ready")
    S.q_staged = sem("q_staged")
    S.q_zero = sem("q_zero")
    S.bt_ready = sem("bt_ready")
    S.mn_y = sem("mn_y")
    S.mn_hi = sem("mn_hi")
    S.mn_ready = sem("mn_ready")
    S.y_done = sem("y_done")
    S.nsa = SoftmaxSems(sem, "nsa")
    S.fox = SoftmaxSems(sem, "fox")
    S.dsa = SoftmaxSems(sem, "dsa")
    return S


class SoftmaxSems:

    def __init__(self, sem, stage):
        self.s = sem(f"{stage}_scores")
        self.max = sem(f"{stage}_max")
        self.p = sem(f"{stage}_probs")
        self.pt = sem(f"{stage}_turned")
        self.ptc = sem(f"{stage}_turned_copied")
        self.o = sem(f"{stage}_out_ready")
        self.out = sem(f"{stage}_out_used")


class Step:

    def __init__(self, b, qk, v, norm, scale=None):
        self.b = b
        self.qk = qk
        self.v = v
        self.norm = norm
        self.scale = scale


def cols(t, j, n=SEQ, w=None):
    w = n if w is None else w
    return t[:, j * n:j * n + w] if isinstance(j, int) else t[:, bass.ds(j * n, w)]


def pe_unit(S, pe, u, g, out, rh, rl, ready=None, n0=0):
    s = u % SLOTS
    pe.wait_ge(S.lo_ready[s], g + 1)
    pe.wait_ge(S.bank_free[s], g + 1)
    for k in range(KT):
        if ready:
            pe.wait_ge(ready, n0 + k + 1)
        pe_tile(S, s, k, out, rh, rl, k, k == 0, k == KT - 1)
    return S.last


def pe_tile(S, s, w, out, rh, rl, k, first, last, lo=0, hi=P):
    nc = S.nc
    wh, wl = (t[s][lo:hi, w * P:(w + 1) * P] for t in (S.wh, S.wl))
    xh, xl = (t[lo:hi, k * SEQ:(k + 1) * SEQ] if isinstance(k, int) else t[lo:hi, bass.ds(k * SEQ, SEQ)] for t in (rh, rl))
    nc.tensor.matmul(out, wh, xh, start=first, stop=False)
    nc.tensor.matmul(out, wh, xl, start=False, stop=False)
    S.last = nc.tensor.matmul(out, wl, xh, start=False, stop=last)


def act_split(S, act, u, g):
    s = u % SLOTS
    act.wait_ge(S.raw_landed[s], 16 * (g + 2))
    S.nc.scalar.activation(S.wh[s][:, :], S.raw[s][:, :], ACT.Copy).then_inc(S.hi_ready[s], 1)


def sp_stream(S, sp, w_dram, groups):
    for s in range(SLOTS):
        sp.dma_start(S.raw[s][:, :], w_dram[s]).then_inc(S.raw_landed[s], 16)
    with sp.Fori(1, groups) as g:
        for s in range(SLOTS):
            sp.wait_ge(S.lo_ready[s], g)
            src = w_dram[bass.ds(g * SLOTS + s, 1), :, :].rearrange("a p n -> (a p) n")
            sp.dma_start(S.raw[s][:, :], src).then_inc(S.raw_landed[s], 16)


def pool_split(S, pool, groups):
    with pool.Fori(0, groups) as g:
        for s in range(SLOTS):
            pool.wait_ge(S.hi_ready[s], g + 1)
            S.nc.gpsimd.tensor_tensor(S.wl[s][:, :], S.raw[s][:, :], S.wh[s][:, :].bitcast(F32),
                                      ALU.subtract).then_inc(S.lo_ready[s], 1)


def attn_pe(S, pe, Z, n0, steps, ident, fill=None):
    nc = S.nc
    N = len(steps)

    def scores(n):
        if n >= 2:
            pe.wait_ge(Z.p, n0 + n - 1)
        for i, (lhsT, rhs, c, w) in enumerate(steps[n].qk):
            m = nc.tensor.matmul(S.X[n % 2][:, c:c + w], lhsT, rhs, start=(i == 0), stop=(i == len(steps[n].qk) - 1),
                                 skip_group_check=True)
        m.then_inc(Z.s, 1)

    def turn(n):
        pe.wait_ge(Z.p, n0 + n + 1)
        if n >= 1:
            pe.wait_ge(Z.ptc, n0 + n)
        for k in range(steps[n].b + 1):
            m = nc.tensor.transpose(S.X[2][:, k * P:(k + 1) * P], S.wk[4 + n % 2][:, k * P:(k + 1) * P], ident)
        m.then_inc(Z.pt, 1)

    scores(0)
    scores(1)
    turn(0)
    for n in range(N):
        if n + 2 < N:
            scores(n + 2)
        if fill:
            fill(n, 0)
        if n + 1 < N:
            turn(n + 1)
        if fill:
            fill(n, 1)
        pe.wait_ge(Z.ptc, n0 + n + 1)
        pe.wait_ge(Z.out, n0 + n + 2)
        b = steps[n].b
        for k in range(b + 1):
            m = nc.tensor.matmul(S.X[3][:, 0:HD], S.wk[6 + n % 2][:, k * P:(k + 1) * P], steps[n].v(k),
                                 start=(k == 0), stop=(k == b))
        m.then_inc(Z.o, 1)


def attn_copy_turned(S, Z, eng, op, n0, n, steps):
    eng.wait_ge(Z.pt, n0 + n + 1)
    if n >= 2:
        eng.wait_ge(Z.o, n0 + n - 1)
    w = (steps[n].b + 1) * P
    op(S.wk[6 + n % 2][:, 0:w], S.X[2][:, 0:w]).then_inc(Z.ptc, 1)


def attn_act(S, act, Z, n0, steps, after=None):
    nc = S.nc
    N = len(steps)

    def exps(n):
        act.wait_ge(Z.max, n0 + n + 1)
        if n >= 2:
            act.wait_ge(Z.pt, n0 + n - 1)
            act.wait_ge(Z.out, n0 + n - 1)
        w = (steps[n].b + 1) * P
        nc.scalar.activation(S.wk[4 + n % 2][:, 0:w], S.X[n % 2][:, 0:w], ACT.Exp, bias=S.nm[n % 4][:, :],
                             accum_out=S.rs[n % 4][:, :]).then_inc(Z.p, 1)

    exps(0)
    exps(1)
    for n in range(N):
        if n % 2:
            attn_copy_turned(S, Z, act, lambda o, i: nc.scalar.activation(o, i, ACT.Copy), n0, n, steps)
        if n + 2 < N:
            exps(n + 2)
        if after:
            after(n)


def attn_dve(S, dve, Z, n0, steps, after=None):
    nc = S.nc
    N = len(steps)

    def rowmax(n):
        dve.wait_ge(Z.s, n0 + n + 1)
        w = (steps[n].b + 1) * P
        nc.vector.tensor_reduce(S.nm[n % 4][:, :], S.X[n % 2][:, 0:w], AX, ALU.max, negate=True).then_inc(Z.max, 1)

    rowmax(0)
    rowmax(1)
    for n in range(N):
        if n % 2 == 0:
            attn_copy_turned(S, Z, dve, nc.vector.tensor_copy, n0, n, steps)
        if n + 2 < N:
            rowmax(n + 2)
        nc.vector.reciprocal(S.rinv[n % 2][:, :], S.rs[n % 4][:, :])
        dve.drain()
        if steps[n].scale:
            steps[n].scale(n)
            dve.drain()
        dve.wait_ge(Z.o, n0 + n + 1)
        steps[n].norm(n)
        if after:
            after(n)


def fox_steps(S, i):
    steps = []
    for e in range(2):
        for b in range(QB):
            w = (b + 1) * P
            qk = [(S.wk[e][:, b * P:w], S.wk[2 + e][:, 0:w], 0, w), (S.idb[:, :], S.causb[:, :], b * P, P)]

            def v(k, e=e):
                return cols2(S.vt, k * A_NVT * P + V_FOX + e * HD, i, 2 * HD, HD)

            def norm(n, b=b, e=e):
                S.nc.vector.tensor_scalar(cols2(S.otok, b * D + e * HD, i, 2 * HD, HD), S.X[3][:, 0:HD],
                                          S.rinv[n % 2][:, :], None, ALU.mult).then_inc(S.fox.out, 1)
            steps.append(Step(b, qk, v, norm))
    return steps


def cols2(t, c0, i, stride, w):
    return t[:, c0 + i * stride:c0 + i * stride + w] if isinstance(i, int) else t[:, bass.ds(i * stride + c0, w)]


def dsa_steps(S, heads):
    steps = []
    for h0, i, q, k in heads:
        for b in range(QB):
            w = (b + 1) * P
            qk = [(q[:, b * P:w], k[:, 0:w], 0, w)]
            if b == 0:
                qk.append((S.idb[:, :], S.chunkb[:, :], 0, P))
            else:
                m0 = (b * (b + 1) // 2 - 1) * P
                qk.append((S.idb[:, :], S.dmask[:, m0:m0 + w], 0, w))

            def v(kt):
                return S.vt[:, kt * A_NVT * P + V_DSA:kt * A_NVT * P + V_DSA + HD]

            def norm(n, b=b, h0=h0, i=i):
                S.nc.vector.tensor_scalar(cols2(S.otok, b * D + (11 + h0) * HD, i, 2 * HD, HD), S.X[3][:, 0:HD],
                                          S.rinv[n % 2][:, :], None, ALU.mult).then_inc(S.dsa.out, 1)
            steps.append(Step(b, qk, v, norm))
    return steps


def tile_rows(S, u, half):
    return S.qkv[64 * half:64 * half + 64, u * SEQ:(u + 1) * SEQ]


def dsa_pair(S, i):
    return dsa_steps(S, [(0, i, S.wk[0], seq(S.qkv, A_DKIK)), (1, i, S.wk[1], seq(S.qkv, A_S4KDK))])


def dsa_last(S):
    return dsa_steps(S, [(4, 0, tile_rows(S, A_S4D4Q, 1), tile_rows(S, A_S4KDK, 1))])


SB0 = [0, 4 * P, 7 * P, 9 * P]


def stk_pe(S, pe, n0, q, k, v, fill=None):
    nc = S.nc

    def z(n):
        i = QB - 1 - n
        if n >= 2:
            pe.wait_ge(S.stk_a, n0 + n - 1)
        nc.tensor.matmul(S.X[n % 2][:, 0:SEQ - i * P], k[:, i * P:(i + 1) * P], q[:, i * P:SEQ], start=True, stop=True,
                         skip_group_check=True).then_inc(S.stk_z, 1)

    z(0)
    for n, i in enumerate(reversed(range(QB))):
        w = SEQ - i * P
        bank = S.X[n % 2]
        if n + 1 < QB:
            z(n + 1)
        if fill:
            fill(n)
        pe.wait_ge(S.stk_sp, n0 + n + 1)
        nc.tensor.matmul(bank[:, 0:w], S.con[:, C_TRI:C_TRI + P], S.sp[:, SB0[i]:SB0[i] + w], start=False, stop=False,
                         skip_group_check=True)
        for j in range(i + 1, QB):
            wj = SEQ - j * P
            nc.tensor.matmul(bank[:, w - wj:w], S.negones[:, :], S.sp[:, SB0[j]:SB0[j] + wj], start=False, stop=False,
                             skip_group_check=True)
        nc.tensor.matmul(bank[:, 0:P], S.idb[:, :], S.strictb[:, :], start=False, stop=True,
                         skip_group_check=True).then_inc(S.stk_c, 1)
    pe.wait_ge(S.stk_a, n0 + QB)
    for b in range(QB):
        for kt in range(b + 1):
            c = SB0[kt] + (b - kt) * P
            m = nc.tensor.matmul(S.X[2][:, b * HD:(b + 1) * HD], S.stk_w[:, c:c + P], v(kt),
                                 start=(kt == 0), stop=(kt == b), skip_group_check=True)
    m.then_inc(S.stk_o, 1)


def stk_act(S, act, n0, after=None):
    nc = S.nc
    for n, i in enumerate(reversed(range(QB))):
        w = SEQ - i * P
        t = S.nz0[:, 0:w]
        act.wait_ge(S.stk_na, n0 + n + 1)
        nc.scalar.activation(t, t, ACT.Exp)
        act.drain()
        nc.scalar.activation(t, t, ACT.Ln, bias=1.0).then_inc(S.stk_ln, 1)
        act.wait_ge(S.stk_c, n0 + n + 1)
        nc.scalar.activation(S.stk_w[:, SB0[i]:SB0[i] + w], S.X[n % 2][:, 0:w], ACT.Exp).then_inc(S.stk_a, 1)
        if after:
            after(n)


def stk_dve(S, dve, n0, h0, out, between=None):
    nc = S.nc
    for n, i in enumerate(reversed(range(QB))):
        w = SEQ - i * P
        t, sp = S.nz0[:, 0:w], S.sp[:, SB0[i]:SB0[i] + w]
        dve.wait_ge(S.stk_z, n0 + n + 1)
        z = S.X[n % 2][:, 0:w]
        nc.vector.tensor_scalar(sp, z, 0.0, None, ALU.max)
        dve.drain()
        nc.vector.scalar_tensor_tensor(out=t, in0=sp, scalar=-2.0, in1=z, op0=ALU.mult, op1=ALU.add).then_inc(S.stk_na, 1)
        if between:
            between()
        dve.wait_ge(S.stk_ln, n0 + n + 1)
        nc.vector.tensor_tensor(sp, sp, t, ALU.add)
        dve.drain()
        nc.vector.tensor_tensor(sp[:, 0:P], sp[:, 0:P], S.con[:, C_ST01:C_ST01 + P], ALU.mult).then_inc(S.stk_sp, 1)
    dve.wait_ge(S.stk_o, h0 + 1)
    nc.vector.tensor_copy(out, S.X[2][:, 0:QB * HD].rearrange("p (b d) -> p b d", b=QB)).then_inc(S.stk_oev, 1)


def otok_head(S, h0, i):
    v = S.otok[:, :].rearrange("p (b d) -> p b d", b=QB)
    c = h0 * HD
    return v[:, :, c:c + HD] if isinstance(i, int) else v[:, :, bass.ds(i * 2 * HD + c, HD)]


def stk_v(S, col, i):
    return lambda kt: cols2(S.vt, kt * A_NVT * P + col, i, 2 * HD, HD)


def ln_mean_pe(S, pe, n0, t_sem, t0, t, i, unit):
    def mean(j):
        pe.wait_ge(t_sem, t0 + j + 1)
        return S.nc.tensor.matmul(S.X[0][:, :], S.ones[:, :], seq(t, j), start=(j == 0), stop=(j == KT - 1))

    for j in range(SLOTS):
        unit(j)
        if 4 * i + j >= 1:
            mean(4 * i + j - 1)
    if i == 1:
        mean(KT - 1).then_inc(S.ln_mean, 1)


def ln_pe(S, pe, n0):
    for j in range(KT):
        pe.wait_ge(S.ln_sq, n0 * KT + j + 1)
        S.nc.tensor.matmul(S.X[1][:, :], S.ones[:, :], S.wk[j % 2][:, :], start=(j == 0),
                           stop=(j == KT - 1)).then_inc(S.ln_var, 1)


def ln_act(S, act, n0, t, g, b, between=None):
    nc = S.nc
    for j in range(KT):
        act.wait_ge(S.ln_d, n0 * KT + j + 1)
        if j >= 2:
            act.wait_ge(S.ln_var, n0 * KT + j - 1)
        nc.scalar.activation(S.wk[j % 2][:, :], t[:, j * SEQ:(j + 1) * SEQ], ACT.Square).then_inc(S.ln_sq, 1)
    act.wait_ge(S.ln_var, n0 * KT + KT)
    nc.scalar.activation(S.wk[2][:, :], S.X[1][:, :], ACT.Sqrt, bias=S.eps[:, :]).then_inc(S.ln_std, 1)
    for j in range(KT):
        act.wait_ge(S.ln_y, n0 * KT + j + 1)
        for o in (seq(S.xh, j), S.wk[4 + j % 4][:, :]):
            m = nc.scalar.activation(o, seq(t, j), ACT.Identity, scale=S.cur[:, g + j:g + j + 1], bias=S.cur[:, b + j:b + j + 1])
        m.then_inc(S.ln_hi, 1)
        if between and j == 1:
            between()


def ln_dve(S, dve, n0, t):
    nc = S.nc
    tiles = [t[:, j * SEQ:(j + 1) * SEQ] for j in range(KT)]
    dve.wait_ge(S.ln_mean, n0 + 1)
    for j in range(KT):
        nc.vector.tensor_tensor(tiles[j], tiles[j], S.X[0][:, :], ALU.subtract).then_inc(S.ln_d, 1)
    dve.wait_ge(S.ln_std, n0 + 1)
    nc.vector.reciprocal(S.wk[3][:, :], S.wk[2][:, :])
    dve.drain()
    for j in range(KT + 2):
        if j < KT:
            nc.vector.tensor_tensor(tiles[j], tiles[j], S.wk[3][:, :], ALU.mult).then_inc(S.ln_y, 1)
        if j >= 2:
            q = j - 2
            dve.wait_ge(S.ln_hi, n0 * KT + q + 1)
            nc.vector.tensor_tensor(seq(S.xl, q), S.wk[4 + q % 4][:, :], seq(S.xh, q).bitcast(F32),
                                    ALU.subtract).then_inc(S.x_ready, 1)


ROPE = [(A_IKF, 0, 64), (A_S4D4Q, 64, 128), (A_S4KDK, 64, 128)] + [(u, 0, P) for u in range(A_DKIK, A_NPROJ)]


def idx_steps():
    return [(b, h) for b in range(1, QB) for h in range(IDX_HEADS)]


def GA(L, u, i=0):
    return L * A_GROUPS + u // SLOTS + i


def gate_fill(S, pe, L, i, first, tiles):
    for x in tiles:
        j, k = divmod(x, KT)
        u = A_GATE + first + j
        s = u % SLOTS
        if k == 0:
            pe.wait_ge(S.lo_ready[s], GA(L, u, i) + 1)
            pe.wait_ge(S.bank_free[s], GA(L, u, i) + 1)
        pe_tile(S, s, k, S.ps[s][:, :], S.xh, S.xl, k, k == 0, k == KT - 1)
        if k == KT - 1:
            S.last.then_inc(S.unit_done[s], 1)


SC0 = [None, 0, 2 * P, 5 * P]


def a_tensor(S, pe):
    nc = S.nc
    ident = S.con[:, C_ID:C_ID + P]
    with pe.Fori(0, DEPTH) as L:
        G = lambda u, i=0: L * A_GROUPS + u // SLOTS + i
        with pe.Fori(0, 6) as i:
            for u in range(SLOTS):
                pe_unit(S, pe, u, G(u, i), S.ps[u][:, :], S.xh, S.xl,
                        None if u else S.x_ready, L * 2 * KT).then_inc(S.unit_done[u], 1)
        for u in (24, 25):
            pe_unit(S, pe, u, G(u), S.ps[u % SLOTS][:, :], S.xh, S.xl).then_inc(S.unit_done[u % SLOTS], 1)
        pe.wait_ge(S.bank_free[25 % SLOTS], G(25) + 2)
        for v in range(A_NVT):
            if v >= 2:
                pe.wait_ge(S.vt_done, L * A_NVT + v - 1)
            for t in range(QB):
                m = nc.tensor.transpose(S.X[2 + v % 2][:, t * P:(t + 1) * P],
                                        S.qkv[:, A_VT[v] * SEQ + t * P:A_VT[v] * SEQ + (t + 1) * P], ident)
            m.then_inc(S.vt_ready, 1)
        pe.wait_ge(S.scaled, L + 1)
        for n, (u, _, _) in enumerate(ROPE):
            if n >= 2:
                pe.wait_ge(S.rope_done, L * len(ROPE) + n - 1)
            nc.tensor.matmul(S.X[n % 2][:, :], S.con[:, C_ROT:C_ROT + P], S.qkv[:, u * SEQ:(u + 1) * SEQ],
                             start=True, stop=True).then_inc(S.rot_ready, 1)
            gate_fill(S, pe, L, 0, ROPE_UNITS, range(32 * n // len(ROPE), 32 * (n + 1) // len(ROPE)))
        pe.wait_ge(S.vt_done, (L + 1) * A_NVT)
        pe.wait_ge(S.rope_done, (L + 1) * len(ROPE))
        for n, (b, h) in enumerate(idx_steps()):
            if n >= 4:
                pe.wait_ge(S.relu_done, L * 24 + n - 3)
            k = tile_rows(S, A_IKF, 0) if h % 2 == 0 else tile_rows(S, A_DKIK, 1)
            q = tile_rows(S, A_IQ + h // 2, h % 2)
            w = (b + 1) * P
            nc.tensor.matmul(S.X[n % 4][:, 0:w], q[:, b * P:w], k[:, 0:w], start=True,
                             stop=True).then_inc(S.idx_ready, 1)
        with pe.Fori(0, 3) as i:
            pe.wait_ge(S.relu_done, (L + 1) * 24)
            pe.wait_ge(S.fox_staged, (L * 3 + i) * 4 + 4)
            pe.wait_ge(S.fox_aug, (L * 3 + i) * 2 + 2)
            attn_pe(S, pe, S.fox, (L * 3 + i) * 8, fox_steps(S, i), ident,
                    lambda n, half: gate_fill(S, pe, L, i, FOX_UNITS, range(4 * n + 2 * half, 4 * n + 2 * half + 2)))
        with pe.Fori(0, 2) as i:
            pe.wait_ge(S.fox.out, (L + 1) * 24 + 2)
            pe.wait_ge(S.q0_zero, L + 1)
            pe.wait_ge(S.s_staged, (L * 2 + i) * 3 + 3)
            for e in range(2):
                h0 = L * 5 + i * 2 + e
                pe.wait_ge(S.stk_oev, h0 + 1)
                stk_pe(S, pe, h0 * QB, S.wk[e], S.wk[2], stk_v(S, V_SB + e * HD, i),
                       lambda n, e=e: gate_fill(S, pe, L, i, STK_UNITS, range(16 * e + 4 * n, 16 * e + 4 * n + 4)))
        pe.wait_ge(S.stk_oev, L * 5 + 5)
        stk_pe(S, pe, (L * 5 + 4) * QB, tile_rows(S, A_S4D4Q, 0), tile_rows(S, A_S4KDK, 0), stk_v(S, V_S4, 0))
        with pe.Fori(0, 2) as i:
            pe.wait_ge(S.stk_oev, L * 5 + 6)
            pe.wait_ge(S.mask_ready, L + 1)
            pe.wait_ge(S.d_staged, (L * 2 + i) * 2 + 2)
            attn_pe(S, pe, S.dsa, L * 20 + i * 8, dsa_pair(S, i), ident)
        attn_pe(S, pe, S.dsa, L * 20 + 16, dsa_last(S), ident)
        pe.wait_ge(S.dsa.out, (L + 1) * 20 + 2)
        for k in range(KT):
            if k >= 4:
                pe.wait_ge(S.ot_done, L * KT + k - 3)
            for b in range(QB):
                m = nc.tensor.transpose(S.X[k % 4][:, b * P:(b + 1) * P],
                                        S.otok[:, b * D + k * P:b * D + (k + 1) * P], ident)
            m.then_inc(S.ot_ready, 1)
        with pe.Fori(0, 2) as i:
            pe.wait_ge(S.ot_done, (L + 1) * KT)
            for jj in range(4):
                u = A_UP + jj
                s = u % SLOTS
                pe.wait_ge(S.lo_ready[s], G(u, i) + 1)
                pe.wait_ge(S.bank_free[s], G(u, i) + 1)
                pe.wait_ge(S.merge_x, L * KT + i * 4 + jj + 1)
                XS, XD = S.X[2 * (jj % 2)][:, :], S.X[2 * (jj % 2) + 1][:, :]
                for k in range(3):
                    pe_tile(S, s, k, S.ps[s][:, :], S.rh, S.rl, k, k == 0, k == 2)
                pe_tile(S, s, 3, XS, S.rh, S.rl, 3, True, False)
                pe_tile(S, s, 4, XS, S.rh, S.rl, 4, False, False)
                pe_tile(S, s, 5, XS, S.rh, S.rl, 5, False, True, 0, 64)
                pe_tile(S, s, 6, XD, S.rh, S.rl, 6, True, False)
                pe_tile(S, s, 5, XD, S.rh, S.rl, 5, False, False, 64, 128)
                pe_tile(S, s, 7, XD, S.rh, S.rl, 7, False, True)
                S.last.then_inc(S.unit_done[s], 1)
        for i in range(2):
            ln_mean_pe(S, pe, L * 2, S.t_ready, L * KT, S.t, i,
                       lambda j: pe_unit(S, pe, A_OUT + j, G(A_OUT + j, i), S.ps[(A_OUT + j) % SLOTS][:, :], S.mh, S.ml,
                                         None if i + j else S.merge_done, L * KT).then_inc(S.unit_done[(A_OUT + j) % SLOTS], 1))
        ln_pe(S, pe, L * 2)
        pe.wait_ge(S.p_ready, L + 1)
        for u in (A_OUT + 6, A_OUT + 7):
            pe.wait_ge(S.bank_free[u % SLOTS], G(u) + 2)
        pe.wait_ge(S.bank_free[(A_PLE + 1) % SLOTS], G(A_PLE + 1) + 1)
        for u in (A_PLE, A_PLE + 1):
            s = u % SLOTS
            pe.wait_ge(S.lo_ready[s], G(u) + 1)
            if u == A_PLE:
                pe.wait_ge(S.bank_free[s], G(u) + 1)
            else:
                pe.wait_ge(S.bank_free[(u - 1) % SLOTS], G(u - 1) + 2)
            for o in range(4):
                for k in range(2):
                    pe_tile(S, s, 2 * o + k, S.ps[o][:, :], S.ph, S.pl, k, k == 0, k == 1)
            S.last.then_inc(S.unit_done[s], 1)
        with pe.Fori(0, 4) as q:
            with pe.Fori(0, 2) as i:
                pe.wait_ge(S.bank_free[(A_PLE + 1) % SLOTS], G(A_PLE + 1) + 2)
                for u in range(A_FFN, A_FFN + SLOTS):
                    pe_unit(S, pe, u, G(u, q * 4 + i), S.ps[u % SLOTS][:, :], S.xh, S.xl,
                            None if u > A_FFN else S.x_ready, L * 2 * KT + KT).then_inc(S.unit_done[u % SLOTS], 1)
            with pe.Fori(0, 2) as i:
                for u in range(A_FFN, A_FFN + SLOTS):
                    pe_unit(S, pe, u, G(u, q * 4 + i + 2), S.ps[u % SLOTS][:, :], S.rh, S.rl,
                            None if u > A_FFN else S.ffn_h, (L * 4 + q) * KT + 2).then_inc(S.unit_done[u % SLOTS], 1)
        for i in range(2):
            ln_mean_pe(S, pe, L * 2 + 1, S.y_ready, L * KT + 2, S.yacc, i,
                       lambda j: pe_unit(S, pe, A_PG + j, G(A_PG + j, i), S.ps[(A_PG + j) % SLOTS][:, :], S.xh,
                                         S.xl).then_inc(S.unit_done[(A_PG + j) % SLOTS], 1))
        ln_pe(S, pe, L * 2 + 1)


def a_scalar(S, act, p_dram):
    nc = S.nc

    def take(u, g, out, func, **kw):
        s = u % SLOTS
        act.wait_ge(S.unit_done[s], g + 1)
        nc.scalar.activation(out, S.ps[s][:, :], func, **kw).then_inc(S.bank_free[s], 1)
        act_split(S, act, u, g)

    for s in range(SLOTS):
        act.wait_ge(S.raw_landed[s], 16)
        nc.scalar.activation(S.wh[s][:, :], S.raw[s][:, :], ACT.Copy).then_inc(S.hi_ready[s], 1)
    with act.Fori(0, DEPTH) as L:
        G = lambda u, i=0: L * A_GROUPS + u // SLOTS + i
        with act.Fori(0, 6) as i:
            for u in range(SLOTS):
                take(u, G(u, i), cols(S.qkv, i * SLOTS + u), ACT.Copy)
        for u in (24, 25):
            take(u, G(u), cols(S.qkv, u), ACT.Copy)
        vt = S.vt[:, :].rearrange("p (t c) -> p t c", t=QB)
        for v in range(A_NVT):
            act.wait_ge(S.vt_ready, L * A_NVT + v + 1)
            nc.scalar.activation(vt[:, :, v * P:(v + 1) * P], S.X[2 + v % 2][:, :].rearrange("p (t c) -> p t c", t=QB),
                                 ACT.Copy).then_inc(S.vt_done, 1)
        nc.scalar.preload_act_table_set("natural_log_exp_and_others")
        act.wait_ge(S.logf_in, L + 1)
        lf = S.wk[5][64:128, :]
        nc.scalar.activation(lf, lf, ACT.Exp)
        act.drain()
        nc.scalar.activation(lf, lf, ACT.Ln, bias=1.0).then_inc(S.logf_out, 1)
        def gate_take(i, first, j):
            u = A_GATE + first + j
            take(u, G(u, i), cols(S.gates, i * SLOTS + first + j), ACT.Copy)

        for j in range(SLOTS):
            gate_take(0, ROPE_UNITS, j)
        for n, (b, h) in enumerate(idx_steps()):
            act.wait_ge(S.idx_ready, L * 24 + n + 1)
            if n >= 2:
                act.wait_ge(S.idx_acc, L * 24 + n - 1)
            w = (b + 1) * P
            nc.scalar.activation(S.r[n % 2][:, 0:w], S.X[n % 4][:, 0:w], ACT.Relu).then_inc(S.relu_done, 1)
        with act.Fori(0, 3) as i:
            for e in range(2):
                src = S.qkv[64 * e:64 * e + 64, :]
                for t, u in ((e, A_FQ), (2 + e, A_FK)):
                    nc.scalar.activation(S.wk[t][0:64, :], cols2(src, u * SEQ, i, SEQ, SEQ), ACT.Copy).then_inc(S.fox_staged, 1)
            attn_act(S, act, S.fox, (L * 3 + i) * 8, fox_steps(S, i),
                     lambda n: n and n % 2 == 0 and gate_take(i, FOX_UNITS, n // 2 - 1))
            gate_take(i, FOX_UNITS, 3)
        nc.scalar.preload_act_table_set("natural_log_exp_and_others")
        act.wait_ge(S.fox.out, (L + 1) * 24 + 2)
        with act.Fori(0, 2) as i:
            act.wait_ge(S.stk_oev, L * 5 + i * 2 + 1)
            nc.scalar.activation(S.wk[2][:, :], cols(S.qkv, i + A_SK), ACT.Copy).then_inc(S.s_staged, 1)
            for e in range(2):
                r = slice(64 * e, 64 * e + 64)
                nc.scalar.activation(S.wk[e][r, :], cols2(S.qkv[r, :], A_SQ * SEQ, i, SEQ, SEQ), ACT.Copy).then_inc(S.s_staged, 1)
            for e in range(2):
                stk_act(S, act, (L * 5 + i * 2 + e) * QB,
                        lambda n, e=e: 4 * e + n and n % 2 == 0 and gate_take(i, STK_UNITS, 2 * e + n // 2 - 1))
            gate_take(i, STK_UNITS, 3)
        stk_act(S, act, (L * 5 + 4) * QB)
        with act.Fori(0, 2) as i:
            act.wait_ge(S.stk_oev, L * 5 + 6)
            for e in range(2):
                r = slice(64 * e, 64 * e + 64)
                nc.scalar.activation(S.wk[e][r, :], cols2(S.qkv[r, :], A_DQ * SEQ, i, SEQ, SEQ), ACT.Copy).then_inc(S.d_staged, 1)
            attn_act(S, act, S.dsa, L * 20 + i * 8, dsa_pair(S, i))
        attn_act(S, act, S.dsa, L * 20 + 16, dsa_last(S))
        for k in range(KT):
            act.wait_ge(S.ot_ready, L * KT + k + 1)
            nc.scalar.activation(S.rh[:, k * SEQ:(k + 1) * SEQ], S.X[k % 4][:, :], ACT.Copy).then_inc(S.ot_hi, 1)
        with act.Fori(0, 2) as i:
            for jj in range(4):
                for d in range(3):
                    t = cols(S.gates, i * SLOTS + d * KT + jj)
                    m = nc.scalar.activation(t, t, ACT.Tanh, scale=0.5)
                m.then_inc(S.gate_tanh, 1)
                u = A_UP + jj
                act.wait_ge(S.unit_done[u % SLOTS], G(u, i) + 1)
                act_split(S, act, u, G(u, i))
        act.wait_ge(S.merge_done, (L + 1) * KT)
        act.dma_start(S.praw[:, :], p_dram[bass.ds(L, 1), :, :].rearrange("a p n -> (a p) n")).then_inc(S.p_landed, 16)
        with act.Fori(0, 2) as i:
            for u in range(A_OUT, A_OUT + SLOTS):
                act.wait_ge(S.unit_done[u % SLOTS], G(u, i) + 1)
                act_split(S, act, u, G(u, i))
        def ple_take(d):
            u = A_PLE + d
            s = u % SLOTS
            act.wait_ge(S.unit_done[s], G(u) + 1)
            for o in range(4):
                m = nc.scalar.activation(cols(S.plep, 4 * d + o), S.ps[o][:, :], ACT.Copy)
            m.then_inc(S.bank_free[s], 1)
            act_split(S, act, u, G(u))

        ln_act(S, act, L * 2, S.t, PA_G1, PA_B1, lambda: ple_take(0))
        ple_take(1)
        with act.Fori(0, 4) as q:
            with act.Fori(0, 2) as i:
                for j in range(SLOTS):
                    u = A_FFN + j
                    s, g = u % SLOTS, G(u, q * 4 + i)
                    act.wait_ge(S.unit_done[s], g + 1)
                    act.wait_ge(S.ffn_h, (L * 4 + q) * KT + i * SLOTS + j + 1)
                    nc.scalar.activation(S.wk[j % 2][:, :], S.ps[s][:, :], ACT.Relu).then_inc(S.bank_free[s], 1)
                    act.drain()
                    nc.scalar.activation(cols(S.rh, i * SLOTS + j), S.wk[j % 2][:, :], ACT.Square).then_inc(S.ffn_act, 1)
                    act_split(S, act, u, g)
            with act.Fori(0, 2) as i:
                for u in range(A_FFN, A_FFN + SLOTS):
                    g = G(u, q * 4 + i + 2)
                    act.wait_ge(S.unit_done[u % SLOTS], g + 1)
                    act_split(S, act, u, g)
        with act.Fori(0, 2) as i:
            for j in range(SLOTS):
                u = A_PG + j
                s, g = u % SLOTS, G(u, i)
                act.wait_ge(S.unit_done[s], g + 1)
                act.wait_ge(S.y_ready, L * KT + i * SLOTS + j + 1)
                nc.scalar.activation(S.wk[4 + j % 2][:, :], S.ps[s][:, :], ACT.Tanh, scale=0.5).then_inc(S.bank_free[s], 1)
                act_split(S, act, u, g)
        ln_act(S, act, L * 2 + 1, S.yacc, PA_G2, PA_B2)


def top_round(S, dve):
    nc = S.nc
    for b in range(1, QB):
        nc.vector.max(S.top[b - 1][:, :], S.score[:, SC0[b]:SC0[b] + (b + 1) * P])
    dve.drain()
    for b in range(1, QB):
        sc = S.score[:, SC0[b]:SC0[b] + (b + 1) * P]
        nc.vector.match_replace(sc, S.top[b - 1][:, :], sc, MARK)
    dve.drain()


assert 4 * QB == TOPK // 8


def a_vector(S, dve):
    nc = S.nc
    with dve.Fori(0, DEPTH) as L:
        G = lambda u, i=0: L * A_GROUPS + u // SLOTS + i
        nc.vector.tensor_copy(S.cur[:, :], cols(S.prmA, L, PA_N))
        dve.drain()
        dve.wait_ge(S.bank_free[25 % SLOTS], G(25) + 2)
        for u, n in ((A_FQ, 3), (A_SQ, 2), (A_S4D4Q, 1), (A_DQ, 2)):
            t = S.qkv[:, u * SEQ:(u + n) * SEQ]
            m = nc.vector.tensor_scalar(t, t, HD ** -0.5, None, ALU.mult)
        m.then_inc(S.scaled, 1)
        f, na = S.c[64:128, :], S.wk[5][64:128, :]
        nc.vector.tensor_scalar(f, S.qkv[64:128, A_IKF * SEQ:(A_IKF + 1) * SEQ], S.cur[64:128, PA_BF:PA_BF + 1], None, ALU.add)
        dve.drain()
        nc.vector.scalar_tensor_tensor(out=na, in0=f, scalar=-1.0, in1=f, op0=ALU.mult, op1=ALU.min).then_inc(S.logf_in, 1)
        for n, (u, lo, hi) in enumerate(ROPE):
            t = S.qkv[lo:hi, u * SEQ:(u + 1) * SEQ]
            a, b = S.wk[n % 2][lo:hi, :], S.wk[2 + n % 2][lo:hi, :]
            nc.vector.tensor_tensor(a, t, S.cos[lo:hi, :], ALU.mult)
            dve.wait_ge(S.rot_ready, L * len(ROPE) + n + 1)
            nc.vector.tensor_tensor(b, S.X[n % 2][lo:hi, :], S.sin[lo:hi, :], ALU.mult)
            dve.drain()
            nc.vector.tensor_tensor(t, a, b, ALU.add).then_inc(S.rope_done, 1)
        nc.vector.memset(S.wk[4][64:128, :], 1.0)
        dve.wait_ge(S.logf_out, L + 1)
        nc.vector.scalar_tensor_tensor(out=f, in0=f, scalar=0.0, in1=na, op0=ALU.min, op1=ALU.subtract)
        dve.drain()
        nc.vector.tensor_tensor_scan(na, S.wk[4][64:128, :], f, 0.0, ALU.mult, ALU.add)
        dve.drain()
        nc.vector.tensor_copy(f, na)
        for e in range(2):
            nc.vector.tensor_scalar(S.wk[2 + e][64:128, :], na, S.con[64:128, C_KA:C_KA + 1], S.con[64:128, C_KB:C_KB + 1],
                                    ALU.mult, ALU.add)
        dve.wait_ge(S.vt_done, (L + 1) * A_NVT)
        for n, (b, h) in enumerate(idx_steps()):
            dve.wait_ge(S.relu_done, L * 24 + n + 1)
            w = (b + 1) * P
            acc = S.sacc[:, SC0[b]:SC0[b] + w]
            iw = S.vt[:, b * A_NVT * P + V_IW + h:b * A_NVT * P + V_IW + h + 1]
            if h == 0:
                nc.vector.tensor_scalar(acc, S.r[n % 2][:, 0:w], iw, None, ALU.mult).then_inc(S.idx_acc, 1)
            else:
                nc.vector.scalar_tensor_tensor(out=acc, in0=S.r[n % 2][:, 0:w], scalar=iw, in1=acc, op0=ALU.mult,
                                               op1=ALU.add).then_inc(S.idx_acc, 1)
            dve.drain()
        for b in range(1, QB):
            nc.vector.memset(S.sacc[0:64, SC0[b] + b * P + 64:SC0[b] + (b + 1) * P], NEG)
        dve.drain()
        nc.vector.tensor_copy(S.score[:, :], S.sacc[:, :])
        with dve.Fori(0, 3) as i:
            for e in range(2):
                qa = S.con[64:128, bass.ds(i * 2 + C_QA + e, 1)]
                qb = S.con[64:128, bass.ds(i * 2 + C_QB + e, 1)]
                nc.vector.tensor_scalar(S.wk[e][64:128, :], f, qa, qb, ALU.mult, ALU.add).then_inc(S.fox_aug, 1)
            attn_dve(S, dve, S.fox, (L * 3 + i) * 8, fox_steps(S, i))
        for e in range(2):
            m = nc.vector.memset(S.wk[e][64 - 64 * e:128 - 64 * e, :], 0.0)
        m.then_inc(S.q0_zero, 1)
        with dve.Fori(0, 2) as i:
            for e in range(2):
                h0 = L * 5 + i * 2 + e
                stk_dve(S, dve, h0 * QB, h0, otok_head(S, 6 + e, i), lambda: top_round(S, dve))
        nc.vector.tensor_scalar(S.dmask[:, :], S.score[:, :], MARK / 2, NEG, ALU.is_gt, ALU.mult).then_inc(S.mask_ready, 1)
        stk_dve(S, dve, (L * 5 + 4) * QB, L * 5 + 4, otok_head(S, 10, 0))
        with dve.Fori(0, 2) as i:
            attn_dve(S, dve, S.dsa, L * 20 + i * 8, dsa_pair(S, i))
        attn_dve(S, dve, S.dsa, L * 20 + 16, dsa_last(S))
        for k in range(KT):
            dve.wait_ge(S.ot_hi, L * KT + k + 1)
            nc.vector.tensor_tensor(S.rl[:, k * SEQ:(k + 1) * SEQ], S.X[k % 4][:, :],
                                    S.rh[:, k * SEQ:(k + 1) * SEQ].bitcast(F32), ALU.subtract).then_inc(S.ot_done, 1)
        with dve.Fori(0, 2) as i:
            for jj in range(4):
                u = A_UP + jj
                s = u % SLOTS
                dve.wait_ge(S.unit_done[s], G(u, i) + 1)
                dve.wait_ge(S.gate_tanh, L * KT + i * 4 + jj + 1)
                a, b, c = S.wk[3 * (jj % 2)][:, :], S.wk[1][:, :], S.wk[2][:, :]
                nc.vector.scalar_tensor_tensor(out=a, in0=cols(S.gates, i * 4 + jj), scalar=1.0, in1=S.ps[s][:, :],
                                               op0=ALU.add, op1=ALU.mult).then_inc(S.bank_free[s], 1)
                for d, o in ((0, b), (1, c)):
                    m = nc.vector.scalar_tensor_tensor(out=o, in0=cols(S.gates, i * 4 + (d + 1) * KT + jj), scalar=1.0,
                                                       in1=S.X[2 * (jj % 2) + d][:, :], op0=ALU.add, op1=ALU.mult)
                m.then_inc(S.merge_x, 1)
                dve.drain()
                nc.vector.tensor_tensor(a, a, b, ALU.add)
                dve.drain()
                nc.vector.tensor_tensor(a, a, c, ALU.add)
                dve.drain()
                mh, ml = cols(S.mh, i * 4 + jj), cols(S.ml, i * 4 + jj)
                nc.vector.tensor_scalar(mh, a, 0.5, None, ALU.mult)
                dve.drain()
                nc.vector.scalar_tensor_tensor(out=ml, in0=a, scalar=0.5, in1=mh.bitcast(F32), op0=ALU.mult,
                                               op1=ALU.subtract).then_inc(S.merge_done, 1)
        dve.wait_ge(S.p_landed, 16 * (L + 1))
        nc.vector.tensor_copy(S.ph[:, :], S.praw[:, :])
        dve.drain()
        nc.vector.tensor_tensor(S.pl[:, :], S.praw[:, :], S.ph[:, :].bitcast(F32), ALU.subtract).then_inc(S.p_ready, 1)
        with dve.Fori(0, 2) as i:
            for j in range(SLOTS):
                u = A_OUT + j
                s = u % SLOTS
                dve.wait_ge(S.unit_done[s], G(u, i) + 1)
                t = cols(S.t, i * SLOTS + j)
                nc.vector.scalar_tensor_tensor(out=t, in0=cols(S.xh, i * SLOTS + j).bitcast(F32), scalar=ALPHA,
                                               in1=S.ps[s][:, :], op0=ALU.mult, op1=ALU.add).then_inc(S.bank_free[s], 1)
                dve.drain()
                nc.vector.scalar_tensor_tensor(out=t, in0=cols(S.xl, i * SLOTS + j).bitcast(F32), scalar=ALPHA,
                                               in1=t, op0=ALU.mult, op1=ALU.add).then_inc(S.t_ready, 1)
        ln_dve(S, dve, L * 2, S.t)
        dve.drain()
        nc.vector.tensor_scalar(S.yacc[:, :], S.xh[:, :].bitcast(F32), ALPHA, None, ALU.mult)
        dve.drain()
        nc.vector.scalar_tensor_tensor(out=S.yacc[:, :], in0=S.xl[:, :].bitcast(F32), scalar=ALPHA, in1=S.yacc[:, :],
                                       op0=ALU.mult, op1=ALU.add)
        with dve.Fori(0, 4) as q:
            with dve.Fori(0, 2) as i:
                for j in range(SLOTS):
                    dve.wait_ge(S.ffn_act, (L * 4 + q) * KT + i * SLOTS + j + 1)
                    h = S.wk[2 + j % 2][:, :]
                    nc.vector.tensor_tensor(h, S.wk[j % 2][:, :], S.wk[j % 2][:, :], ALU.mult)
                    dve.drain()
                    nc.vector.tensor_tensor(cols(S.rl, i * SLOTS + j), h, cols(S.rh, i * SLOTS + j).bitcast(F32),
                                            ALU.subtract).then_inc(S.ffn_h, 1)
            with dve.Fori(0, 2) as i:
                for j in range(SLOTS):
                    u = A_FFN + j
                    s = u % SLOTS
                    dve.wait_ge(S.unit_done[s], G(u, q * 4 + i + 2) + 1)
                    y = cols(S.yacc, i * SLOTS + j)
                    nc.vector.tensor_tensor(y, y, S.ps[s][:, :], ALU.add).then_inc(S.bank_free[s], 1)
        with dve.Fori(0, 2) as i:
            for j in range(SLOTS):
                u = A_PG + j
                s = u % SLOTS
                dve.wait_ge(S.bank_free[s], G(u, i) + 2)
                a, y = S.wk[6 + j % 2][:, :], cols(S.yacc, i * SLOTS + j)
                nc.vector.scalar_tensor_tensor(out=a, in0=S.wk[4 + j % 2][:, :], scalar=1.0, in1=cols(S.plep, i * SLOTS + j),
                                               op0=ALU.add, op1=ALU.mult)
                dve.drain()
                nc.vector.scalar_tensor_tensor(out=y, in0=a, scalar=0.5, in1=y, op0=ALU.mult,
                                               op1=ALU.add).then_inc(S.y_ready, 1)
        ln_dve(S, dve, L * 2 + 1, S.yacc)


def GB(L, u, i=0):
    return DEPTH * A_GROUPS + L * B_GROUPS + u // SLOTS + i


def seq(t, j):
    return t[:, j * SEQ:(j + 1) * SEQ]


def rms_pe(S, pe, n0, j):
    pe.wait_ge(S.rms_sq, n0 * KT + j + 1)
    S.nc.tensor.matmul(S.X[1][:, :], S.ones[:, :], S.wk[j % 4][:, :], start=(j == 0),
                       stop=(j == KT - 1)).then_inc(S.rms_var, 1)


def rms_square(S, act, n0, j):
    act.wait_ge(S.res_ready, n0 * KT + j + 1)
    if j >= 4:
        act.wait_ge(S.rms_var, n0 * KT + j - 3)
    S.nc.scalar.activation(S.wk[j % 4][:, :], seq(S.res, j), ACT.Square).then_inc(S.rms_sq, 1)


def rms_root(S, act, n0):
    act.wait_ge(S.rms_var, n0 * KT + KT)
    S.nc.scalar.activation(S.wk[2][:, :], S.X[1][:, :], ACT.Sqrt, bias=S.eps2[:, :]).then_inc(S.rms_std, 1)


def rms_act(S, act, n0):
    rms_root(S, act, n0)
    for j in range(KT):
        act.wait_ge(S.rms_y, n0 * KT + j + 1)
        S.nc.scalar.activation(seq(S.xh, j), S.wk[4 + j % 4][:, :], ACT.Copy).then_inc(S.rms_hi, 1)


def rms_dve(S, dve, n0):
    nc = S.nc
    dve.wait_ge(S.rms_std, n0 + 1)
    nc.vector.reciprocal(S.wk[3][:, :], S.wk[2][:, :])
    dve.drain()
    for j in range(KT + 2):
        if j < KT:
            nc.vector.scalar_tensor_tensor(out=S.wk[4 + j % 4][:, :], in0=seq(S.res, j), scalar=S.curB[:, PB_G + j:PB_G + j + 1],
                                           in1=S.wk[3][:, :], op0=ALU.mult, op1=ALU.mult).then_inc(S.rms_y, 1)
        if j >= 2:
            q = j - 2
            dve.wait_ge(S.rms_hi, n0 * KT + q + 1)
            nc.vector.tensor_tensor(seq(S.xl, q), S.wk[4 + q % 4][:, :], seq(S.xh, q).bitcast(F32),
                                    ALU.subtract).then_inc(S.x_ready, 1)
            dve.drain()


PARTNER = (0, 2, 3, 0)


def pairs_pe(S, pe, L, u, rh, rl, k0, ready=None, n0=0):
    s = u % SLOTS
    pe.wait_ge(S.lo_ready[s], GB(L, u) + 1)
    pe.wait_ge(S.bank_free[s], GB(L, u) + 1)
    if u == B_OUTN + 3:
        pe.wait_ge(S.bank_free[0], GB(L, B_OUTN) + 2)
    for o, bank in ((0, S.ps[s]), (1, S.X[PARTNER[s]])):
        for k in range(4):
            if ready:
                pe.wait_ge(ready, n0 + k + 1)
            pe_tile(S, s, 4 * o + k, bank[:, :], rh, rl, k0 + k, k == 0, k == 3)
    S.last.then_inc(S.unit_done[s], 1)


def nsa_steps(S, i):
    steps = []
    for tt in range(2):
        for src, k, br in (("s", S.kv["ks"], 1), ("w", S.kv["kw"], 2)):
            for e in range(2):
                for b in range(QB):
                    w = (b + 1) * P
                    qk = [(S.wk[2 * tt + e][:, b * P:w], k[:, 0:w], 0, w),
                          (S.idb[:, :], S.causb[:, :], b * P, P)]

                    def v(kt, src=src, e=e):
                        return S.vtok[src][:, kt * P + e * HD:kt * P + (e + 1) * HD]

                    def scale(n, b=b, e=e, br=br, tt=tt):
                        gate = cols2(S.gate, b * 3 * B_HEADS + e * 12 + tt * 3 + br, i, 6, 1)
                        S.nc.vector.tensor_scalar(S.rg[n % 2][:, :], S.rinv[n % 2][:, :], gate, None, ALU.mult)

                    def norm(n, b=b, e=e, tt=tt):
                        o = cols2(S.ot2, b * 512 + e * 256 + tt * HD, i, 2 * HD, HD)
                        S.nc.vector.scalar_tensor_tensor(out=o, in0=S.X[3][:, 0:HD], scalar=S.rg[n % 2][:, :], in1=o,
                                                         op0=ALU.mult, op1=ALU.add).then_inc(S.nsa.out, 1)
                    steps.append(Step(b, qk, v, norm, scale))
    return steps


def out_fill(S, pe, L, i, n):
    j, k = divmod(n, KT)
    o, kk = divmod(k, 4)
    g = GB(L, B_OUTL, i)
    if k == 0:
        pe.wait_ge(S.lo_ready[j], g + 1)
        if j >= 2:
            pe.wait_ge(S.bank_free[j - 2], g + 2)
        else:
            pe.wait_ge(S.bank_free[j + 2], g + 1)
    pe_tile(S, j, k, S.ps[2 * (j % 2) + o][:, :], S.xh, S.xl, i * 4 + kk, kk == 0, kk == 3)
    if k == KT - 1:
        S.last.then_inc(S.unit_done[j], 1)


def out_add(S, dve, L, i, j):
    dve.wait_ge(S.unit_done[j], GB(L, B_OUTL, i) + 1)
    S.nc.vector.tensor_tensor(seq(S.res, 2 * j), seq(S.res, 2 * j), S.ps[2 * (j % 2)][:, :], ALU.add)
    S.nc.vector.tensor_tensor(seq(S.res, 2 * j + 1), seq(S.res, 2 * j + 1), S.ps[2 * (j % 2) + 1][:, :],
                              ALU.add).then_inc(S.bank_free[j], 1)


def rope_tiles(S):
    return [S.kv[n][:, :] for n in ("kc", "ks", "kw")] + [seq(S.q, t) for t in range(4)]


NROPE = 7


def b_tensor(S, pe):
    nc = S.nc
    ident = S.con[:, C_ID:C_ID + P]
    for j in range(KT):
        rms_pe(S, pe, 0, j)
    with pe.Fori(0, DEPTH) as L:
        with pe.Fori(0, 8) as i:
            for u in range(SLOTS):
                pe_unit(S, pe, u, GB(L, u, i), S.ps[u][:, :], S.xh, S.xl, None if u else S.x_ready,
                        KT * (1 + 2 * DEPTH) + L * KT).then_inc(S.unit_done[u], 1)
        for u in (32, 33, 34):
            pe_unit(S, pe, u, GB(L, u), S.ps[u % SLOTS][:, :], S.xh, S.xl).then_inc(S.unit_done[u % SLOTS], 1)
        pe.wait_ge(S.bank_free[B_G % SLOTS], GB(L, B_G) + 2)
        for v, name in enumerate(("vs", "vw", "gl")):
            if v >= 2:
                pe.wait_ge(S.bvt_done, L * 2 + 1)
            for t in range(QB):
                m = nc.tensor.transpose(S.X[2 + v % 2][:, t * P:(t + 1) * P], S.kv[name][:, t * P:(t + 1) * P], ident)
            m.then_inc(S.bvt_ready, 1)
        for n, t in enumerate(rope_tiles(S)):
            if n >= 2:
                pe.wait_ge(S.b_rope_done, L * NROPE + n - 1)
            nc.tensor.matmul(S.X[n % 2][:, :], S.con[:, C_ROT:C_ROT + P], t, start=True, stop=True).then_inc(S.b_rot_ready, 1)
        s = B_BD % SLOTS
        pe.wait_ge(S.lo_ready[s], GB(L, B_BD) + 1)
        pe.wait_ge(S.xc_split, L + 1)
        pe.wait_ge(S.b_rope_done, (L + 1) * NROPE)
        pe.wait_ge(S.bvt_done, L * 2 + 2)
        pe.wait_ge(S.gl_done, L + 1)
        for t in range(4):
            if t >= 2:
                pe.wait_ge(S.lru_gate, L * 4 + t - 1)
            for d in range(2):
                pe_tile(S, s, 2 * t + d, S.X[2 * (t % 2) + d][:, :], S.xh, S.xl, t, True, True)
            S.last.then_inc(S.lru_ready, 1)
        S.last = nc.tensor.matmul(S.ps[s][:, 0:P], ident, ident, start=True, stop=True)
        S.last.then_inc(S.unit_done[s], 1)
        pe.wait_ge(S.lru_gate, L * 4 + 4)
        for kv in range(2):
            pe.wait_ge(S.blk_ready, L * 2 + kv + 1)
            for m in range(2):
                for half in range(2):
                    u = B_CMP1 + 4 * kv + 2 * m + half
                    s = u % SLOTS
                    pe.wait_ge(S.lo_ready[s], GB(L, u) + 1)
                    out = S.X[kv][:, m * HD:m * HD + NB2]
                    for k in range(KT):
                        lp = half * KT + k
                        c = (4 + 2 * kv) * SEQ + lp * NB2
                        wh, wl = (t[s][:, k * P:(k + 1) * P] for t in (S.wh, S.wl))
                        bh, bl = (t[:, c:c + NB2] for t in (S.xh, S.xl))
                        nc.tensor.matmul(out, wh, bh, start=(lp == 0), stop=False, skip_group_check=True)
                        nc.tensor.matmul(out, wh, bl, start=False, stop=False, skip_group_check=True)
                        mm = nc.tensor.matmul(out, wl, bh, start=False, stop=(lp == 15), skip_group_check=True)
                    mm.then_inc(S.unit_done[s], 1)
        s = B_CMP2 % SLOTS
        pe.wait_ge(S.lo_ready[s], GB(L, B_CMP2) + 1)
        pe.wait_ge(S.hid_split, L * 2 + 1)
        for m in range(2):
            wh, wl = (t[s][:, m * P:(m + 1) * P] for t in (S.wh, S.wl))
            bh, bl = (t[:, m * NB2:(m + 1) * NB2] for t in (S.hkh, S.hkl))
            for i, (a, b) in enumerate(((wh, bh), (wh, bl), (wl, bh))):
                mm = nc.tensor.matmul(S.X[2][:, 0:NB2], a, b, start=(m == 0 and i == 0), stop=(m == 1 and i == 2))
        mm.then_inc(S.unit_done[s], 1)
        s = (B_CMP2 + 1) % SLOTS
        pe.wait_ge(S.lo_ready[s], GB(L, B_CMP2 + 1) + 1)
        pe.wait_ge(S.hid_split, L * 2 + 2)
        for g in range(2):
            for m in range(2):
                wh, wl = (t[s][:, m * P:m * P + HD] for t in (S.wh, S.wl))
                bh, bl = (t[:, (2 * m + g) * P:(2 * m + g + 1) * P] for t in (S.hvh, S.hvl))
                for i, (a, b) in enumerate(((bh, wh), (bh, wl), (bl, wh))):
                    mm = nc.tensor.matmul(S.X[3][:, g * HD:(g + 1) * HD], a, b, start=(m == 0 and i == 0),
                                          stop=(m == 1 and i == 2), skip_group_check=True)
        mm.then_inc(S.unit_done[s], 1)
        pe.wait_ge(S.kcb_ready, L + 1)
        for b in range(QB):
            for t in range(B_REP):
                o = S.X[b // 2][:, (b % 2) * 256:(b % 2 + 1) * 256].rearrange("p (g t n) -> p g t n", g=2, t=B_REP)[:, :, t, :]
                mm = nc.tensor.matmul(o, S.q[:, t * SEQ + b * P:t * SEQ + (b + 1) * P],
                                      S.kcb[:, :].rearrange("p (g n) -> p g n", g=2), start=True, stop=True, skip_group_check=True)
            if b % 2:
                mm.then_inc(S.cs_ready, 1)
        pe.wait_ge(S.vbd_ready, L + 1)
        for h in range(2):
            pe.wait_ge(S.cp_ready, L * 2 + h + 1)
            for k in range(4):
                mm = nc.tensor.transpose(S.X[2 + h][:, k * P:(k + 1) * P], S.wk[4 + h][:, k * P:(k + 1) * P], ident)
            mm.then_inc(S.cpt_ready, 1)
        for b in range(QB):
            pe.wait_ge(S.cpt_copied, L * 2 + b // 2 + 1)
            if b >= 2:
                pe.wait_ge(S.oc_done, L * 4 + b - 1)
            for g in range(2):
                c = ((b % 2) * 2 + g) * P
                mm = nc.tensor.matmul(S.X[b % 2][:, g * 256:(g + 1) * 256], S.wk[6 + b // 2][:, c:c + P],
                                      S.vbd[:, g * 256:(g + 1) * 256], start=True, stop=True, skip_group_check=True)
            mm.then_inc(S.oc_ready, 1)
        pe.wait_ge(S.oc_done, L * 4 + 4)
        pe.wait_ge(S.dw_done, L + 1)
        for t in range(4):
            mm = nc.tensor.matmul(S.X[0][:, :], S.ones[:, :], seq(S.cacc, t), start=(t == 0), stop=(t == 3))
        mm.then_inc(S.cl_mean, 1)
        for t in range(4):
            pe.wait_ge(S.cl_sq, L * 4 + t + 1)
            nc.tensor.matmul(S.X[1][:, :], S.ones[:, :], S.wk[t][:, :], start=(t == 0), stop=(t == 3)).then_inc(S.cl_var, 1)
        for u in (B_PW2, B_PW2 + 1):
            pairs_pe(S, pe, L, u, S.xh, S.xl, 4, S.un_ready, L * 4)
        with pe.Fori(0, 2) as i:
            pe.wait_ge(S.lru_done, L + 1)
            pe.wait_ge(S.mc_ready, L * 4 + 4)
            pe.wait_ge(S.q_zero, L + 1)
            pe.wait_ge(S.q_staged, L * 8 + i * 4 + 4)
            attn_pe(S, pe, S.nsa, L * 64 + i * 32, nsa_steps(S, i), ident,
                    lambda n, half: half and out_fill(S, pe, L, i, n))
        pe.wait_ge(S.nsa.out, (L + 1) * 64 + 2)
        for k in range(4):
            for b in range(QB):
                mm = nc.tensor.transpose(S.X[k][:, b * P:(b + 1) * P], S.ot2[:, b * 512 + k * P:b * 512 + (k + 1) * P], ident)
            mm.then_inc(S.bt_ready, 1)
        for j in range(4):
            pairs_pe(S, pe, L, B_OUTN + j, S.mnh, S.mnl, 0, None if j else S.mn_ready, L * 4)
            for x in range(2 * j - 2, 2 * j):
                if x >= 0:
                    rms_pe(S, pe, L + 1, x)
        rms_pe(S, pe, L + 1, KT - 2)
        rms_pe(S, pe, L + 1, KT - 1)


def b_scalar(S, act, T):
    nc = S.nc

    def take(L, u, i, out, func, **kw):
        s = u % SLOTS
        act.wait_ge(S.unit_done[s], GB(L, u, i) + 1)
        nc.scalar.activation(out, S.ps[s][:, :], func, **kw).then_inc(S.bank_free[s], 1)
        act_split(S, act, u, GB(L, u, i))

    def used(L, u, i=0):
        act.wait_ge(S.unit_done[u % SLOTS], GB(L, u, i) + 1)
        act_split(S, act, u, GB(L, u, i))

    act.dma_start(S.prmB[:, :], T["prm_b"]).then_inc(S.pb_landed, 16)
    for j in range(KT):
        rms_square(S, act, 0, j)
    with act.Fori(0, DEPTH) as L:
        rms_act(S, act, L)
        act.wait_ge(S.x_ready, KT * (2 + 2 * DEPTH) + L * KT)
        act.dma_start(S.pos[:, :], T["pos"].to_broadcast([P, SEQ])).then_inc(S.pb_landed, 16)
        act.wait_ge(S.lam_in, L + 1)
        nc.scalar.activation(S.lam[0][:, :], S.lam[0][:, :], ACT.Exp).then_inc(S.lam_out, 1)
        for j in range(SLOTS):
            c = j * UC_W + CONV_K - 1
            take(L, B_GA + j, 0, S.uc[:, c:c + SEQ], ACT.Copy, scale=0.5)
        act.wait_ge(S.ang_ready, L + 1)
        nc.scalar.activation(S.sin[:, :], S.wk[0][:, :], ACT.Sin)
        nc.scalar.activation(S.cos[:, :], S.wk[1][:, :], ACT.Sin, scale=-1.0, bias=S.halfpi[:, :]).then_inc(S.tab_ready, 1)
        for j in range(SLOTS):
            if j >= 2:
                act.wait_ge(S.glu_done, L * 4 + j - 1)
            take(L, B_GB + j, 0, S.wk[6 + j % 2][:, :], ACT.Tanh, scale=0.5)
        for j in range(SLOTS):
            c = j * UP_W + LRU_K - 1
            take(L, B_U + j, 0, S.up[:, c:c + SEQ], ACT.Copy)
        for u0, z in ((B_ZL, S.zl), (B_ZC, S.zc), (B_ZN, S.zn)):
            for j in range(SLOTS):
                take(L, u0 + j, 0, seq(z, j), ACT.Silu)
        for j in range(SLOTS):
            take(L, B_Q + j, 0, seq(S.q, j), ACT.Copy, scale=HD ** -0.5)
        for j, name in enumerate(("kc", "ks", "kw", "vc", "vs", "vw")):
            take(L, B_KV + j, 0, S.kv[name][:, :], ACT.Copy)
        take(L, B_G, 0, S.kv["gl"][:, :], ACT.Tanh, scale=0.5, bias=S.curB[:, PB_BG:PB_BG + 1])
        for v, name in enumerate("sw"):
            act.wait_ge(S.bvt_ready, L * 3 + v + 1)
            nc.scalar.activation(S.vtok[name][:, :], S.X[2 + v][:, :], ACT.Copy).then_inc(S.bvt_done, 1)
        for kv, name in enumerate(("kc", "vc")):
            if kv == 0:
                act.wait_ge(S.b_rope_done, L * NROPE + 1)
            for g in range(2):
                for l2 in range(2):
                    src = S.kv[name][64 * g:64 * g + 64, :]
                    o = S.blk[kv][64 * l2:64 * l2 + 64, :].rearrange("p (a g n) -> p a g n", a=16, g=2)[:, :, g, :]
                    for half in range(2):
                        i = src[:, 16 * half:16 * half + 16 * NBLK].rearrange("p (n a l) -> p a n l", a=8, l=2)[:, :, :, l2]
                        m = nc.scalar.activation(o[:, 8 * half:8 * half + 8, :], i, ACT.Copy)
            m.then_inc(S.blk_raw, 1)
        act.wait_ge(S.blk_ready, L * 2 + 2)
        for t in range(4):
            act.wait_ge(S.lru_ready, L * 4 + t + 1)
            nc.scalar.activation(seq(S.la, t), S.X[2 * (t % 2)][:, :], ACT.Tanh, scale=0.5, bias=S.curB[:, PB_BA + t:PB_BA + t + 1])
            nc.scalar.activation(seq(S.lri, t), S.X[2 * (t % 2) + 1][:, :], ACT.Tanh, scale=0.5,
                                 bias=S.curB[:, PB_BI + t:PB_BI + t + 1]).then_inc(S.lru_gate, 1)
        used(L, B_BD)
        act.wait_ge(S.nla_ready, L + 1)
        nc.scalar.activation(S.ls[:, :], S.la[:, :], ACT.Tanh).then_inc(S.s_ready, 1)
        act.drain()
        nc.scalar.activation(S.la[:, :], S.la[:, :], ACT.Exp, scale=-1.0).then_inc(S.a_ready, 1)
        act.wait_ge(S.b2_ready, L + 1)
        nc.scalar.activation(S.ls[:, :], S.ls[:, :], ACT.Sqrt, bias=S.tiny[:, :]).then_inc(S.beta_ready, 1)
        for kv in range(2):
            for u in range(4):
                used(L, B_CMP1 + 4 * kv + u)
            if kv == 0:
                act.wait_ge(S.lru_done, L + 1)
            nc.scalar.activation(S.wk[0][:, kv * 2 * HD:kv * 2 * HD + 2 * NB2].rearrange("p (m n) -> p m n", m=2),
                                 S.X[kv][:, 0:2 * HD].rearrange("p (m n) -> p m n", m=2)[:, :, 0:NB2],
                                 ACT.Silu).then_inc(S.hid_act, 1)
        used(L, B_CMP2)
        used(L, B_CMP2 + 1)
        for h in range(2):
            act.wait_ge(S.cexp_in, L * 2 + h + 1)
            nc.scalar.activation(S.wk[4 + h][:, :], S.wk[4 + h][:, :], ACT.Exp).then_inc(S.cexp_out, 1)
        for h in range(2):
            act.wait_ge(S.cpt_ready, L * 2 + h + 1)
            nc.scalar.activation(S.wk[6 + h][:, :], S.X[2 + h][:, :], ACT.Copy).then_inc(S.cpt_copied, 1)
        for t in range(4):
            act.wait_ge(S.cl_d, L * 4 + t + 1)
            nc.scalar.activation(S.wk[t][:, :], seq(S.cacc, t), ACT.Square).then_inc(S.cl_sq, 1)
        act.wait_ge(S.cl_var, L * 4 + 4)
        nc.scalar.activation(S.wk[4][:, :], S.X[1][:, :], ACT.Sqrt, scale=2.0, bias=S.eps2[:, :]).then_inc(S.cl_std, 1)
        for t in range(4):
            act.wait_ge(S.cl_y, L * 4 + t + 1)
            nc.scalar.activation(seq(S.cacc, t), seq(S.cacc, t), ACT.Silu)
            act.drain()
            nc.scalar.activation(seq(S.xh, 4 + t), seq(S.cacc, t), ACT.Copy).then_inc(S.cl_hi, 1)
        used(L, B_PW2)
        used(L, B_PW2 + 1)
        for t in range(4):
            act.wait_ge(S.mc_y, L * 4 + t + 1)
            nc.scalar.activation(seq(S.xh, 4 + t), seq(S.zc, t), ACT.Copy).then_inc(S.mc_hi, 1)
        with act.Fori(0, 2) as i:
            for tt in range(2):
                for e in range(2):
                    r = slice(64 * e, 64 * e + 64)
                    nc.scalar.activation(S.wk[2 * tt + e][r, :], cols2(S.q[r, :], tt * SEQ, i, 2 * SEQ, SEQ),
                                         ACT.Copy).then_inc(S.q_staged, 1)
            attn_act(S, act, S.nsa, L * 64 + i * 32, nsa_steps(S, i),
                     lambda n: n and n % KT == 0 and used(L, B_OUTL + n // KT - 1, i))
            used(L, B_OUTL + 3, i)
        for k in range(4):
            act.wait_ge(S.mn_y, L * 4 + k + 1)
            nc.scalar.activation(seq(S.mnh, k), seq(S.zn, k), ACT.Copy).then_inc(S.mn_hi, 1)
        for j in range(4):
            used(L, B_OUTN + j)
            for x in (2 * j, 2 * j + 1):
                rms_square(S, act, L + 1, x)
    rms_root(S, act, DEPTH)


def free_bank(S, dve, u):
    s = u % SLOTS
    S.nc.vector.memset(S.tick[:, 24 + s:25 + s], 0.0).then_inc(S.bank_free[s], 1)


def b_rope_tables(S, dve, L):
    nc = S.nc
    ang, k, r = S.wk[2][:, :], S.wk[3][:, :], S.wk[0][:, :]
    two_pi = (6.25, 0.033203125, 2 * math.pi - 6.25 - 0.033203125)
    magic = 1.5 * 2.0 ** 23
    dve.wait_ge(S.pb_landed, 16 * (L + 2))
    nc.vector.tensor_copy(ang, S.pos[:, :])
    dve.drain()
    nc.vector.tensor_scalar(ang, ang, S.prmB[:, PB_INV:PB_INV + 1], None, ALU.mult)
    dve.drain()
    nc.vector.tensor_scalar(k, ang, 1 / (2 * math.pi), magic, ALU.mult, ALU.add)
    dve.drain()
    nc.vector.tensor_scalar(k, k, magic, None, ALU.subtract)
    dve.drain()
    nc.vector.scalar_tensor_tensor(out=r, in0=k, scalar=-two_pi[0], in1=ang, op0=ALU.mult, op1=ALU.add)
    for part in two_pi[1:]:
        dve.drain()
        nc.vector.scalar_tensor_tensor(out=r, in0=k, scalar=-part, in1=r, op0=ALU.mult, op1=ALU.add)
    dve.drain()
    nc.vector.tensor_scalar(r, r, 3.1415925, -3.1415925, ALU.min, ALU.max)
    dve.drain()
    nc.vector.scalar_tensor_tensor(out=S.wk[1][:, :], in0=r, scalar=-1.0, in1=r, op0=ALU.mult, op1=ALU.max).then_inc(S.ang_ready, 1)


def b_softplus(S, dve, L):
    nc = S.nc
    e, y, y2, p, m = (t[:, :] for t in S.lam)
    lam = S.curB[:, PB_LAM:PB_LAM + 4]
    dve.wait_ge(S.lam_out, L + 1)
    nc.vector.tensor_scalar(y, e, 2.0, None, ALU.add)
    dve.drain()
    nc.vector.reciprocal(y, y)
    dve.drain()
    nc.vector.tensor_tensor(y, y, e, ALU.mult)
    dve.drain()
    nc.vector.tensor_tensor(y2, y, y, ALU.mult)
    dve.drain()
    nc.vector.tensor_scalar(p, y2, 1 / 15, None, ALU.mult)
    for k in range(13, 1, -2):
        dve.drain()
        nc.vector.scalar_tensor_tensor(out=p, in0=p, scalar=1 / k, in1=y2, op0=ALU.add, op1=ALU.mult)
    dve.drain()
    nc.vector.scalar_tensor_tensor(out=p, in0=p, scalar=1.0, in1=y, op0=ALU.add, op1=ALU.mult)
    nc.vector.tensor_scalar(m, lam, -4.0, 0.0, ALU.mult, ALU.max)
    dve.drain()
    nc.vector.scalar_tensor_tensor(out=lam, in0=p, scalar=8.0, in1=m, op0=ALU.mult, op1=ALU.add)
    dve.drain()


def b_vector(S, dve):
    nc = S.nc
    col = lambda c: S.curB[:, c:c + 1]
    stt = nc.vector.scalar_tensor_tensor
    dve.drain()
    for j in range(KT):
        nc.vector.tensor_tensor(seq(S.res, j), seq(S.xh, j).bitcast(F32), seq(S.xl, j).bitcast(F32),
                                ALU.add).then_inc(S.res_ready, 1)
    dve.wait_ge(S.pb_landed, 16)
    with dve.Fori(0, DEPTH) as L:
        nc.vector.tensor_copy(S.curB[:, :], cols(S.prmB, L, PB_N))
        for t, w, pad in ((S.uc, UC_W, CONV_K - 1), (S.up, UP_W, LRU_K - 1)):
            for j in range(4):
                nc.vector.memset(t[:, j * w:j * w + pad], 0.0)
        dve.drain()
        half = S.curB[:, PB_BG:PB_LAM]
        nc.vector.tensor_scalar(half, half, 0.5, None, ALU.mult)
        lam = S.curB[:, PB_LAM:PB_LAM + 4]
        stt(out=S.lam[0][:, :], in0=lam, scalar=-1.0, in1=lam, op0=ALU.mult, op1=ALU.min).then_inc(S.lam_in, 1)
        rms_dve(S, dve, L)
        b_rope_tables(S, dve, L)
        b_softplus(S, dve, L)
        for j in range(4):
            u = B_GB + j
            dve.wait_ge(S.bank_free[u % SLOTS], GB(L, u) + 2)
            t = S.uc[:, j * UC_W + CONV_K - 1:(j + 1) * UC_W]
            stt(out=t, in0=S.wk[6 + j % 2][:, :], scalar=1.0, in1=t, op0=ALU.add, op1=ALU.mult).then_inc(S.glu_done, 1)
        for k in range(LRU_K):
            for t in range(4):
                src, o, w = S.up[:, t * UP_W + k:t * UP_W + k + SEQ], seq(S.xc, t), col(PB_LCW + t * LRU_K + k)
                if k == 0:
                    dve.wait_ge(S.bank_free[t], GB(L, B_U + t) + 2)
                    nc.vector.tensor_scalar(o, src, w, col(PB_LCB + t), ALU.mult, ALU.add)
                else:
                    stt(out=o, in0=src, scalar=w, in1=o, op0=ALU.mult, op1=ALU.add)
            dve.drain()
        for t in range(4):
            nc.vector.tensor_scalar(seq(S.cacc, t), S.uc[:, t * UC_W:t * UC_W + SEQ], col(PB_DW + t * CONV_K), col(PB_DWB + t),
                                    ALU.mult, ALU.add)
        dve.drain()
        with dve.Fori(1, CONV_K) as k:
            for t in range(4):
                stt(out=seq(S.cacc, t), in0=S.uc[:, bass.ds(k + t * UC_W, SEQ)], scalar=S.curB[:, bass.ds(k + (PB_DW + t * CONV_K), 1)],
                    in1=seq(S.cacc, t), op0=ALU.mult, op1=ALU.add)
            dve.drain()
        x4h, x4l = S.xh[:, 0:4 * SEQ], S.xl[:, 0:4 * SEQ]
        dve.wait_ge(S.unit_done[B_G % SLOTS], GB(L, B_G) + 1)
        nc.vector.tensor_copy(x4h, S.xc[:, :]).then_inc(S.dw_done, 1)
        dve.drain()
        nc.vector.tensor_tensor(x4l, S.xc[:, :], x4h.bitcast(F32), ALU.subtract).then_inc(S.xc_split, 1)
        dve.wait_ge(S.bvt_ready, L * 3 + 3)
        nc.vector.tensor_scalar(S.gate[:, :].rearrange("p (b c) -> p b c", b=QB),
                                S.X[2][:, :].rearrange("p (b c) -> p b c", b=QB)[:, :, 0:3 * B_HEADS], 1.0, 0.5,
                                ALU.add, ALU.mult).then_inc(S.gl_done, 1)
        dve.wait_ge(S.tab_ready, L + 1)
        for n, t in enumerate(rope_tiles(S)):
            a, b = S.wk[4 + n % 2][:, :], S.wk[6 + n % 2][:, :]
            nc.vector.tensor_tensor(a, t, S.cos[:, :], ALU.mult)
            dve.wait_ge(S.b_rot_ready, L * NROPE + n + 1)
            nc.vector.tensor_tensor(b, S.X[n % 2][:, :], S.sin[:, :], ALU.mult)
            dve.drain()
            nc.vector.tensor_tensor(t, a, b, ALU.add).then_inc(S.b_rope_done, 1)
        for kv in range(2):
            dve.wait_ge(S.blk_raw, L * 2 + kv + 1)
            t = S.blk[kv][:, :].rearrange("p (a n) -> p a n", a=16)
            pos = S.curB[:, PB_POS + 16 * kv:PB_POS + 16 * kv + 16]
            c = (4 + 2 * kv) * SEQ
            bh, bl = S.xh[:, c:c + 16 * NB2], S.xl[:, c:c + 16 * NB2]
            nc.vector.tensor_tensor(t, t, pos.unsqueeze(2).to_broadcast([P, 16, NB2]), ALU.add)
            dve.drain()
            nc.vector.tensor_copy(bh, S.blk[kv][:, :])
            dve.drain()
            nc.vector.tensor_tensor(bl, S.blk[kv][:, :], bh.bitcast(F32), ALU.subtract).then_inc(S.blk_ready, 1)
        dve.wait_ge(S.lru_gate, L * 4 + 4)
        free_bank(S, dve, B_BD)
        for t in range(4):
            m = nc.vector.tensor_scalar(seq(S.la, t), seq(S.la, t), 1.0, col(PB_LAM + t), ALU.add, ALU.mult)
        m.then_inc(S.nla_ready, 1)
        stt(out=S.lri[:, :], in0=S.lri[:, :], scalar=1.0, in1=S.xc[:, :], op0=ALU.add, op1=ALU.mult)
        dve.wait_ge(S.s_ready, L + 1)
        nc.vector.tensor_scalar(S.lrt[:, :], S.ls[:, :], 1.0, None, ALU.add)
        dve.drain()
        nc.vector.reciprocal(S.lrt[:, :], S.lrt[:, :])
        dve.drain()
        stt(out=S.ls[:, :], in0=S.ls[:, :], scalar=2.0, in1=S.lrt[:, :], op0=ALU.mult, op1=ALU.mult).then_inc(S.b2_ready, 1)
        dve.wait_ge(S.beta_ready, L + 1)
        stt(out=S.lri[:, :], in0=S.lri[:, :], scalar=0.5, in1=S.ls[:, :], op0=ALU.mult, op1=ALU.mult)
        dve.drain()
        for t in range(4):
            dve.wait_ge(S.a_ready, L + 1)
            nc.vector.tensor_tensor_scan(seq(S.lrt, t), seq(S.la, t), seq(S.lri, t), 0.0, ALU.mult, ALU.add)
        dve.drain()
        nc.vector.tensor_tensor(S.la[:, :], S.lrt[:, :], S.zl[:, :], ALU.mult)
        dve.drain()
        nc.vector.tensor_copy(x4h, S.la[:, :])
        dve.drain()
        nc.vector.tensor_tensor(x4l, S.la[:, :], x4h.bitcast(F32), ALU.subtract).then_inc(S.lru_done, 1)
        nc.vector.memset(S.kcb[:, :], 0.0)
        nc.vector.memset(S.vbd[:, :], 0.0)
        dve.drain()
        for kv in range(2):
            dve.wait_ge(S.hid_act, L * 2 + kv + 1)
            for u in range(4):
                free_bank(S, dve, B_CMP1 + 4 * kv + u)
            h = S.wk[0][:, kv * 2 * HD:kv * 2 * HD + 2 * NB2]
            if kv == 0:
                nc.vector.tensor_copy(S.hkh[:, :], h)
                dve.drain()
                nc.vector.tensor_tensor(S.hkl[:, :], h, S.hkh[:, :].bitcast(F32), ALU.subtract).then_inc(S.hid_split, 1)
            else:
                nc.vector.memset(S.hvh[:, :].bitcast(F32), 0.0)
                nc.vector.memset(S.hvl[:, :].bitcast(F32), 0.0)
                dve.drain()
                rep = lambda x, i: x[:, i * P:(i + 1) * P].rearrange("p (j n) -> p j n", j=4)[:, :, 0:NBLK]
                one = lambda i: h[:, i * NBLK:(i + 1) * NBLK].unsqueeze(1).to_broadcast([P, 4, NBLK])
                for i in range(4):
                    nc.vector.tensor_copy(rep(S.hvh, i), one(i))
                dve.drain()
                for i in range(4):
                    m = nc.vector.tensor_tensor(rep(S.hvl, i), one(i), rep(S.hvh, i).bitcast(F32), ALU.subtract)
                m.then_inc(S.hid_split, 1)
        dve.wait_ge(S.unit_done[B_CMP2 % SLOTS], GB(L, B_CMP2) + 1)
        for g in range(2):
            m = nc.vector.tensor_copy(S.kcb[64 * g:64 * g + 64, 32 * g:32 * g + NBLK],
                                      S.X[2][64 * g:64 * g + 64, g * NBLK:(g + 1) * NBLK])
        m.then_inc(S.kcb_ready, 1)
        dve.wait_ge(S.unit_done[(B_CMP2 + 1) % SLOTS], GB(L, B_CMP2 + 1) + 1)
        for g in range(2):
            for t in range(4):
                m = nc.vector.tensor_copy(S.vbd[32 * t:32 * t + 32, (4 * g + t) * HD:(4 * g + t + 1) * HD],
                                          S.X[3][32 * t:32 * t + 32, g * HD:(g + 1) * HD])
        m.then_inc(S.vbd_ready, 1)
        free_bank(S, dve, B_CMP2)
        free_bank(S, dve, B_CMP2 + 1)
        for h in range(2):
            dve.wait_ge(S.cs_ready, L * 2 + h + 1)
            p4 = S.wk[4 + h][:, :].rearrange("p (b t n) -> p b t n", b=2, t=B_HEADS)
            p3 = S.wk[4 + h][:, :].rearrange("p (r n) -> p r n", n=32)
            mask = S.cmask[:, 64 * h:64 * h + 64].rearrange("p (b n) -> p b n", b=2).unsqueeze(2).to_broadcast([P, 2, B_HEADS, 32])
            mx = S.cmx[:, 16 * h:16 * h + 16]
            nc.vector.tensor_tensor(p4, S.X[h][:, :].rearrange("p (b t n) -> p b t n", b=2, t=B_HEADS), mask, ALU.add)
            dve.drain()
            nc.vector.tensor_reduce(mx, p3, AX, ALU.max)
            dve.drain()
            nc.vector.tensor_scalar(mx, mx, NEG / 10, None, ALU.max)
            dve.drain()
            nc.vector.tensor_tensor(p3, p3, mx.unsqueeze(2).to_broadcast([P, 16, 32]), ALU.subtract).then_inc(S.cexp_in, 1)
        for h in range(2):
            dve.wait_ge(S.cexp_out, L * 2 + h + 1)
            p3 = S.wk[4 + h][:, :].rearrange("p (r n) -> p r n", n=32)
            sm = S.csum[:, 16 * h:16 * h + 16]
            nc.vector.tensor_reduce(sm, p3, AX, ALU.add)
            dve.drain()
            nc.vector.tensor_scalar(sm, sm, 1e-30, None, ALU.max)
            dve.drain()
            nc.vector.reciprocal(sm, sm)
            dve.drain()
            gate = S.gate[:, 48 * h:48 * h + 48].rearrange("p (r c) -> p r c", c=3)[:, :, 0]
            nc.vector.tensor_tensor(sm, sm, gate, ALU.mult)
            dve.drain()
            nc.vector.tensor_tensor(p3, p3, sm.unsqueeze(2).to_broadcast([P, 16, 32]), ALU.mult).then_inc(S.cp_ready, 1)
        for b in range(QB):
            dve.wait_ge(S.oc_ready, L * 4 + b + 1)
            nc.vector.tensor_copy(S.ot2[:, b * 512:(b + 1) * 512], S.X[b % 2][:, :]).then_inc(S.oc_done, 1)
        dve.wait_ge(S.cl_mean, L + 1)
        for t in range(4):
            stt(out=seq(S.cacc, t), in0=S.X[0][:, :], scalar=-2.0, in1=seq(S.cacc, t), op0=ALU.mult, op1=ALU.add).then_inc(S.cl_d, 1)
        dve.wait_ge(S.cl_std, L + 1)
        nc.vector.reciprocal(S.wk[5][:, :], S.wk[4][:, :])
        dve.drain()
        for t in range(4):
            nc.vector.tensor_tensor(seq(S.cacc, t), seq(S.cacc, t), S.wk[5][:, :], ALU.mult)
        dve.drain()
        for t in range(4):
            nc.vector.tensor_scalar(seq(S.cacc, t), seq(S.cacc, t), col(PB_LNG + t), col(PB_LNB + t),
                                    ALU.mult, ALU.add).then_inc(S.cl_y, 1)
        for t in range(4):
            dve.wait_ge(S.cl_hi, L * 4 + t + 1)
            nc.vector.tensor_tensor(seq(S.xl, 4 + t), seq(S.cacc, t), seq(S.xh, 4 + t).bitcast(F32), ALU.subtract).then_inc(S.un_ready, 1)
        for d in range(2):
            u = B_PW2 + d
            s = u % SLOTS
            dve.wait_ge(S.unit_done[s], GB(L, u) + 1)
            nc.vector.tensor_tensor(seq(S.zc, 2 * d), seq(S.zc, 2 * d), S.ps[s][:, :], ALU.mult).then_inc(S.mc_y, 1)
            nc.vector.tensor_tensor(seq(S.zc, 2 * d + 1), seq(S.zc, 2 * d + 1), S.X[PARTNER[s]][:, :], ALU.mult).then_inc(S.mc_y, 1)
            dve.drain()
            free_bank(S, dve, u)
        for t in range(4):
            dve.wait_ge(S.mc_hi, L * 4 + t + 1)
            nc.vector.tensor_tensor(seq(S.xl, 4 + t), seq(S.zc, t), seq(S.xh, 4 + t).bitcast(F32), ALU.subtract).then_inc(S.mc_ready, 1)

        for n in range(4):
            e = 1 - n % 2
            m = nc.vector.memset(S.wk[n][64 * e:64 * e + 64, :], 0.0)
        m.then_inc(S.q_zero, 1)
        with dve.Fori(0, 2) as i:
            attn_dve(S, dve, S.nsa, L * 64 + i * 32, nsa_steps(S, i),
                     lambda n: n and n % KT == 0 and out_add(S, dve, L, i, n // KT - 1))
            out_add(S, dve, L, i, 3)
            dve.drain()
        for k in range(4):
            dve.wait_ge(S.bt_ready, L * 4 + k + 1)
            nc.vector.tensor_tensor(seq(S.zn, k), seq(S.zn, k), S.X[k][:, :], ALU.mult).then_inc(S.mn_y, 1)
        for k in range(4):
            dve.wait_ge(S.mn_hi, L * 4 + k + 1)
            nc.vector.tensor_tensor(seq(S.mnl, k), seq(S.zn, k), seq(S.mnh, k).bitcast(F32), ALU.subtract).then_inc(S.mn_ready, 1)
        for j in range(4):
            s = (B_OUTN + j) % SLOTS
            dve.wait_ge(S.unit_done[s], GB(L, B_OUTN + j) + 1)
            nc.vector.tensor_tensor(seq(S.res, 2 * j), seq(S.res, 2 * j), S.ps[s][:, :], ALU.add).then_inc(S.res_ready, 1)
            nc.vector.tensor_tensor(seq(S.res, 2 * j + 1), seq(S.res, 2 * j + 1), S.X[PARTNER[s]][:, :],
                                    ALU.add).then_inc(S.res_ready, 1)
            free_bank(S, dve, B_OUTN + j)
    dve.wait_ge(S.rms_std, DEPTH + 1)
    nc.vector.reciprocal(S.wk[3][:, :], S.wk[2][:, :])
    dve.drain()
    for j in range(KT):
        stt(out=seq(S.res, j), in0=seq(S.res, j), scalar=S.prmB[:, PB_FINAL + j:PB_FINAL + j + 1], in1=S.wk[3][:, :],
            op0=ALU.mult, op1=ALU.mult).then_inc(S.y_done, 1)


def prime(S, dve, sems):
    for n, sm in enumerate([sm for sm, times in sems for _ in range(times)]):
        S.nc.vector.memset(S.tick[:, n:n + 1], 0.0).then_inc(sm, 1)


def setup_sync(S, sp, T):
    for dst, src in ((S.con, T["con"]), (S.cos, T["cos"]), (S.sin, T["sin"]), (S.prmA, T["prm_a"]), (S.t, T["x"]), (S.cmask, T["cmask"])):
        sp.dma_start(dst[:, :], src).then_inc(S.con_landed, 16)


def setup_vector(S, dve):
    nc = S.nc
    prime(S, dve, [(b, 1) for b in S.bank_free] + [(S.stk_oev, 1), (S.merge_x, 2), (S.ffn_h, 2), (S.y_ready, 2),
                                                   (S.fox.out, 2), (S.dsa.out, 2), (S.nsa.out, 2)])
    nc.vector.memset(S.ones[:, :], 1.0 / D)
    nc.vector.memset(S.negones[:, :], -1.0)
    nc.vector.memset(S.eps[:, :], LN_EPS)
    nc.vector.memset(S.eps2[:, :], RMS_EPS)
    nc.vector.memset(S.halfpi[:, :], math.pi / 2)
    nc.vector.memset(S.tiny[:, :], 1e-30)
    dve.wait_ge(S.con_landed, 16 * 6)
    for dst, c in ((S.idb, C_ID), (S.causb, C_CAUS), (S.strictb, C_STRICT), (S.chunkb, C_CHUNK)):
        nc.vector.tensor_copy(dst[:, :], S.con[:, c:c + P])
    nc.vector.tensor_copy(S.xh[:, :], S.t[:, :])
    dve.drain()
    for k in range(KT):
        nc.vector.tensor_tensor(S.xl[:, k * SEQ:(k + 1) * SEQ], S.t[:, k * SEQ:(k + 1) * SEQ],
                                S.xh[:, k * SEQ:(k + 1) * SEQ].bitcast(F32), ALU.subtract).then_inc(S.x_ready, 1)


def program(nc, T, out):
    with ExitStack() as ctx:
        S = plan(nc, ctx)
        groups = T["w"].shape[0] // SLOTS
        block = ctx.enter_context(nc.Block())

        @block.sync
        def _(sp):
            setup_sync(S, sp, T)
            sp_stream(S, sp, T["w"], groups)
            for j in range(KT):
                sp.wait_ge(S.y_done, j + 1)
                sp.dma_start(out[:, j * SEQ:(j + 1) * SEQ], seq(S.res, j)).then_inc(S.out_done, 16)
            sp.wait_ge(S.out_done, 16 * KT)

        @block.gpsimd
        def _(pool):
            pool_split(S, pool, groups)

        @block.tensor
        def _(pe):
            a_tensor(S, pe)
            b_tensor(S, pe)

        @block.scalar
        def _(act):
            a_scalar(S, act, T["p"])
            b_scalar(S, act, T)

        @block.vector
        def _(dve):
            setup_vector(S, dve)
            a_vector(S, dve)
            b_vector(S, dve)


def feature_major(a):
    n, f = a.shape
    return np.ascontiguousarray(a.reshape(n, f // P, P).transpose(2, 1, 0).reshape(P, -1))


def unit_of(w):
    return w.reshape(KT, P, P).transpose(1, 0, 2).reshape(P, KT * P)


def units_of(w):
    return [unit_of(w[:, c:c + P]) for c in range(0, w.shape[1], P)]


def units_a(a, l):
    w = np.asarray(a["w_in"][l])
    sizes = (384, 384, 384, 6, 320, 320, 320, 320, 64, 64, 512, 64, 8, 3 * D)
    at = np.cumsum((0,) + sizes)
    fq, fk, fv, ff, sq, sk, sv, dq, dk, dv, iq, ik, iw, g = (w[:, at[n]:at[n + 1]] for n in range(14))
    zero = lambda n: np.zeros((D, n), w.dtype)
    cat = lambda *x: np.concatenate(x, axis=1)
    proj = cat(fv, sv[:, :256], sv[:, 256:], dv, fq, fk, sq[:, :256], sk[:, :256],
               ik, ff, zero(2), iw, zero(16), ff, zero(26), sq[:, 256:], dq[:, 256:], sk[:, 256:], dk, dk, ik,
               dq[:, :256], iq)
    up = np.concatenate([np.asarray(a[k][l]) for k in ("w_up_fox", "w_up_sb", "w_up_dsa")], axis=0)
    fin, fout = np.asarray(a["w_ff_in"][l]), np.asarray(a["w_ff_out"][l])
    ffn = [m for q in range(4) for m in units_of(fin[:, q * D:(q + 1) * D]) + units_of(fout[q * D:(q + 1) * D])]
    ple = np.asarray(a["w_ple"][l]).reshape(2, P, 2, 4, P).transpose(2, 1, 3, 0, 4).reshape(2, P, KT * P)
    all_ = (units_of(proj) + units_of(g) + units_of(up) + units_of(np.asarray(a["w_out"][l])) + list(ple) + ffn
            + units_of(np.asarray(a["w_ple_gate"][l])))
    assert len(all_) == A_UNITS
    return all_


def units_b(a, l):
    w = np.asarray(a["w_in_2"][l])
    sizes = (512, 128, 128, 128, 128, 128, 128, 24, 512, 512, 512, 512, 512, 512)
    at = np.cumsum((0,) + sizes)
    q, kc, vc, ks, vs, kw, vw, gl, zn, ul, zl, ga, gb, zc = (w[:, at[n]:at[n + 1]] for n in range(14))
    q = q.reshape(D, 2, B_REP, HD).transpose(0, 2, 1, 3).reshape(D, 512)
    gl = np.concatenate([gl, np.zeros((D, P - 24), w.dtype)], axis=1)
    plain = units_of(np.concatenate([ga, gb, ul, zl, zc, zn, q, kc, ks, kw, vc, vs, vw, gl], axis=1))
    bd = np.zeros((KT, P, P), w.dtype)
    for t in range(4):
        for d, name in enumerate(("lru_w_a_2", "lru_w_i_2")):
            for e in range(2):
                bd[2 * t + d, 64 * e:64 * e + 64, 64 * e:64 * e + 64] = np.asarray(a[name])[l, 2 * t + e]
    w1, w2 = np.asarray(a["cmp_w1_2"][l]), np.asarray(a["cmp_w2_2"][l])
    c1 = [unit_of(w1[kv, h * D:(h + 1) * D, m * P:(m + 1) * P]) for kv in range(2) for m in range(2) for h in range(2)]
    c2 = np.zeros((2, D, P), w.dtype)
    c2[0, 0:256] = np.concatenate([w2[0], w2[0]], axis=1)
    c2[1, 0:256, 0:HD] = w2[1]

    def pairs(m):
        return [np.concatenate([unit4(m[:, c + o * P:c + (o + 1) * P]) for o in range(2)], axis=1)
                for c in range(0, m.shape[1], 2 * P)]

    def unit4(m):
        return m.reshape(4, P, P).transpose(1, 0, 2).reshape(P, 4 * P)

    wo = np.asarray(a["w_out_2"][l])
    all_ = (plain + [bd.transpose(1, 0, 2).reshape(P, KT * P)] + c1 + [unit_of(c2[0]), unit_of(c2[1])]
            + pairs(np.asarray(a["conv_w_pw2_2"][l])) + pairs(wo[512:1024]) + pairs(wo[1024:]) + pairs(wo[:512]))
    assert len(all_) == B_UNITS
    return all_


def params_b(a):
    out = np.zeros((P, SEQ), np.float32)

    def tiles(v, n):
        return np.asarray(v).reshape(n, P).T

    for l in range(DEPTH):
        c = out[:, l * PB_N:(l + 1) * PB_N]
        c[:, PB_G:PB_G + KT] = tiles(a["norm_g_2"][l], KT)
        c[0:3 * B_HEADS, PB_BG] = np.asarray(a["b_gate_2"][l])
        for at, name in ((PB_BA, "lru_b_a_2"), (PB_BI, "lru_b_i_2"), (PB_LAM, "lru_lam_2"), (PB_LCB, "lru_conv_b_2"),
                         (PB_DWB, "conv_dw_b_2"), (PB_LNG, "conv_ln_g_2"), (PB_LNB, "conv_ln_b_2")):
            c[:, at:at + 4] = tiles(a[name][l], 4)
        c[:, PB_LCW:PB_LCW + 16] = np.asarray(a["lru_conv_w_2"][l]).reshape(LRU_K, 4, P).transpose(2, 1, 0).reshape(P, -1)
        c[:, PB_DW:PB_DW + 4 * CONV_K] = np.asarray(a["conv_dw_w_2"][l]).reshape(CONV_K, 4, P).transpose(2, 1, 0).reshape(P, -1)
        c[:, PB_POS:PB_POS + 32] = np.asarray(a["cmp_pos_2"][l]).reshape(32, P).T
    out[:, PB_FINAL:PB_FINAL + KT] = tiles(a["final_g_2"], KT)
    out[:, PB_INV] = np.tile(np.float32(10000.0) ** (-np.arange(0, HD, 2, dtype=np.float32) / np.float32(HD)), 4)
    return out


def cmp_mask():
    t = np.arange(P)[:, None, None] + P * np.arange(QB)[None, :, None]
    n = np.arange(32)[None, None, :]
    return np.where((16 * n + 31 <= t) & (n < NBLK), 0.0, NEG).astype(np.float32).reshape(P, QB * 32)


def constants():
    c = np.zeros((P, C_N), np.float32)
    i, j = np.arange(P)[:, None], np.arange(P)[None, :]
    c[:, C_ID:C_ID + P] = i == j
    half, same = HD // 2, i // HD == j // HD
    c[:, C_ROT:C_ROT + P] = np.where(same & (i == j + half), -1.0, np.where(same & (i == j - half), 1.0, 0.0))
    c[:, C_TRI:C_TRI + P] = np.where(i >= j, -1.0, 0.0)
    c[:, C_CAUS:C_CAUS + P] = np.where(j > i, NEG, 0.0)
    c[:, C_STRICT:C_STRICT + P] = np.where(i >= j, NEG, 0.0)
    c[:, C_ST01:C_ST01 + P] = i < j
    c[:, C_CHUNK:C_CHUNK + P] = np.where(j // 64 > i // 64, NEG, 0.0)
    for h in range(6):
        c[96 + h, C_QA + h] = 1.0
        c[64 + h, C_QB + h] = 1.0
    c[64:96, C_KA] = -1.0
    c[96:, C_KB] = 1.0
    return c


def rope_constants():
    inv = np.float32(10000.0) ** (-np.arange(32, dtype=np.float32) / np.float32(32))
    ang = (np.arange(SEQ, dtype=np.float32)[:, None] * inv[None, :]).astype(np.float32)
    rep = lambda t: np.ascontiguousarray(np.tile(t.T, (4, 1)).astype(np.float32))
    return rep(np.cos(ang)), rep(np.sin(ang))


def arrays_of(a):
    prm = np.zeros((P, DEPTH, PA_N), np.float32)
    for l in range(DEPTH):
        for c, name in ((PA_G1, "ln1_g"), (PA_B1, "ln1_b"), (PA_G2, "ln2_g"), (PA_B2, "ln2_b")):
            prm[:, l, c:c + KT] = np.asarray(a[name][l]).reshape(KT, P).T
        prm[64:70, l, PA_BF] = np.asarray(a["b_forget"][l])
        prm[96:102, l, PA_BF] = np.asarray(a["b_forget"][l])
    cos, sin = rope_constants()
    units = [u for l in range(DEPTH) for u in units_a(a, l)] + [u for l in range(DEPTH) for u in units_b(a, l)]
    units += [np.zeros((P, KT * P), np.float32)] * SLOTS
    return {
        "x": feature_major(np.asarray(a["x"])[0]),
        "p": np.stack([feature_major(np.asarray(a["p"])[l, 0]) for l in range(DEPTH)]),
        "w": np.stack(units), "con": constants(), "cos": cos, "sin": sin, "prm_a": prm.reshape(P, -1),
        "prm_b": params_b(a), "cmask": cmp_mask(), "pos": np.asarray(a["positions_2"]),
    }


def kernel(**inputs):
    import concourse.bacc as bacc
    from concourse.bass_utils import run_bass_kernel_spmd

    nc = bacc.Bacc("TRN2", target_bir_lowering=False, num_devices=1)
    arrays = arrays_of(inputs)
    T = {k: nc.dram_tensor(k, v.shape, mybir.dt.from_np(v.dtype), kind="ExternalInput").ap() for k, v in arrays.items()}
    out = nc.dram_tensor("out", (P, KT * SEQ), F32, kind="ExternalOutput").ap()
    program(nc, T, out)
    r = run_bass_kernel_spmd(nc, [arrays], core_ids=[0])
    y = np.asarray(r.results[0]["out"]).reshape(P, KT, SEQ)
    return np.ascontiguousarray(y.transpose(2, 1, 0).reshape(1, SEQ, D))
```

```python
from contextlib import ExitStack
import math

import numpy as np

import concourse.bass as bass
from concourse import mybir

F32 = mybir.dt.float32
F32R = mybir.dt.float32r
BF16 = mybir.dt.bfloat16
I32 = mybir.dt.int32
ALU = mybir.AluOpType
ACT = mybir.ActivationFunctionType
AX = mybir.AxisListType.X

P = 128
SEQ = 512
D = 1024
KT = D // P
QB = SEQ // P
HD = 64
SLOTS = 4
DEPTH = 2
NEG = -1e30
MARK = -3e38
ALPHA = (2 * DEPTH) ** 0.25
LN_EPS = 1e-5
TOPK = 128
IDX_HEADS = 8

A_FV, A_SV, A_SDV, A_FQ, A_FK, A_SQ, A_SK = 0, 3, 5, 6, 9, 12, 14
A_IKF, A_S4D4Q, A_S4KDK, A_DKIK, A_DQ, A_IQ = 16, 17, 18, 19, 20, 22
A_NPROJ = 26
A_GATE = A_NPROJ
A_UP = A_GATE + 3 * KT
A_OUT = A_UP + KT
A_PLE = A_OUT + KT
A_FFN = A_PLE + 2
A_PG = A_FFN + 64
A_UNITS = A_PG + KT
assert A_UNITS % SLOTS == 0
A_GROUPS = A_UNITS // SLOTS
A_VT = (0, 1, 2, 3, 4, 5, A_IKF)
A_NVT = len(A_VT)
ROPE_UNITS, FOX_UNITS, STK_UNITS = 0, 4, 16
ROPE_TILES = 20
V_FOX, V_SB, V_S4, V_DSA, V_IW = 0, 384, 640, 704, 6 * P + 72

C_ID, C_ROT, C_TRI, C_CAUS, C_STRICT, C_ST01, C_CHUNK = (P * n for n in range(7))
C_QA = 7 * P
C_QB = C_QA + 6
C_KA = C_QB + 6
C_KB = C_KA + 1
C_N = C_KB + 1

PA_G1, PA_B1, PA_G2, PA_B2, PA_BF, PA_N = 0, 8, 16, 24, 32, 33

B_GA, B_GB, B_U, B_KV, B_G, B_Q, B_ZL, B_ZC, B_ZN = 0, 4, 8, 12, 18, 19, 23, 27, 31
B_BD = 35
B_CMP1 = 36
B_CMP2 = 44
B_PW2 = 46
B_OUTL, B_OUTC, B_OUTN = 48, 52, 56
B_UNITS = 60
B_GROUPS = B_UNITS // SLOTS
B_HEADS, B_REP = 8, 4
CONV_K, LRU_K = 31, 4
UC_W, UP_W = CONV_K - 1 + SEQ, LRU_K - 1 + SEQ
NBLK = 31
NB2 = 2 * NBLK
RMS_EPS = 1e-6
PB_G, PB_BG, PB_BA, PB_BI, PB_LAM, PB_LCW, PB_LCB = 0, 8, 9, 13, 17, 21, 37
PB_DW, PB_DWB, PB_LNG, PB_LNB, PB_POS, PB_N = 41, 165, 169, 173, 177, 209
PB_FINAL, PB_INV = DEPTH * PB_N, DEPTH * PB_N + KT


class Plan:
    pass


def plan(nc, ctx):
    S = Plan()
    S.nc = nc
    base = -(-nc.sbuf_base // 64) * 64

    def at(name, shape, dt, kb):
        return nc.alloc_sbuf_tensor_at(name, shape, dt, offset=base + int(kb * 1024))

    W = KT * P
    WK = 187.75
    S.raw = [at(f"w_raw{s}", [P, W], F32, 4 * s) for s in range(SLOTS)]
    S.wh = [at(f"w_hi{s}", [P, W], F32R, 16 + 4 * s) for s in range(SLOTS)]
    S.wl = [at(f"w_lo{s}", [P, W], F32R, 32 + 4 * s) for s in range(SLOTS)]
    S.xh = at("x_hi", [P, KT * SEQ], F32R, 48)
    S.xl = at("x_lo", [P, KT * SEQ], F32R, 64)
    S.gates = at("gates", [P, 3 * KT * SEQ], F32, 80)
    S.ml = at("merged_lo", [P, KT * SEQ], F32R, 80)
    S.plep = at("ple_proj", [P, KT * SEQ], F32, 80)
    S.qkv = at("proj", [P, A_NPROJ * SEQ], F32, 96)
    S.t = at("ln_in", [P, KT * SEQ], F32, 96)
    S.yacc = at("ffn_sum", [P, KT * SEQ], F32, 96)
    S.praw = at("p_raw", [P, 2 * SEQ], F32, 112)
    S.ph = at("p_hi", [P, 2 * SEQ], F32R, 116)
    S.pl = at("p_lo", [P, 2 * SEQ], F32R, 120)
    S.r = [at(f"idx_relu{e}", [P, SEQ], F32, 96 + 2 * e) for e in range(2)]
    S.sacc = at("idx_sum", [P, 9 * P], F32, 100)
    S.nz = [at(f"neg_abs{e}", [P, n], F32, kb) for e, n, kb in ((0, 3 * P, WK + 16.5), (1, SEQ, 128))]
    S.score = at("idx_score", [P, 9 * P], F32, 140)
    S.dmask = at("sparse_mask", [P, 9 * P], BF16, 144.5)
    S.rh = at("rhs_hi", [P, KT * SEQ], F32R, 130)
    S.rl = at("rhs_lo", [P, KT * SEQ], F32R, 146)
    S.vt = at("v_tok", [P, QB * A_NVT * P], F32, 148)
    S.otok = at("o_tok", [P, QB * D], F32, 162)
    S.mh = at("merged_hi", [P, KT * SEQ], F32R, 162)
    S.cos = at("cos", [P, SEQ], F32, 178)
    S.sin = at("sin", [P, SEQ], F32, 180)
    S.con = at("constants", [P, C_N], F32, 182)
    S.ones = at("ones", [P, P], F32, 185.75)
    S.negones = at("neg_ones", [P, P], F32, 186.25)
    S.idb = at("ident_bf", [P, P], BF16, 186.75)
    S.causb = at("causal_bf", [P, P], BF16, 187)
    S.strictb = at("strict_bf", [P, P], BF16, 187.25)
    S.chunkb = at("chunk_bf", [P, P], BF16, 187.5)
    S.wk = [at(f"work{n}", [P, SEQ], F32, WK + 2 * n) for n in range(8)]
    S.sp = at("softplus_sum", [P, 11 * P], F32, WK + 6)
    S.stk_w = at("stick_weights", [P, 10 * P], F32, WK + 11.5)
    S.c = at("log_f_sum", [P, SEQ], F32, WK + 16)
    o = [(WK + 18) * 1024]

    def small(name, n, dt=F32):
        o[0] += 4 * n
        return nc.alloc_sbuf_tensor_at(name, [P, n], dt, offset=base + int(o[0] - 4 * n), align_bytes=4)

    S.prmA = small("params_a", DEPTH * PA_N)
    S.cur = small("params_cur", PA_N)
    S.nm = [small(f"neg_max{e}", 1) for e in range(4)]
    S.rs = [small(f"row_sum{e}", 1) for e in range(4)]
    S.rinv = [small(f"row_inv{e}", 1) for e in range(2)]
    S.top = [small(f"top8_{b}", 8) for b in range(3)]
    S.tick = small("tick", 32)
    S.eps = small("ln_eps", 1)
    S.res = at("residual", [P, KT * SEQ], F32, 80)
    S.q = at("b_q", [P, 4 * SEQ], F32, 96)
    S.kv = {n: at(f"b_{n}", [P, SEQ], F32, 104 + 2 * i) for i, n in enumerate(("kc", "ks", "kw", "vc", "vs", "vw", "gl"))}
    S.vbd = at("cmp_values", [P, 2 * 4 * HD], F32, 104)
    S.vtok = {"s": at("b_vs_tok", [P, SEQ], F32, 174.75), "w": at("b_vw_tok", [P, SEQ], F32, 112)}
    S.gate = at("b_gate_tok", [P, QB * 3 * B_HEADS], F32, 116)
    S.cmx, S.csum = (at(f"cmp_{n}", [P, QB * B_HEADS], F32, 116.5 + d) for n, d in (("max", 0), ("sum", 0.25)))
    S.mnh, S.mnl = at("nsa_hi", [P, 4 * SEQ], F32R, 96), at("nsa_lo", [P, 4 * SEQ], F32R, 104)
    S.zl, S.zc, S.zn = (at(f"silu_z_{n}", [P, 4 * SEQ], F32, 118 + 8 * i) for i, n in enumerate(("lru", "conv", "nsa")))
    S.uc = at("glu_out", [P, 4 * UC_W], F32, 142)
    S.ls = at("lru_tanh", [P, 4 * SEQ], F32, 142)
    S.ot2 = at("b_o_tok", [P, QB * 512], F32, 142)
    S.cacc = at("conv_sum", [P, 4 * SEQ], F32, 150.5)
    S.up = at("lru_in", [P, 4 * UP_W], F32, 158.5)
    S.la = at("lru_log_a", [P, 4 * SEQ], F32, 158.5)
    S.xc = at("lru_conv", [P, 4 * SEQ], F32, 166.75)
    S.xch, S.xcl = at("lru_conv_hi", [P, 4 * SEQ], F32R, 142), at("lru_conv_lo", [P, 4 * SEQ], F32R, 158.5)
    S.hkh, S.hkl = (at(f"cmp_hid_k_{n}", [P, 2 * NB2], F32R, 176.75 + d) for n, d in (("hi", 0), ("lo", 0.5)))
    S.kcb = at("cmp_keys", [P, HD], F32, 177.75)
    S.blk = [at(f"cmp_blocks_{n}", [P, 16 * NB2], F32, WK + 4 * i) for i, n in enumerate("kv")]
    S.lri, S.lrt = at("lru_i", [P, 4 * SEQ], F32, 48), at("lru_tmp", [P, 4 * SEQ], F32, 64)
    S.lnsq = [S.kv["vc"], S.kv["vw"]]
    S.hvh, S.hvl = (at(f"cmp_hid_v_{n}", [P, SEQ], F32R, WK + 2 * i) for i, n in ((1, "hi"), (2, "lo")))
    S.pos = at("positions", [P, SEQ], I32, WK + 8)
    S.prmB = at("params_b", [P, SEQ], F32, WK + 16)
    S.cmask = small("cmp_mask", QB * 32)
    S.curB = small("params_b_cur", PB_N)
    S.lam = [small(f"lam{n}", 4) for n in range(5)]
    S.rg = [small(f"gate_inv{e}", 1) for e in range(2)]
    S.eps2, S.halfpi, S.tiny = small("rms_eps", 1), small("half_pi", 1), small("tiny", 1)

    S.ps = [nc.alloc_psum_tensor(f"bank{n}", [P, SEQ], F32) for n in range(8)]
    S.X = S.ps[4:]

    def sem(name):
        return ctx.enter_context(nc.semaphore(name))

    def ring(name):
        return [sem(f"{name}{s}") for s in range(SLOTS)]

    S.raw_landed, S.hi_ready, S.lo_ready = ring("raw_landed"), ring("hi_ready"), ring("lo_ready")
    S.unit_done, S.bank_free = ring("unit_done"), ring("bank_free")
    S.sem = sem
    S.con_landed = sem("con_landed")
    S.x_ready = sem("x_ready")
    S.scaled = sem("scaled")
    S.rot_ready = sem("rot_ready")
    S.rope_done = sem("rope_done")
    S.vt_ready = sem("vt_ready")
    S.vt_done = sem("vt_done")
    S.logf_in = sem("logf_in")
    S.logf_out = sem("logf_out")
    S.idx_ready = sem("idx_ready")
    S.relu_done = sem("relu_done")
    S.idx_acc = sem("idx_acc")
    S.mask_ready = sem("mask_ready")
    S.fox_staged = sem("fox_staged")
    S.fox_aug = sem("fox_aug")
    S.s_staged = sem("s_staged")
    S.d_staged = sem("d_staged")
    S.stk_z = sem("stk_z")
    S.stk_na = sem("stk_na")
    S.stk_ln = sem("stk_ln")
    S.stk_sp = sem("stk_sp")
    S.stk_c = sem("stk_c")
    S.stk_a = sem("stk_a")
    S.stk_o = sem("stk_o")
    S.stk_oev = sem("stk_oev")
    S.ot_ready = sem("ot_ready")
    S.ot_hi = sem("ot_hi")
    S.ot_done = sem("ot_done")
    S.merge_x = sem("merge_x")
    S.merge_done = sem("merge_done")
    S.t_ready = sem("t_ready")
    S.ln_mean = sem("ln_mean")
    S.ln_d = sem("ln_d")
    S.ln_sq = sem("ln_sq")
    S.ln_var = sem("ln_var")
    S.ln_std = sem("ln_std")
    S.ln_y = sem("ln_y")
    S.ln_hi = sem("ln_hi")
    S.ffn_act = sem("ffn_act")
    S.ffn_h = sem("ffn_h")
    S.p_landed = sem("p_landed")
    S.p_ready = sem("p_ready")
    S.y_ready = sem("y_ready")
    S.out_done = sem("out_done")
    S.pb_landed = sem("pb_landed")
    S.ang_ready = sem("ang_ready")
    S.tab_ready = sem("tab_ready")
    S.res_ready = sem("res_ready")
    S.rms_sq = sem("rms_sq")
    S.rms_var = sem("rms_var")
    S.rms_std = sem("rms_std")
    S.rms_y = sem("rms_y")
    S.rms_hi = sem("rms_hi")
    S.lam_in = sem("lam_in")
    S.lam_out = sem("lam_out")
    S.glu_done = sem("glu_done")
    S.bvt_ready = sem("bvt_ready")
    S.bvt_done = sem("bvt_done")
    S.gl_done = sem("gl_done")
    S.gate_tanh = sem("gate_tanh")
    S.q0_zero = sem("q0_zero")
    S.b_rot_ready = sem("b_rot_ready")
    S.b_rope_done = sem("b_rope_done")
    S.xc_split = sem("xc_split")
    S.lru_ready = sem("lru_ready")
    S.lru_gate = sem("lru_gate")
    S.nla_ready = sem("nla_ready")
    S.a_ready = sem("a_ready")
    S.b2_ready = sem("b2_ready")
    S.beta_ready = sem("beta_ready")
    S.lru_scanned, S.lru_done = sem("lru_scanned"), sem("lru_done")
    S.blk_raw = [sem(f"blk_raw_{n}") for n in "kv"]
    S.blk_ready = sem("blk_ready")
    S.hid_act = sem("hid_act")
    S.hid_turned = sem("hid_turned")
    S.hid_split = sem("hid_split")
    S.kcb_ready = sem("kcb_ready")
    S.vbd_ready = sem("vbd_ready")
    S.cs_ready = sem("cs_ready")
    S.cexp_in = sem("cexp_in")
    S.cexp_out = sem("cexp_out")
    S.cp_ready = sem("cp_ready")
    S.cpt_ready = sem("cpt_ready")
    S.cpt_copied = sem("cpt_copied")
    S.oc_ready = sem("oc_ready")
    S.oc_done = sem("oc_done")
    S.dw_done, S.xc_hi = sem("dw_done"), sem("xc_hi")
    S.cl_mean = sem("cl_mean")
    S.cl_d = sem("cl_d")
    S.cl_sq = sem("cl_sq")
    S.cl_var = sem("cl_var")
    S.cl_std = sem("cl_std")
    S.cl_y = sem("cl_y")
    S.cl_hi = sem("cl_hi")
    S.un_ready = sem("un_ready")
    S.first_out, S.first_added = sem("first_out"), sem("first_added")
    S.mc_y = sem("mc_y")
    S.mc_hi = sem("mc_hi")
    S.mc_ready = sem("mc_ready")
    S.q_staged = sem("q_staged")
    S.q_zero = sem("q_zero")
    S.bt_ready = sem("bt_ready")
    S.mn_y = sem("mn_y")
    S.mn_hi = sem("mn_hi")
    S.mn_ready = sem("mn_ready")
    S.y_done = sem("y_done")
    S.nsa = SoftmaxSems(sem, "nsa")
    S.fox = SoftmaxSems(sem, "fox")
    S.dsa = SoftmaxSems(sem, "dsa")
    return S


class SoftmaxSems:

    def __init__(self, sem, stage):
        self.s = sem(f"{stage}_scores")
        self.max = sem(f"{stage}_max")
        self.p = sem(f"{stage}_probs")
        self.pt = sem(f"{stage}_turned")
        self.ptc = [sem(f"{stage}_turned_copied_{n}") for n in ("even", "odd")]
        self.o = sem(f"{stage}_out_ready")
        self.out = sem(f"{stage}_out_used")


class Step:

    def __init__(self, b, qk, v, norm, scale=None, ready=()):
        self.b = b
        self.ready = ready
        self.qk = qk
        self.v = v
        self.norm = norm
        self.scale = scale


def cols(t, j, n=SEQ, w=None):
    w = n if w is None else w
    return t[:, j * n:j * n + w] if isinstance(j, int) else t[:, bass.ds(j * n, w)]


def pe_unit(S, pe, u, g, out, rh, rl, ready=None, n0=0):
    s = u % SLOTS
    pe.wait_ge(S.lo_ready[s], g + 1)
    pe.wait_ge(S.bank_free[s], g + 1)
    for k in range(KT):
        if ready:
            pe.wait_ge(ready, n0 + k + 1)
        pe_tile(S, s, k, out, rh, rl, k, k == 0, k == KT - 1)
    return S.last


def pe_tile(S, s, w, out, rh, rl, k, first, last, lo=0, hi=P):
    nc = S.nc
    wh, wl = (t[s][lo:hi, w * P:(w + 1) * P] for t in (S.wh, S.wl))
    xh, xl = (t[lo:hi, k * SEQ:(k + 1) * SEQ] if isinstance(k, int) else t[lo:hi, bass.ds(k * SEQ, SEQ)] for t in (rh, rl))
    nc.tensor.matmul(out, wh, xh, start=first, stop=False)
    nc.tensor.matmul(out, wh, xl, start=False, stop=False)
    S.last = nc.tensor.matmul(out, wl, xh, start=False, stop=last)


def act_split(S, act, u, g):
    s = u % SLOTS
    act.wait_ge(S.raw_landed[s], 16 * (g + 2))
    S.nc.scalar.activation(S.wh[s][:, :], S.raw[s][:, :], ACT.Copy).then_inc(S.hi_ready[s], 1)


def sp_stream(S, sp, w_dram, groups):
    for s in range(SLOTS):
        sp.dma_start(S.raw[s][:, :], w_dram[s]).then_inc(S.raw_landed[s], 16)
    with sp.Fori(1, groups) as g:
        for s in range(SLOTS):
            sp.wait_ge(S.lo_ready[s], g)
            src = w_dram[bass.ds(g * SLOTS + s, 1), :, :].rearrange("a p n -> (a p) n")
            sp.dma_start(S.raw[s][:, :], src).then_inc(S.raw_landed[s], 16)


def pool_split(S, pool, s, g):
    pool.wait_ge(S.hi_ready[s], g + 1)
    S.nc.gpsimd.tensor_tensor(S.wl[s][:, :], S.raw[s][:, :], S.wh[s][:, :].bitcast(F32), ALU.subtract).then_inc(S.lo_ready[s], 1)


def pool_program(S, pool):
    nc = S.nc

    def splits(n, first):
        with pool.Fori(0, n) as g:
            for s in range(SLOTS):
                pool_split(S, pool, s, first + g)

    splits(DEPTH * A_GROUPS, 0)
    with pool.Fori(0, DEPTH) as L:
        gates = -(-B_BD // SLOTS)
        splits(gates, GB(L, 0))
        pool.wait_ge(S.xc_hi, L + 1)
        nc.gpsimd.tensor_tensor(S.xcl[:, :], S.xc[:, :], S.xch[:, :].bitcast(F32), ALU.subtract).then_inc(S.xc_split, 1)
        last = B_OUTL // SLOTS
        splits(last - gates, GB(L, gates * SLOTS))
        x4h, x4l = S.xh[:, 0:4 * SEQ], S.xl[:, 0:4 * SEQ]
        pool.wait_ge(S.lru_scanned, L + 1)
        nc.gpsimd.tensor_tensor(x4h, S.lrt[:, :], S.zl[:, :], ALU.mult)
        nc.gpsimd.tensor_tensor(S.la[:, :], S.lrt[:, :], S.zl[:, :], ALU.mult)
        pool.drain()
        nc.gpsimd.tensor_tensor(x4l, S.la[:, :], x4h.bitcast(F32), ALU.subtract).then_inc(S.lru_done, 1)
        splits(1, GB(L, B_OUTL))
        for t in range(4):
            pool.wait_ge(S.mc_hi, L * 4 + t + 1)
            nc.gpsimd.tensor_tensor(seq(S.xl, 4 + t), seq(S.zc, t), seq(S.xh, 4 + t).bitcast(F32), ALU.subtract).then_inc(S.mc_ready, 1)
        splits(B_GROUPS - last - 1, GB(L, B_OUTC))
    for s in range(SLOTS):
        pool_split(S, pool, s, DEPTH * (A_GROUPS + B_GROUPS))




def turned(S, n):
    return (S.X[2], S.ps[2])[n % 2]


def out_of(S, n):
    return (S.X[3], S.ps[3])[n % 2][:, 0:HD]


def attn_pe(S, pe, Z, n0, steps, ident, fill=None):
    nc = S.nc
    N = len(steps)

    def scores(n):
        if n >= 2:
            pe.wait_ge(Z.p, n0 + n - 1)
        for sem, count in steps[n].ready:
            pe.wait_ge(sem, count)
        for i, (lhsT, rhs, c, w) in enumerate(steps[n].qk):
            m = nc.tensor.matmul(S.X[n % 2][:, c:c + w], lhsT, rhs, start=(i == 0), stop=(i == len(steps[n].qk) - 1),
                                 skip_group_check=True)
        m.then_inc(Z.s, 1)

    def turn(n):
        pe.wait_ge(Z.p, n0 + n + 1)
        if n >= 2:
            pe.wait_ge(Z.ptc[n % 2], n0 + n // 2 * 2)
        o = turned(S, n)
        for k in range(steps[n].b + 1):
            m = nc.tensor.transpose(o[:, k * P:(k + 1) * P], S.wk[4 + n % 2][:, k * P:(k + 1) * P], ident)
        m.then_inc(Z.pt, 1)

    scores(0)
    scores(1)
    turn(0)
    for n in range(N):
        if n + 2 < N:
            scores(n + 2)
        if fill:
            fill(n, 0)
        if n + 1 < N:
            turn(n + 1)
        if fill:
            fill(n, 1)
        pe.wait_ge(Z.ptc[n % 2], n0 + n // 2 * 2 + 2)
        pe.wait_ge(Z.out, n0 + n + 1)
        b = steps[n].b
        for k in range(b + 1):
            m = nc.tensor.matmul(out_of(S, n), S.wk[6 + n % 2][:, k * P:(k + 1) * P], steps[n].v(k),
                                 start=(k == 0), stop=(k == b))
        m.then_inc(Z.o, 1)


def attn_copy_turned(S, Z, eng, op, n0, n, steps):
    eng.wait_ge(Z.pt, n0 + n + 1)
    if n >= 2:
        eng.wait_ge(Z.o, n0 + n - 1)
    w = (steps[n].b + 1) * P
    op(S.wk[6 + n % 2][:, 0:w], turned(S, n)[:, 0:w]).then_inc(Z.ptc[n % 2], 2)


def attn_act(S, act, Z, n0, steps, after=None):
    nc = S.nc
    N = len(steps)

    def exps(n):
        act.wait_ge(Z.max, n0 + n + 1)
        if n >= 2:
            act.wait_ge(Z.pt, n0 + n - 1)
            act.wait_ge(Z.out, n0 + n - 1)
        w = (steps[n].b + 1) * P
        nc.scalar.activation(S.wk[4 + n % 2][:, 0:w], S.X[n % 2][:, 0:w], ACT.Exp, bias=S.nm[n % 4][:, :],
                             accum_out=S.rs[n % 4][:, :]).then_inc(Z.p, 1)

    exps(0)
    exps(1)
    for n in range(N):
        if n % 2:
            attn_copy_turned(S, Z, act, lambda o, i: nc.scalar.activation(o, i, ACT.Copy), n0, n, steps)
        if n + 2 < N:
            exps(n + 2)
        if after:
            after(n)


def attn_dve(S, dve, Z, n0, steps, after=None):
    nc = S.nc
    N = len(steps)

    def rowmax(n):
        dve.wait_ge(Z.s, n0 + n + 1)
        w = (steps[n].b + 1) * P
        nc.vector.tensor_reduce(S.nm[n % 4][:, :], S.X[n % 2][:, 0:w], AX, ALU.max, negate=True).then_inc(Z.max, 1)

    def store(n):
        nc.vector.reciprocal(S.rinv[n % 2][:, :], S.rs[n % 4][:, :])
        dve.drain()
        if steps[n].scale:
            steps[n].scale(n)
            dve.drain()
        dve.wait_ge(Z.o, n0 + n + 1)
        steps[n].norm(n)

    rowmax(0)
    rowmax(1)
    for n in range(N):
        if n % 2 == 0:
            attn_copy_turned(S, Z, dve, nc.vector.tensor_copy, n0, n, steps)
        if n + 2 < N:
            rowmax(n + 2)
        if n >= 1:
            store(n - 1)
        if after:
            after(n)
    store(N - 1)


def fox_steps(S, L, i):
    steps = []
    for e in range(2):
        staged = ((S.fox_staged, L * 14 + i * 4 + 2 * e + 2), (S.fox_aug, L * 7 + i * 2 + e + 1))
        for b in range(QB):
            w = (b + 1) * P
            qk = [(S.wk[e][:, b * P:w], S.wk[2 + e][:, 0:w], 0, w), (S.idb[:, :], S.causb[:, :], b * P, P)]

            def v(k, e=e):
                return cols2(S.vt, k * A_NVT * P + V_FOX + e * HD, i, 2 * HD, HD)

            def norm(n, b=b, e=e):
                S.nc.vector.tensor_scalar(cols2(S.otok, b * D + e * HD, i, 2 * HD, HD), out_of(S, n),
                                          S.rinv[n % 2][:, :], None, ALU.mult).then_inc(S.fox.out, 1)
            steps.append(Step(b, qk, v, norm, ready=() if b else staged))
    return steps


def cols2(t, c0, i, stride, w):
    return t[:, c0 + i * stride:c0 + i * stride + w] if isinstance(i, int) else t[:, bass.ds(i * stride + c0, w)]


def dsa_steps(S, heads):
    steps = []
    for h0, i, q, k in heads:
        for b in range(QB):
            w = (b + 1) * P
            qk = [(q[:, b * P:w], k[:, 0:w], 0, w)]
            if b == 0:
                qk.append((S.idb[:, :], S.chunkb[:, :], 0, P))
            else:
                m0 = (b * (b + 1) // 2 - 1) * P
                qk.append((S.idb[:, :], S.dmask[:, m0:m0 + w], 0, w))

            def v(kt):
                return S.vt[:, kt * A_NVT * P + V_DSA:kt * A_NVT * P + V_DSA + HD]

            def norm(n, b=b, h0=h0, i=i):
                S.nc.vector.tensor_scalar(cols2(S.otok, b * D + (11 + h0) * HD, i, 2 * HD, HD), out_of(S, n),
                                          S.rinv[n % 2][:, :], None, ALU.mult).then_inc(S.dsa.out, 1)
            steps.append(Step(b, qk, v, norm))
    return steps


def tile_rows(S, u, half):
    return S.qkv[64 * half:64 * half + 64, u * SEQ:(u + 1) * SEQ]


def dsa_pair(S, i):
    return dsa_steps(S, [(0, i, S.wk[0], seq(S.qkv, A_DKIK)), (1, i, S.wk[1], seq(S.qkv, A_S4KDK))])


def dsa_last(S):
    return dsa_steps(S, [(4, 0, tile_rows(S, A_S4D4Q, 1), tile_rows(S, A_S4KDK, 1))])


SB0 = [0, 4 * P, 7 * P, 9 * P]


def sp_col(i, e):
    return SB0[i] + (e % 2) * P if i == QB - 1 else SB0[i]


def stk_bank(S, m):
    return (S.X[0], S.X[1], S.X[3], S.ps[2])[m % QB]


def stk_pe(S, pe, n0, h0, heads, fill=None):
    nc = S.nc
    N = len(heads) * QB

    def z(m):
        e, n = divmod(m, QB)
        q, k, _ = heads[e]
        i = QB - 1 - n
        if m >= QB:
            pe.wait_ge(S.stk_a, n0 + m - QB + 1)
        nc.tensor.matmul(stk_bank(S, m)[:, 0:SEQ - i * P], k[:, i * P:(i + 1) * P], q[:, i * P:SEQ], start=True, stop=True,
                         skip_group_check=True).then_inc(S.stk_z, 1)

    def values(e):
        pe.wait_ge(S.stk_a, n0 + (e + 1) * QB)
        pe.wait_ge(S.stk_oev, h0 + e + 1)
        for b in range(QB):
            for kt in range(b + 1):
                c = SB0[kt] + (b - kt) * P
                m = nc.tensor.matmul(S.X[2][:, b * HD:(b + 1) * HD], S.stk_w[:, c:c + P], heads[e][2](kt),
                                     start=(kt == 0), stop=(kt == b), skip_group_check=True)
        m.then_inc(S.stk_o, 1)

    z(0)
    z(1)
    for m in range(N):
        e, n = divmod(m, QB)
        i = QB - 1 - n
        w = SEQ - i * P
        bank = stk_bank(S, m)
        if m + 2 < N:
            z(m + 2)
        if fill:
            fill(m)
        if n == 0 and e > 0:
            values(e - 1)
        pe.wait_ge(S.stk_sp, n0 + m + 1)
        nc.tensor.matmul(bank[:, 0:w], S.con[:, C_TRI:C_TRI + P], S.sp[:, sp_col(i, e):sp_col(i, e) + w], start=False,
                         stop=False, skip_group_check=True)
        for j in range(i + 1, QB):
            wj = SEQ - j * P
            nc.tensor.matmul(bank[:, w - wj:w], S.negones[:, :], S.sp[:, sp_col(j, e):sp_col(j, e) + wj], start=False,
                             stop=False, skip_group_check=True)
        nc.tensor.matmul(bank[:, 0:P], S.idb[:, :], S.strictb[:, :], start=False, stop=True,
                         skip_group_check=True).then_inc(S.stk_c, 1)
    values(len(heads) - 1)


def stk_act(S, act, n0, heads, after=None):
    nc = S.nc
    N = heads * QB
    width = lambda m: (m % QB + 1) * P

    def log(m):
        t = S.nz[m % 2][:, 0:width(m)]
        act.wait_ge(S.stk_na, n0 + m + 1)
        nc.scalar.activation(t, t, ACT.Exp)
        act.drain()
        nc.scalar.activation(t, t, ACT.Ln, bias=1.0).then_inc(S.stk_ln, 1)

    log(0)
    for m in range(N):
        if m + 1 < N:
            log(m + 1)
        act.wait_ge(S.stk_c, n0 + m + 1)
        c = SB0[QB - 1 - m % QB]
        nc.scalar.activation(S.stk_w[:, c:c + width(m)], stk_bank(S, m)[:, 0:width(m)], ACT.Exp).then_inc(S.stk_a, 1)
        if after:
            after(m)


def stk_dve(S, dve, n0, h0, outs, between=None):
    nc = S.nc
    N = len(outs) * QB

    def output(e):
        dve.wait_ge(S.stk_o, h0 + e + 1)
        nc.vector.tensor_copy(outs[e], S.X[2][:, 0:QB * HD].rearrange("p (b d) -> p b d", b=QB)).then_inc(S.stk_oev, 1)

    def step(m):
        e, n = divmod(m, QB)
        i = QB - 1 - n
        w = SEQ - i * P
        return e, n, S.nz[m % 2][:, 0:w], S.sp[:, sp_col(i, e):sp_col(i, e) + w], stk_bank(S, m)[:, 0:w]

    def parts(m):
        e, n, t, sp, z = step(m)
        dve.wait_ge(S.stk_z, n0 + m + 1)
        if n == 1 and e > 0:
            dve.wait_ge(S.stk_c, n0 + m - 1)
        nc.vector.tensor_scalar(sp, z, 0.0, None, ALU.max)
        dve.drain()
        nc.vector.scalar_tensor_tensor(out=t, in0=sp, scalar=-2.0, in1=z, op0=ALU.mult, op1=ALU.add).then_inc(S.stk_na, 1)

    def softplus(m):
        _, _, t, sp, _ = step(m)
        dve.wait_ge(S.stk_ln, n0 + m + 1)
        nc.vector.tensor_tensor(sp, sp, t, ALU.add)
        dve.drain()
        nc.vector.tensor_tensor(sp[:, 0:P], sp[:, 0:P], S.con[:, C_ST01:C_ST01 + P], ALU.mult).then_inc(S.stk_sp, 1)

    parts(0)
    for m in range(N):
        e, n = divmod(m, QB)
        if m + 1 < N and n > 0:
            parts(m + 1)
        if between:
            between(m)
        softplus(m)
        if m + 1 < N and n == 0:
            parts(m + 1)
        if n == 0 and e > 0:
            output(e - 1)
    output(len(outs) - 1)


def otok_head(S, h0, i):
    v = S.otok[:, :].rearrange("p (b d) -> p b d", b=QB)
    c = h0 * HD
    return v[:, :, c:c + HD] if isinstance(i, int) else v[:, :, bass.ds(i * 2 * HD + c, HD)]


def stk_v(S, col, i):
    return lambda kt: cols2(S.vt, kt * A_NVT * P + col, i, 2 * HD, HD)


def ln_mean_pe(S, pe, n0, t_sem, t0, t, i, unit):
    def mean(j):
        pe.wait_ge(t_sem, t0 + j + 1)
        return S.nc.tensor.matmul(S.X[0][:, :], S.ones[:, :], seq(t, j), start=(j == 0), stop=(j == KT - 1))

    for j in range(SLOTS):
        unit(j)
        if 4 * i + j >= 1:
            mean(4 * i + j - 1)
    if i == 1:
        mean(KT - 1).then_inc(S.ln_mean, 1)


def ln_pe(S, pe, n0):
    for j in range(KT):
        pe.wait_ge(S.ln_sq, n0 * KT + j + 1)
        S.nc.tensor.matmul(S.X[1][:, :], S.ones[:, :], S.wk[j % 2][:, :], start=(j == 0),
                           stop=(j == KT - 1)).then_inc(S.ln_var, 1)


def ln_act(S, act, n0, t, g, b, between=None):
    nc = S.nc
    for j in range(KT):
        act.wait_ge(S.ln_d, n0 * KT + j + 1)
        if j >= 2:
            act.wait_ge(S.ln_var, n0 * KT + j - 1)
        nc.scalar.activation(S.wk[j % 2][:, :], t[:, j * SEQ:(j + 1) * SEQ], ACT.Square).then_inc(S.ln_sq, 1)
    act.wait_ge(S.ln_var, n0 * KT + KT)
    nc.scalar.activation(S.wk[2][:, :], S.X[1][:, :], ACT.Sqrt, bias=S.eps[:, :]).then_inc(S.ln_std, 1)
    for j in range(KT):
        act.wait_ge(S.ln_y, n0 * KT + j + 1)
        for o in (seq(S.xh, j), S.wk[4 + j % 4][:, :]):
            m = nc.scalar.activation(o, seq(t, j), ACT.Identity, scale=S.cur[:, g + j:g + j + 1], bias=S.cur[:, b + j:b + j + 1])
        m.then_inc(S.ln_hi, 1)
        if between and j == 1:
            between()


def ln_dve(S, dve, n0, t):
    nc = S.nc
    tiles = [t[:, j * SEQ:(j + 1) * SEQ] for j in range(KT)]
    dve.wait_ge(S.ln_mean, n0 + 1)
    for j in range(KT):
        nc.vector.tensor_tensor(tiles[j], tiles[j], S.X[0][:, :], ALU.subtract).then_inc(S.ln_d, 1)
    dve.wait_ge(S.ln_std, n0 + 1)
    nc.vector.reciprocal(S.wk[3][:, :], S.wk[2][:, :])
    dve.drain()
    for j in range(KT + 2):
        if j < KT:
            nc.vector.tensor_tensor(tiles[j], tiles[j], S.wk[3][:, :], ALU.mult).then_inc(S.ln_y, 1)
        if j >= 2:
            q = j - 2
            dve.wait_ge(S.ln_hi, n0 * KT + q + 1)
            nc.vector.tensor_tensor(seq(S.xl, q), S.wk[4 + q % 4][:, :], seq(S.xh, q).bitcast(F32),
                                    ALU.subtract).then_inc(S.x_ready, 1)


ROPE = [(A_IKF, 0, 64), (A_S4D4Q, 64, 128), (A_S4KDK, 64, 128)] + [(u, 0, P) for u in range(A_DKIK, A_NPROJ)]


def idx_steps():
    return [(b, h) for b in range(1, QB) for h in range(IDX_HEADS)]


def GA(L, u, i=0):
    return L * A_GROUPS + u // SLOTS + i


def gate_fill(S, pe, L, i, first, tiles):
    for x in tiles:
        j, k = divmod(x, KT)
        u = A_GATE + first + j
        s = u % SLOTS
        if k == 0:
            pe.wait_ge(S.lo_ready[s], GA(L, u, i) + 1)
            pe.wait_ge(S.bank_free[(u - 2) % SLOTS], GA(L, u - 2, i) + 2)
        pe_tile(S, s, k, S.ps[u % 2][:, :], S.xh, S.xl, k, k == 0, k == KT - 1)
        if k == KT - 1:
            S.last.then_inc(S.unit_done[s], 1)


SC0 = [None, 0, 2 * P, 5 * P]


def a_tensor(S, pe):
    nc = S.nc
    ident = S.con[:, C_ID:C_ID + P]
    with pe.Fori(0, DEPTH) as L:
        G = lambda u, i=0: L * A_GROUPS + u // SLOTS + i
        with pe.Fori(0, 6) as i:
            for u in range(SLOTS):
                pe_unit(S, pe, u, G(u, i), S.ps[u][:, :], S.xh, S.xl,
                        None if u else S.x_ready, L * 2 * KT).then_inc(S.unit_done[u], 1)
        for u in (24, 25):
            pe_unit(S, pe, u, G(u), S.ps[u % SLOTS][:, :], S.xh, S.xl).then_inc(S.unit_done[u % SLOTS], 1)
        pe.wait_ge(S.bank_free[25 % SLOTS], G(25) + 2)
        for v in range(A_NVT):
            if v >= 2:
                pe.wait_ge(S.vt_done, L * A_NVT + v - 1)
            for t in range(QB):
                m = nc.tensor.transpose(S.X[2 + v % 2][:, t * P:(t + 1) * P],
                                        S.qkv[:, A_VT[v] * SEQ + t * P:A_VT[v] * SEQ + (t + 1) * P], ident)
            m.then_inc(S.vt_ready, 1)
        pe.wait_ge(S.scaled, L + 1)
        for n, (u, _, _) in enumerate(ROPE):
            if n >= 2:
                pe.wait_ge(S.rope_done, L * len(ROPE) + n - 1)
            nc.tensor.matmul(S.X[n % 2][:, :], S.con[:, C_ROT:C_ROT + P], S.qkv[:, u * SEQ:(u + 1) * SEQ],
                             start=True, stop=True).then_inc(S.rot_ready, 1)
            gate_fill(S, pe, L, 0, ROPE_UNITS, range(ROPE_TILES * n // len(ROPE), ROPE_TILES * (n + 1) // len(ROPE)))
        pe.wait_ge(S.vt_done, (L + 1) * A_NVT)
        pe.wait_ge(S.rope_done, (L + 1) * len(ROPE))
        for n, (b, h) in enumerate(idx_steps()):
            if n >= 4:
                pe.wait_ge(S.relu_done, L * 24 + n - 3)
            k = tile_rows(S, A_IKF, 0) if h % 2 == 0 else tile_rows(S, A_DKIK, 1)
            q = tile_rows(S, A_IQ + h // 2, h % 2)
            w = (b + 1) * P
            nc.tensor.matmul(S.X[n % 4][:, 0:w], q[:, b * P:w], k[:, 0:w], start=True,
                             stop=True).then_inc(S.idx_ready, 1)
            if n % 2 == 0:
                gate_fill(S, pe, L, 0, ROPE_UNITS, [ROPE_TILES + n // 2])
        with pe.Fori(0, 3) as i:
            pe.wait_ge(S.relu_done, (L + 1) * 24)
            attn_pe(S, pe, S.fox, (L * 3 + i) * 8, fox_steps(S, L, i), ident,
                    lambda n, half: gate_fill(S, pe, L, i, FOX_UNITS, range(4 * n + 2 * half, 4 * n + 2 * half + 2)))
        with pe.Fori(0, 2) as i:
            pe.wait_ge(S.fox.out, (L + 1) * 24 + 2)
            pe.wait_ge(S.q0_zero, L + 1)
            pe.wait_ge(S.s_staged, (L * 2 + i) * 3 + 3)
            stk_pe(S, pe, (L * 5 + i * 2) * QB, L * 5 + i * 2,
                   [(S.wk[e], S.wk[2], stk_v(S, V_SB + e * HD, i)) for e in range(2)],
                   lambda m: gate_fill(S, pe, L, i, STK_UNITS, range(4 * m, 4 * m + 4)))
        stk_pe(S, pe, (L * 5 + 4) * QB, L * 5 + 4,
               [(tile_rows(S, A_S4D4Q, 0), tile_rows(S, A_S4KDK, 0), stk_v(S, V_S4, 0))])
        with pe.Fori(0, 2) as i:
            pe.wait_ge(S.stk_oev, L * 5 + 6)
            pe.wait_ge(S.mask_ready, L + 1)
            pe.wait_ge(S.d_staged, (L * 2 + i) * 2 + 2)
            attn_pe(S, pe, S.dsa, L * 20 + i * 8, dsa_pair(S, i), ident)
        attn_pe(S, pe, S.dsa, L * 20 + 16, dsa_last(S), ident)
        pe.wait_ge(S.dsa.out, (L + 1) * 20 + 2)
        for k in range(KT):
            if k >= 4:
                pe.wait_ge(S.ot_done, L * KT + k - 3)
            for b in range(QB):
                m = nc.tensor.transpose(S.X[k % 4][:, b * P:(b + 1) * P],
                                        S.otok[:, b * D + k * P:b * D + (k + 1) * P], ident)
            m.then_inc(S.ot_ready, 1)
        with pe.Fori(0, 2) as i:
            pe.wait_ge(S.ot_done, (L + 1) * KT)
            for jj in range(4):
                u = A_UP + jj
                s = u % SLOTS
                pe.wait_ge(S.lo_ready[s], G(u, i) + 1)
                pe.wait_ge(S.bank_free[s], G(u, i) + 1)
                pe.wait_ge(S.merge_x, L * KT + i * 4 + jj + 1)
                XS, XD = S.X[2 * (jj % 2)][:, :], S.X[2 * (jj % 2) + 1][:, :]
                for k in range(3):
                    pe_tile(S, s, k, S.ps[s][:, :], S.rh, S.rl, k, k == 0, k == 2)
                pe_tile(S, s, 3, XS, S.rh, S.rl, 3, True, False)
                pe_tile(S, s, 4, XS, S.rh, S.rl, 4, False, False)
                pe_tile(S, s, 5, XS, S.rh, S.rl, 5, False, True, 0, 64)
                pe_tile(S, s, 6, XD, S.rh, S.rl, 6, True, False)
                pe_tile(S, s, 5, XD, S.rh, S.rl, 5, False, False, 64, 128)
                pe_tile(S, s, 7, XD, S.rh, S.rl, 7, False, True)
                S.last.then_inc(S.unit_done[s], 1)
        for i in range(2):
            ln_mean_pe(S, pe, L * 2, S.t_ready, L * KT, S.t, i,
                       lambda j: pe_unit(S, pe, A_OUT + j, G(A_OUT + j, i), S.ps[(A_OUT + j) % SLOTS][:, :], S.mh, S.ml,
                                         None if i + j else S.merge_done, L * KT).then_inc(S.unit_done[(A_OUT + j) % SLOTS], 1))
        ln_pe(S, pe, L * 2)
        pe.wait_ge(S.p_ready, L + 1)
        for u in (A_OUT + 6, A_OUT + 7):
            pe.wait_ge(S.bank_free[u % SLOTS], G(u) + 2)
        pe.wait_ge(S.bank_free[(A_PLE + 1) % SLOTS], G(A_PLE + 1) + 1)
        for u in (A_PLE, A_PLE + 1):
            s = u % SLOTS
            pe.wait_ge(S.lo_ready[s], G(u) + 1)
            if u == A_PLE:
                pe.wait_ge(S.bank_free[s], G(u) + 1)
            else:
                pe.wait_ge(S.bank_free[(u - 1) % SLOTS], G(u - 1) + 2)
            for o in range(4):
                for k in range(2):
                    pe_tile(S, s, 2 * o + k, S.ps[o][:, :], S.ph, S.pl, k, k == 0, k == 1)
            S.last.then_inc(S.unit_done[s], 1)
        with pe.Fori(0, 4) as q:
            with pe.Fori(0, 2) as i:
                pe.wait_ge(S.bank_free[(A_PLE + 1) % SLOTS], G(A_PLE + 1) + 2)
                for u in range(A_FFN, A_FFN + SLOTS):
                    pe_unit(S, pe, u, G(u, q * 4 + i), S.ps[u % SLOTS][:, :], S.xh, S.xl,
                            None if u > A_FFN else S.x_ready, L * 2 * KT + KT).then_inc(S.unit_done[u % SLOTS], 1)
            with pe.Fori(0, 2) as i:
                for u in range(A_FFN, A_FFN + SLOTS):
                    pe_unit(S, pe, u, G(u, q * 4 + i + 2), S.ps[u % SLOTS][:, :], S.rh, S.rl,
                            None if u > A_FFN else S.ffn_h, (L * 4 + q) * KT + 2).then_inc(S.unit_done[u % SLOTS], 1)
        for i in range(2):
            ln_mean_pe(S, pe, L * 2 + 1, S.y_ready, L * KT + 2, S.yacc, i,
                       lambda j: pe_unit(S, pe, A_PG + j, G(A_PG + j, i), S.ps[(A_PG + j) % SLOTS][:, :], S.xh,
                                         S.xl).then_inc(S.unit_done[(A_PG + j) % SLOTS], 1))
        ln_pe(S, pe, L * 2 + 1)


def a_scalar(S, act, p_dram):
    nc = S.nc

    def take(u, g, out, func, banks=SLOTS):
        s = u % SLOTS
        act.wait_ge(S.unit_done[s], g + 1)
        nc.scalar.activation(out, S.ps[u % banks][:, :], func).then_inc(S.bank_free[s], 1)
        act_split(S, act, u, g)

    for s in range(SLOTS):
        act.wait_ge(S.raw_landed[s], 16)
        nc.scalar.activation(S.wh[s][:, :], S.raw[s][:, :], ACT.Copy).then_inc(S.hi_ready[s], 1)
    with act.Fori(0, DEPTH) as L:
        G = lambda u, i=0: L * A_GROUPS + u // SLOTS + i
        with act.Fori(0, 6) as i:
            for u in range(SLOTS):
                take(u, G(u, i), cols(S.qkv, i * SLOTS + u), ACT.Copy)
        for u in (24, 25):
            take(u, G(u), cols(S.qkv, u), ACT.Copy)
        vt = S.vt[:, :].rearrange("p (t c) -> p t c", t=QB)
        for v in range(A_NVT):
            act.wait_ge(S.vt_ready, L * A_NVT + v + 1)
            nc.scalar.activation(vt[:, :, v * P:(v + 1) * P], S.X[2 + v % 2][:, :].rearrange("p (t c) -> p t c", t=QB),
                                 ACT.Copy).then_inc(S.vt_done, 1)
        nc.scalar.preload_act_table_set("natural_log_exp_and_others")
        act.wait_ge(S.logf_in, L + 1)
        lf = S.wk[5][64:128, :]
        nc.scalar.activation(lf, lf, ACT.Exp)
        act.drain()
        nc.scalar.activation(lf, lf, ACT.Ln, bias=1.0).then_inc(S.logf_out, 1)
        def gate_take(i, first, j):
            u = A_GATE + first + j
            take(u, G(u, i), cols(S.gates, i * SLOTS + first + j), ACT.Copy, 2)

        for j in range(2):
            gate_take(0, ROPE_UNITS, j)
        for n, (b, h) in enumerate(idx_steps()):
            act.wait_ge(S.idx_ready, L * 24 + n + 1)
            if n >= 2:
                act.wait_ge(S.idx_acc, L * 24 + n - 1)
            w = (b + 1) * P
            nc.scalar.activation(S.r[n % 2][:, 0:w], S.X[n % 4][:, 0:w], ACT.Relu).then_inc(S.relu_done, 1)
            if n == 9:
                gate_take(0, ROPE_UNITS, 2)
        gate_take(0, ROPE_UNITS, 3)
        def fox_stage(e, i):
            src = S.qkv[64 * e:64 * e + 64, :]
            for t, u in ((e, A_FQ), (2 + e, A_FK)):
                nc.scalar.activation(S.wk[t][0:64, :], cols2(src, u * SEQ, i, SEQ, SEQ), ACT.Copy).then_inc(S.fox_staged, 1)

        def fox_after(n, i):
            if n == 0:
                fox_stage(1, i)
            if n == 5:
                fox_stage(0, i + 1)
            if n and n % 2 == 0:
                gate_take(i, FOX_UNITS, n // 2 - 1)

        fox_stage(0, 0)
        with act.Fori(0, 3) as i:
            attn_act(S, act, S.fox, (L * 3 + i) * 8, fox_steps(S, L, i),
                     lambda n: fox_after(n, i))
            gate_take(i, FOX_UNITS, 3)
        nc.scalar.preload_act_table_set("natural_log_exp_and_others")
        act.wait_ge(S.fox.out, (L + 1) * 24 + 2)
        with act.Fori(0, 2) as i:
            act.wait_ge(S.stk_oev, L * 5 + i * 2 + 1)
            nc.scalar.activation(S.wk[2][:, :], cols(S.qkv, i + A_SK), ACT.Copy).then_inc(S.s_staged, 1)
            for e in range(2):
                r = slice(64 * e, 64 * e + 64)
                nc.scalar.activation(S.wk[e][r, :], cols2(S.qkv[r, :], A_SQ * SEQ, i, SEQ, SEQ), ACT.Copy).then_inc(S.s_staged, 1)
            stk_act(S, act, (L * 5 + i * 2) * QB, 2, lambda m: m and m % 2 == 0 and gate_take(i, STK_UNITS, m // 2 - 1))
            gate_take(i, STK_UNITS, 3)
        stk_act(S, act, (L * 5 + 4) * QB, 1)
        with act.Fori(0, 2) as i:
            act.wait_ge(S.stk_oev, L * 5 + 6)
            for e in range(2):
                r = slice(64 * e, 64 * e + 64)
                nc.scalar.activation(S.wk[e][r, :], cols2(S.qkv[r, :], A_DQ * SEQ, i, SEQ, SEQ), ACT.Copy).then_inc(S.d_staged, 1)
            attn_act(S, act, S.dsa, L * 20 + i * 8, dsa_pair(S, i))
        attn_act(S, act, S.dsa, L * 20 + 16, dsa_last(S))
        for k in range(KT):
            act.wait_ge(S.ot_ready, L * KT + k + 1)
            nc.scalar.activation(S.rh[:, k * SEQ:(k + 1) * SEQ], S.X[k % 4][:, :], ACT.Copy).then_inc(S.ot_hi, 1)
        with act.Fori(0, 2) as i:
            for jj in range(4):
                for d in range(3):
                    t = cols(S.gates, i * SLOTS + d * KT + jj)
                    m = nc.scalar.activation(t, t, ACT.Tanh, scale=0.5)
                m.then_inc(S.gate_tanh, 1)
                u = A_UP + jj
                act.wait_ge(S.unit_done[u % SLOTS], G(u, i) + 1)
                act_split(S, act, u, G(u, i))
        act.wait_ge(S.merge_done, (L + 1) * KT)
        act.dma_start(S.praw[:, :], p_dram[bass.ds(L, 1), :, :].rearrange("a p n -> (a p) n")).then_inc(S.p_landed, 16)
        with act.Fori(0, 2) as i:
            for u in range(A_OUT, A_OUT + SLOTS):
                act.wait_ge(S.unit_done[u % SLOTS], G(u, i) + 1)
                act_split(S, act, u, G(u, i))
        def ple_take(d):
            u = A_PLE + d
            s = u % SLOTS
            act.wait_ge(S.unit_done[s], G(u) + 1)
            for o in range(4):
                m = nc.scalar.activation(cols(S.plep, 4 * d + o), S.ps[o][:, :], ACT.Copy)
            m.then_inc(S.bank_free[s], 1)
            act_split(S, act, u, G(u))

        ln_act(S, act, L * 2, S.t, PA_G1, PA_B1, lambda: ple_take(0))
        ple_take(1)
        with act.Fori(0, 4) as q:
            with act.Fori(0, 2) as i:
                for j in range(SLOTS):
                    u = A_FFN + j
                    s, g = u % SLOTS, G(u, q * 4 + i)
                    act.wait_ge(S.unit_done[s], g + 1)
                    act.wait_ge(S.ffn_h, (L * 4 + q) * KT + i * SLOTS + j + 1)
                    nc.scalar.activation(S.wk[j % 2][:, :], S.ps[s][:, :], ACT.Relu).then_inc(S.bank_free[s], 1)
                    act.drain()
                    nc.scalar.activation(cols(S.rh, i * SLOTS + j), S.wk[j % 2][:, :], ACT.Square).then_inc(S.ffn_act, 1)
                    act_split(S, act, u, g)
            with act.Fori(0, 2) as i:
                for u in range(A_FFN, A_FFN + SLOTS):
                    g = G(u, q * 4 + i + 2)
                    act.wait_ge(S.unit_done[u % SLOTS], g + 1)
                    act_split(S, act, u, g)
        with act.Fori(0, 2) as i:
            for j in range(SLOTS):
                u = A_PG + j
                s, g = u % SLOTS, G(u, i)
                act.wait_ge(S.unit_done[s], g + 1)
                act.wait_ge(S.y_ready, L * KT + i * SLOTS + j + 1)
                nc.scalar.activation(S.wk[4 + j % 2][:, :], S.ps[s][:, :], ACT.Tanh, scale=0.5).then_inc(S.bank_free[s], 1)
                act_split(S, act, u, g)
        ln_act(S, act, L * 2 + 1, S.yacc, PA_G2, PA_B2)


def top_round(S, dve, half):
    nc = S.nc
    for b in range(1, QB):
        sc = S.score[:, SC0[b]:SC0[b] + (b + 1) * P]
        if half == 0:
            nc.vector.max(S.top[b - 1][:, :], sc)
        else:
            nc.vector.match_replace(sc, S.top[b - 1][:, :], sc, MARK)
    dve.drain()


assert 3 * 4 + 4 == TOPK // 8


def a_vector(S, dve):
    nc = S.nc
    with dve.Fori(0, DEPTH) as L:
        G = lambda u, i=0: L * A_GROUPS + u // SLOTS + i
        nc.vector.tensor_copy(S.cur[:, :], cols(S.prmA, L, PA_N))
        dve.drain()
        dve.wait_ge(S.bank_free[25 % SLOTS], G(25) + 2)
        for u, n in ((A_FQ, 3), (A_SQ, 2), (A_S4D4Q, 1), (A_DQ, 2)):
            t = S.qkv[:, u * SEQ:(u + n) * SEQ]
            m = nc.vector.tensor_scalar(t, t, HD ** -0.5, None, ALU.mult)
        m.then_inc(S.scaled, 1)
        f, na = S.c[64:128, :], S.wk[5][64:128, :]
        nc.vector.tensor_scalar(f, S.qkv[64:128, A_IKF * SEQ:(A_IKF + 1) * SEQ], S.cur[64:128, PA_BF:PA_BF + 1], None, ALU.add)
        dve.drain()
        nc.vector.scalar_tensor_tensor(out=na, in0=f, scalar=-1.0, in1=f, op0=ALU.mult, op1=ALU.min).then_inc(S.logf_in, 1)
        for n, (u, lo, hi) in enumerate(ROPE):
            t = S.qkv[lo:hi, u * SEQ:(u + 1) * SEQ]
            a, b = S.wk[n % 2][lo:hi, :], S.wk[2 + n % 2][lo:hi, :]
            nc.vector.tensor_tensor(a, t, S.cos[lo:hi, :], ALU.mult)
            dve.wait_ge(S.rot_ready, L * len(ROPE) + n + 1)
            nc.vector.tensor_tensor(b, S.X[n % 2][lo:hi, :], S.sin[lo:hi, :], ALU.mult)
            dve.drain()
            nc.vector.tensor_tensor(t, a, b, ALU.add).then_inc(S.rope_done, 1)
        nc.vector.memset(S.wk[4][64:128, :], 1.0)
        dve.wait_ge(S.logf_out, L + 1)
        nc.vector.scalar_tensor_tensor(out=f, in0=f, scalar=0.0, in1=na, op0=ALU.min, op1=ALU.subtract)
        dve.drain()
        nc.vector.tensor_tensor_scan(na, S.wk[4][64:128, :], f, 0.0, ALU.mult, ALU.add)
        dve.drain()
        nc.vector.tensor_copy(f, na)
        for e in range(2):
            nc.vector.tensor_scalar(S.wk[2 + e][64:128, :], na, S.con[64:128, C_KA:C_KA + 1], S.con[64:128, C_KB:C_KB + 1],
                                    ALU.mult, ALU.add)
        dve.wait_ge(S.vt_done, (L + 1) * A_NVT)
        for n, (b, h) in enumerate(idx_steps()):
            dve.wait_ge(S.relu_done, L * 24 + n + 1)
            w = (b + 1) * P
            acc = S.sacc[:, SC0[b]:SC0[b] + w]
            iw = S.vt[:, b * A_NVT * P + V_IW + h:b * A_NVT * P + V_IW + h + 1]
            if h == 0:
                nc.vector.tensor_scalar(acc, S.r[n % 2][:, 0:w], iw, None, ALU.mult).then_inc(S.idx_acc, 1)
            else:
                nc.vector.scalar_tensor_tensor(out=acc, in0=S.r[n % 2][:, 0:w], scalar=iw, in1=acc, op0=ALU.mult,
                                               op1=ALU.add).then_inc(S.idx_acc, 1)
            dve.drain()
        for b in range(1, QB):
            nc.vector.memset(S.sacc[0:64, SC0[b] + b * P + 64:SC0[b] + (b + 1) * P], NEG)
        dve.drain()
        nc.vector.tensor_copy(S.score[:, :], S.sacc[:, :])
        def fox_rows(e, i):
            qa, qb = cols2(S.con[64:128, :], C_QA + e, i, 2, 1), cols2(S.con[64:128, :], C_QB + e, i, 2, 1)
            nc.vector.tensor_scalar(S.wk[e][64:128, :], f, qa, qb, ALU.mult, ALU.add).then_inc(S.fox_aug, 1)

        def fox_after(n, i):
            if n == 4:
                fox_rows(0, i + 1)
            top_round(S, dve, n % 2)

        fox_rows(0, 0)
        with dve.Fori(0, 3) as i:
            fox_rows(1, i)
            attn_dve(S, dve, S.fox, (L * 3 + i) * 8, fox_steps(S, L, i), lambda n: fox_after(n, i))
        for e in range(2):
            m = nc.vector.memset(S.wk[e][64 - 64 * e:128 - 64 * e, :], 0.0)
        m.then_inc(S.q0_zero, 1)
        with dve.Fori(0, 2) as i:
            stk_dve(S, dve, (L * 5 + i * 2) * QB, L * 5 + i * 2, [otok_head(S, 6 + e, i) for e in range(2)],
                    lambda m: m % QB in (2, 3) and top_round(S, dve, m % QB - 2))
        nc.vector.tensor_scalar(S.dmask[:, :], S.score[:, :], MARK / 2, NEG, ALU.is_gt, ALU.mult).then_inc(S.mask_ready, 1)
        stk_dve(S, dve, (L * 5 + 4) * QB, L * 5 + 4, [otok_head(S, 10, 0)])
        with dve.Fori(0, 2) as i:
            attn_dve(S, dve, S.dsa, L * 20 + i * 8, dsa_pair(S, i))
        attn_dve(S, dve, S.dsa, L * 20 + 16, dsa_last(S))
        for k in range(KT):
            dve.wait_ge(S.ot_hi, L * KT + k + 1)
            nc.vector.tensor_tensor(S.rl[:, k * SEQ:(k + 1) * SEQ], S.X[k % 4][:, :],
                                    S.rh[:, k * SEQ:(k + 1) * SEQ].bitcast(F32), ALU.subtract).then_inc(S.ot_done, 1)
        with dve.Fori(0, 2) as i:
            for jj in range(4):
                u = A_UP + jj
                s = u % SLOTS
                dve.wait_ge(S.unit_done[s], G(u, i) + 1)
                dve.wait_ge(S.gate_tanh, L * KT + i * 4 + jj + 1)
                a, b, c = S.wk[3 * (jj % 2)][:, :], S.wk[1][:, :], S.wk[2][:, :]
                nc.vector.scalar_tensor_tensor(out=a, in0=cols(S.gates, i * 4 + jj), scalar=1.0, in1=S.ps[s][:, :],
                                               op0=ALU.add, op1=ALU.mult).then_inc(S.bank_free[s], 1)
                for d, o in ((0, b), (1, c)):
                    m = nc.vector.scalar_tensor_tensor(out=o, in0=cols(S.gates, i * 4 + (d + 1) * KT + jj), scalar=1.0,
                                                       in1=S.X[2 * (jj % 2) + d][:, :], op0=ALU.add, op1=ALU.mult)
                m.then_inc(S.merge_x, 1)
                dve.drain()
                nc.vector.tensor_tensor(a, a, b, ALU.add)
                dve.drain()
                nc.vector.tensor_tensor(a, a, c, ALU.add)
                dve.drain()
                mh, ml = cols(S.mh, i * 4 + jj), cols(S.ml, i * 4 + jj)
                nc.vector.tensor_scalar(mh, a, 0.5, None, ALU.mult)
                dve.drain()
                nc.vector.scalar_tensor_tensor(out=ml, in0=a, scalar=0.5, in1=mh.bitcast(F32), op0=ALU.mult,
                                               op1=ALU.subtract).then_inc(S.merge_done, 1)
        dve.wait_ge(S.p_landed, 16 * (L + 1))
        nc.vector.tensor_copy(S.ph[:, :], S.praw[:, :])
        dve.drain()
        nc.vector.tensor_tensor(S.pl[:, :], S.praw[:, :], S.ph[:, :].bitcast(F32), ALU.subtract).then_inc(S.p_ready, 1)
        with dve.Fori(0, 2) as i:
            for j in range(SLOTS):
                u = A_OUT + j
                s = u % SLOTS
                dve.wait_ge(S.unit_done[s], G(u, i) + 1)
                t = cols(S.t, i * SLOTS + j)
                nc.vector.scalar_tensor_tensor(out=t, in0=cols(S.xh, i * SLOTS + j).bitcast(F32), scalar=ALPHA,
                                               in1=S.ps[s][:, :], op0=ALU.mult, op1=ALU.add).then_inc(S.bank_free[s], 1)
                dve.drain()
                nc.vector.scalar_tensor_tensor(out=t, in0=cols(S.xl, i * SLOTS + j).bitcast(F32), scalar=ALPHA,
                                               in1=t, op0=ALU.mult, op1=ALU.add).then_inc(S.t_ready, 1)
        ln_dve(S, dve, L * 2, S.t)
        dve.drain()
        nc.vector.tensor_scalar(S.yacc[:, :], S.xh[:, :].bitcast(F32), ALPHA, None, ALU.mult)
        dve.drain()
        nc.vector.scalar_tensor_tensor(out=S.yacc[:, :], in0=S.xl[:, :].bitcast(F32), scalar=ALPHA, in1=S.yacc[:, :],
                                       op0=ALU.mult, op1=ALU.add)
        with dve.Fori(0, 4) as q:
            with dve.Fori(0, 2) as i:
                for j in range(SLOTS):
                    dve.wait_ge(S.ffn_act, (L * 4 + q) * KT + i * SLOTS + j + 1)
                    h = S.wk[2 + j % 2][:, :]
                    nc.vector.tensor_tensor(h, S.wk[j % 2][:, :], S.wk[j % 2][:, :], ALU.mult)
                    dve.drain()
                    nc.vector.tensor_tensor(cols(S.rl, i * SLOTS + j), h, cols(S.rh, i * SLOTS + j).bitcast(F32),
                                            ALU.subtract).then_inc(S.ffn_h, 1)
            with dve.Fori(0, 2) as i:
                for j in range(SLOTS):
                    u = A_FFN + j
                    s = u % SLOTS
                    dve.wait_ge(S.unit_done[s], G(u, q * 4 + i + 2) + 1)
                    y = cols(S.yacc, i * SLOTS + j)
                    nc.vector.tensor_tensor(y, y, S.ps[s][:, :], ALU.add).then_inc(S.bank_free[s], 1)
        with dve.Fori(0, 2) as i:
            for j in range(SLOTS):
                u = A_PG + j
                s = u % SLOTS
                dve.wait_ge(S.bank_free[s], G(u, i) + 2)
                a, y = S.wk[6 + j % 2][:, :], cols(S.yacc, i * SLOTS + j)
                nc.vector.scalar_tensor_tensor(out=a, in0=S.wk[4 + j % 2][:, :], scalar=1.0, in1=cols(S.plep, i * SLOTS + j),
                                               op0=ALU.add, op1=ALU.mult)
                dve.drain()
                nc.vector.scalar_tensor_tensor(out=y, in0=a, scalar=0.5, in1=y, op0=ALU.mult,
                                               op1=ALU.add).then_inc(S.y_ready, 1)
        ln_dve(S, dve, L * 2 + 1, S.yacc)


def GB(L, u, i=0):
    return DEPTH * A_GROUPS + L * B_GROUPS + u // SLOTS + i


def seq(t, j):
    return t[:, j * SEQ:(j + 1) * SEQ]


def rms_pe(S, pe, n0, j):
    pe.wait_ge(S.rms_sq, n0 * KT + j + 1)
    S.nc.tensor.matmul(S.X[1][:, :], S.ones[:, :], S.wk[j % 4][:, :], start=(j == 0),
                       stop=(j == KT - 1)).then_inc(S.rms_var, 1)


def rms_square(S, act, n0, j):
    act.wait_ge(S.res_ready, n0 * KT + j + 1)
    if j >= 4:
        act.wait_ge(S.rms_var, n0 * KT + j - 3)
    S.nc.scalar.activation(S.wk[j % 4][:, :], seq(S.res, j), ACT.Square).then_inc(S.rms_sq, 1)


def rms_root(S, act, n0):
    act.wait_ge(S.rms_var, n0 * KT + KT)
    S.nc.scalar.activation(S.wk[2][:, :], S.X[1][:, :], ACT.Sqrt, bias=S.eps2[:, :]).then_inc(S.rms_std, 1)


def rms_act(S, act, n0):
    rms_root(S, act, n0)
    for j in range(KT):
        act.wait_ge(S.rms_y, n0 * KT + j + 1)
        S.nc.scalar.activation(seq(S.xh, j), S.wk[4 + j % 4][:, :], ACT.Copy).then_inc(S.rms_hi, 1)


def rms_dve(S, dve, n0):
    nc = S.nc
    dve.wait_ge(S.rms_std, n0 + 1)
    nc.vector.reciprocal(S.wk[3][:, :], S.wk[2][:, :])
    dve.drain()
    for j in range(KT + 2):
        if j < KT:
            nc.vector.scalar_tensor_tensor(out=S.wk[4 + j % 4][:, :], in0=seq(S.res, j), scalar=S.curB[:, PB_G + j:PB_G + j + 1],
                                           in1=S.wk[3][:, :], op0=ALU.mult, op1=ALU.mult).then_inc(S.rms_y, 1)
        if j >= 2:
            q = j - 2
            dve.wait_ge(S.rms_hi, n0 * KT + q + 1)
            nc.vector.tensor_tensor(seq(S.xl, q), S.wk[4 + q % 4][:, :], seq(S.xh, q).bitcast(F32),
                                    ALU.subtract).then_inc(S.x_ready, 1)
            dve.drain()


def partner(S, u):
    s = u % SLOTS
    return S.ps[s - 2] if u < B_OUTL else S.X[(0, 2, 3, 0)[s]]


def pairs_pe(S, pe, L, u, rh, rl, k0, ready=None, n0=0):
    s = u % SLOTS
    pe.wait_ge(S.lo_ready[s], GB(L, u) + 1)
    pe.wait_ge(S.bank_free[s], GB(L, u) + 1)
    if u == B_OUTN + 3:
        pe.wait_ge(S.bank_free[0], GB(L, B_OUTN) + 2)
    for o, bank in ((0, S.ps[s]), (1, partner(S, u))):
        for k in range(4):
            if ready:
                pe.wait_ge(ready, n0 + k + 1)
            pe_tile(S, s, 4 * o + k, bank[:, :], rh, rl, k0 + k, k == 0, k == 3)
    S.last.then_inc(S.unit_done[s], 1)


def nsa_steps(S, L, i):
    steps = []
    for tt in range(2):
        staged = ((S.q_staged, L * 10 + i * 4 + 2 * tt + 2),)
        for src, k, br in (("s", S.kv["ks"], 1), ("w", S.kv["kw"], 2)):
            for e in range(2):
                for b in range(QB):
                    w = (b + 1) * P
                    qk = [(S.wk[2 * tt + e][:, b * P:w], k[:, 0:w], 0, w),
                          (S.idb[:, :], S.causb[:, :], b * P, P)]

                    def v(kt, src=src, e=e):
                        return S.vtok[src][:, kt * P + e * HD:kt * P + (e + 1) * HD]

                    def scale(n, b=b, e=e, br=br, tt=tt):
                        gate = cols2(S.gate, b * 3 * B_HEADS + e * 12 + tt * 3 + br, i, 6, 1)
                        S.nc.vector.tensor_scalar(S.rg[n % 2][:, :], S.rinv[n % 2][:, :], gate, None, ALU.mult)

                    def norm(n, b=b, e=e, tt=tt):
                        o = cols2(S.ot2, b * 512 + e * 256 + tt * HD, i, 2 * HD, HD)
                        S.nc.vector.scalar_tensor_tensor(out=o, in0=out_of(S, n), scalar=S.rg[n % 2][:, :], in1=o,
                                                         op0=ALU.mult, op1=ALU.add).then_inc(S.nsa.out, 1)
                    steps.append(Step(b, qk, v, norm, scale, () if b or e or br == 2 else staged))
    return steps


def out_fill(S, pe, L, i, n):
    j, k = divmod(n, KT)
    o, kk = divmod(k, 4)
    g = GB(L, B_OUTL, i)
    if k == 0:
        pe.wait_ge(S.lo_ready[j], g + 1)
        pe.wait_ge(S.first_added, L * 8 + i * 4 + j + 1)
    if k == 4:
        pe.wait_ge(S.bank_free[(j - 1) % SLOTS], g + 2 if j else g + 1)
    pe_tile(S, j, k, S.ps[o][:, :], S.xh, S.xl, i * 4 + kk, kk == 0, kk == 3)
    if k == 3:
        S.last.then_inc(S.first_out, 1)
    if k == KT - 1:
        S.last.then_inc(S.unit_done[j], 1)


def out_add(S, dve, L, i, j, o):
    if o == 0:
        dve.wait_ge(S.first_out, L * 8 + i * 4 + j + 1)
    else:
        dve.wait_ge(S.unit_done[j], GB(L, B_OUTL, i) + 1)
    r = seq(S.res, 2 * j + o)
    S.nc.vector.tensor_tensor(r, r, S.ps[o][:, :], ALU.add).then_inc(S.bank_free[j] if o else S.first_added, 1)


def rope_tiles(S):
    return [S.kv[n][:, :] for n in ("kc", "ks", "kw")] + [seq(S.q, t) for t in range(4)]


NROPE = 7
ROPE_AT = 8


def b_tensor(S, pe):
    nc = S.nc
    ident = S.con[:, C_ID:C_ID + P]
    for j in range(KT):
        rms_pe(S, pe, 0, j)
    with pe.Fori(0, DEPTH) as L:
        with pe.Fori(0, 5) as i:
            for u in range(SLOTS):
                pe_unit(S, pe, u, GB(L, u, i), S.ps[u][:, :], S.xh, S.xl, None if u else S.x_ready,
                        KT * (1 + 2 * DEPTH) + L * KT).then_inc(S.unit_done[u], 1)
        for u in range(20, B_ZL):
            pe_unit(S, pe, u, GB(L, u), S.ps[u % SLOTS][:, :], S.xh, S.xl).then_inc(S.unit_done[u % SLOTS], 1)
        for x in range(12):
            if x == 0:
                pe.wait_ge(S.bank_free[B_G % SLOTS], GB(L, B_G) + 2)
            if x == 2:
                pe.wait_ge(S.bvt_done, L * 2 + 1)
            if x < 3:
                for t in range(QB):
                    m = nc.tensor.transpose(S.X[2 + x % 2][:, t * P:(t + 1) * P],
                                            S.kv[("vs", "vw", "gl")[x]][:, t * P:(t + 1) * P], ident)
                m.then_inc(S.bvt_ready, 1)
            if x == ROPE_AT:
                pe.wait_ge(S.bank_free[(B_Q + 3) % SLOTS], GB(L, B_Q + 3) + 2)
            for n in range(max(0, 2 * (x - ROPE_AT)), max(0, min(NROPE, 2 * (x - ROPE_AT) + 2))):
                if n >= 2:
                    pe.wait_ge(S.b_rope_done, L * NROPE + n - 1)
                nc.tensor.matmul(S.X[n % 2][:, :], S.con[:, C_ROT:C_ROT + P], rope_tiles(S)[n], start=True,
                                 stop=True).then_inc(S.b_rot_ready, 1)
            if x == 11:
                pe.wait_ge(S.dw_done, L + 1)                                
                pe.wait_ge(S.gl_done, L + 1)
                for t in range(4):
                    mm = nc.tensor.matmul(S.X[2][:, :], S.ones[:, :], seq(S.cacc, t), start=(t == 0), stop=(t == 3))
                mm.then_inc(S.cl_mean, 1)
            u = B_ZL + x
            pe_unit(S, pe, u, GB(L, u), S.ps[u % SLOTS][:, :], S.xh, S.xl).then_inc(S.unit_done[u % SLOTS], 1)
        s = B_BD % SLOTS
        for u in range(B_BD - SLOTS, B_BD):
            pe.wait_ge(S.bank_free[u % SLOTS], GB(L, u) + 2)
        pe.wait_ge(S.lo_ready[s], GB(L, B_BD) + 1)
        pe.wait_ge(S.xc_split, L + 1)
        for t in range(4):
            if t >= 2:
                pe.wait_ge(S.lru_gate, L * 4 + t - 1)
            for d in range(2):
                pe_tile(S, s, 2 * t + d, S.ps[2 * (t % 2) + d][:, :], S.xch, S.xcl, t, True, True)
            S.last.then_inc(S.lru_ready if t < 3 else S.unit_done[s], 1)
        pe.wait_ge(S.b_rope_done, (L + 1) * NROPE)
        for kv in range(2):
            pe.wait_ge(S.blk_ready, L * 2 + kv + 1)
            for q in range(4):
                u = B_CMP1 + 4 * kv + q
                s = u % SLOTS
                if kv == 0 and q == 2:
                    pe.wait_ge(S.lru_gate, L * 4 + 4)
                    for t in range(4):
                        pe.wait_ge(S.cl_sq, L * 4 + t + 1)
                        nc.tensor.matmul(S.ps[1][:, :], S.ones[:, :], S.lnsq[t % 2][:, :], start=(t == 0), stop=(t == 3)).then_inc(S.cl_var, 1)
                pe.wait_ge(S.lo_ready[s], GB(L, u) + 1)
                for k in range(4):
                    lp = 4 * q + k
                    c = (4 + 2 * kv) * SEQ + lp * NB2
                    wh, wl = (t[s][:, k * 256:(k + 1) * 256] for t in (S.wh, S.wl))
                    bh, bl = (t[:, c:c + NB2] for t in (S.xh, S.xl))
                    out = S.X[kv][0:NB2, 0:256]
                    nc.tensor.matmul(out, bh, wh, start=(lp == 0), stop=False)
                    nc.tensor.matmul(out, bl, wh, start=False, stop=False)
                    mm = nc.tensor.matmul(out, bh, wl, start=False, stop=(lp == 15))
                mm.then_inc(S.unit_done[s], 1)
        pe.wait_ge(S.bvt_done, L * 2 + 2)
        pe.wait_ge(S.cl_d, L * 4 + 4)
        for kv in range(2):
            pe.wait_ge(S.hid_act, L * 2 + kv + 1)
            for m in range(2):
                mm = nc.tensor.matmul(S.X[2 + kv][:, m * HD:m * HD + NB2],
                                      S.wk[0][0:NB2, kv * 256 + m * P:kv * 256 + (m + 1) * P], ident[0:NB2, 0:NB2],
                                      start=True, stop=True, skip_group_check=True)
            mm.then_inc(S.hid_turned, 1)
        s = B_CMP2 % SLOTS
        pe.wait_ge(S.lo_ready[s], GB(L, B_CMP2) + 1)
        pe.wait_ge(S.bvt_done, L * 2 + 2)
        pe.wait_ge(S.gl_done, L + 1)
        pe.wait_ge(S.hid_split, L * 2 + 1)
        for m in range(2):
            wh, wl = (t[s][:, m * P:(m + 1) * P] for t in (S.wh, S.wl))
            bh, bl = (t[:, m * NB2:(m + 1) * NB2] for t in (S.hkh, S.hkl))
            for i, (a, b) in enumerate(((wh, bh), (wh, bl), (wl, bh))):
                mm = nc.tensor.matmul(S.X[2][:, P:P + NB2], a, b, start=(m == 0 and i == 0), stop=(m == 1 and i == 2),
                                      skip_group_check=True)
        mm.then_inc(S.unit_done[s], 1)
        s = (B_CMP2 + 1) % SLOTS
        pe.wait_ge(S.lo_ready[s], GB(L, B_CMP2 + 1) + 1)
        pe.wait_ge(S.hid_split, L * 2 + 2)
        for g in range(2):
            for m in range(2):
                wh, wl = (t[s][:, m * P:m * P + HD] for t in (S.wh, S.wl))
                bh, bl = (t[:, (2 * m + g) * P:(2 * m + g + 1) * P] for t in (S.hvh, S.hvl))
                for i, (a, b) in enumerate(((bh, wh), (bh, wl), (bl, wh))):
                    mm = nc.tensor.matmul(S.X[3][:, P + g * HD:P + (g + 1) * HD], a, b, start=(m == 0 and i == 0),
                                          stop=(m == 1 and i == 2), skip_group_check=True)
        mm.then_inc(S.unit_done[s], 1)
        pe.wait_ge(S.kcb_ready, L + 1)
        for b in range(QB):
            for t in range(B_REP):
                o = S.X[b // 2][:, (b % 2) * 256:(b % 2 + 1) * 256].rearrange("p (g t n) -> p g t n", g=2, t=B_REP)[:, :, t, :]
                mm = nc.tensor.matmul(o, S.q[:, t * SEQ + b * P:t * SEQ + (b + 1) * P],
                                      S.kcb[:, :].rearrange("p (g n) -> p g n", g=2), start=True, stop=True, skip_group_check=True)
            if b % 2:
                mm.then_inc(S.cs_ready, 1)
        for u in (B_PW2, B_PW2 + 1):
            pairs_pe(S, pe, L, u, S.xh, S.xl, 4, S.un_ready, L * 4)
        pe.wait_ge(S.vbd_ready, L + 1)
        for h in range(2):
            pe.wait_ge(S.cp_ready, L * 2 + h + 1)
            for k in range(4):
                mm = nc.tensor.transpose(S.X[2 + h][:, k * P:(k + 1) * P], S.wk[4 + h][:, k * P:(k + 1) * P], ident)
            mm.then_inc(S.cpt_ready, 1)
        for b in range(QB):
            pe.wait_ge(S.cpt_copied, L * 2 + b // 2 + 1)
            if b >= 2:
                pe.wait_ge(S.oc_done, L * 4 + b - 1)
            for g in range(2):
                c = ((b % 2) * 2 + g) * P
                mm = nc.tensor.matmul(S.X[b % 2][:, g * 256:(g + 1) * 256], S.wk[6 + b // 2][:, c:c + P],
                                      S.vbd[:, g * 256:(g + 1) * 256], start=True, stop=True, skip_group_check=True)
            mm.then_inc(S.oc_ready, 1)
        with pe.Fori(0, 2) as i:
            pe.wait_ge(S.lru_done, L + 1)
            pe.wait_ge(S.oc_done, L * 4 + 4)
            pe.wait_ge(S.mc_y, L * 4 + 4)
            pe.wait_ge(S.mc_ready, L * 4 + i * 4 + 1)
            pe.wait_ge(S.q_zero, L + 1)
            attn_pe(S, pe, S.nsa, L * 64 + i * 32, nsa_steps(S, L, i), ident,
                    lambda n, half: half and out_fill(S, pe, L, i, n))
        pe.wait_ge(S.nsa.out, (L + 1) * 64 + 2)
        for k in range(4):
            for b in range(QB):
                mm = nc.tensor.transpose(S.X[k][:, b * P:(b + 1) * P], S.ot2[:, b * 512 + k * P:b * 512 + (k + 1) * P], ident)
            mm.then_inc(S.bt_ready, 1)
        for j in range(4):
            pairs_pe(S, pe, L, B_OUTN + j, S.mnh, S.mnl, 0, None if j else S.mn_ready, L * 4)
            for x in range(2 * j - 2, 2 * j):
                if x >= 0:
                    rms_pe(S, pe, L + 1, x)
        rms_pe(S, pe, L + 1, KT - 2)
        rms_pe(S, pe, L + 1, KT - 1)


def b_scalar(S, act, T):
    nc = S.nc

    def take(L, u, i, out, func, **kw):
        s = u % SLOTS
        act.wait_ge(S.unit_done[s], GB(L, u, i) + 1)
        nc.scalar.activation(out, S.ps[s][:, :], func, **kw).then_inc(S.bank_free[s], 1)
        act_split(S, act, u, GB(L, u, i))

    def used(L, u, i=0):
        act.wait_ge(S.unit_done[u % SLOTS], GB(L, u, i) + 1)
        act_split(S, act, u, GB(L, u, i))

    act.dma_start(S.prmB[:, :], T["prm_b"]).then_inc(S.pb_landed, 16)
    for j in range(KT):
        rms_square(S, act, 0, j)
    with act.Fori(0, DEPTH) as L:
        rms_act(S, act, L)
        act.wait_ge(S.x_ready, KT * (2 + 2 * DEPTH) + L * KT)
        act.dma_start(S.pos[:, :], T["pos"].to_broadcast([P, SEQ])).then_inc(S.pb_landed, 16)
        act.wait_ge(S.lam_in, L + 1)
        nc.scalar.activation(S.lam[0][:, :], S.lam[0][:, :], ACT.Exp).then_inc(S.lam_out, 1)
        for j in range(SLOTS):
            c = j * UC_W + CONV_K - 1
            take(L, B_GA + j, 0, S.uc[:, c:c + SEQ], ACT.Copy, scale=0.5)
        act.wait_ge(S.ang_ready, L + 1)
        nc.scalar.activation(S.sin[:, :], S.wk[0][:, :], ACT.Sin)
        nc.scalar.activation(S.cos[:, :], S.wk[1][:, :], ACT.Sin, scale=-1.0, bias=S.halfpi[:, :]).then_inc(S.tab_ready, 1)
        for j in range(SLOTS):
            if j >= 2:
                act.wait_ge(S.glu_done, L * 4 + j - 1)
            take(L, B_GB + j, 0, S.wk[6 + j % 2][:, :], ACT.Tanh, scale=0.5)
        for j in range(SLOTS):
            c = j * UP_W + LRU_K - 1
            take(L, B_U + j, 0, S.up[:, c:c + SEQ], ACT.Copy)
        for j, name in enumerate(("kc", "ks", "kw", "vc", "vs", "vw")):
            take(L, B_KV + j, 0, S.kv[name][:, :], ACT.Copy)
        take(L, B_G, 0, S.kv["gl"][:, :], ACT.Tanh, scale=0.5, bias=S.curB[:, PB_BG:PB_BG + 1])
        for j in range(SLOTS):
            take(L, B_Q + j, 0, seq(S.q, j), ACT.Copy, scale=HD ** -0.5)

        def cut_blocks(kv, name):
            for g in range(2):
                for l2 in range(2):
                    src = S.kv[name][64 * g:64 * g + 64, :]
                    o = S.blk[kv][64 * l2:64 * l2 + 64, :].rearrange("p (a g n) -> p a g n", a=16, g=2)[:, :, g, :]
                    for half in range(2):
                        i = src[:, 16 * half:16 * half + 16 * NBLK].rearrange("p (n a l) -> p a n l", a=8, l=2)[:, :, :, l2]
                        m = nc.scalar.activation(o[:, 8 * half:8 * half + 8, :], i, ACT.Copy)
            m.then_inc(S.blk_raw[kv], 1)

        for x in range(12):
            z = (S.zl, S.zc, S.zn)[x // 4]
            take(L, B_ZL + x, 0, seq(z, x % 4), ACT.Silu)
            if x < 2:
                act.wait_ge(S.bvt_ready, L * 3 + x + 1)
                nc.scalar.activation(S.vtok["sw"[x]][:, :], S.X[2 + x][:, :], ACT.Copy).then_inc(S.bvt_done, 1)
            if x == 5:
                cut_blocks(1, "vc")
            if x == 10:
                act.wait_ge(S.dw_done, L + 1)
                nc.scalar.activation(S.xch[:, :], S.xc[:, :], ACT.Copy).then_inc(S.xc_hi, 1)
            if x == ROPE_AT + 1:
                act.wait_ge(S.b_rope_done, L * NROPE + 1)
                cut_blocks(0, "kc")
        for t in range(4):
            if t < 3:
                act.wait_ge(S.lru_ready, L * 3 + t + 1)
            else:
                act.wait_ge(S.unit_done[B_BD % SLOTS], GB(L, B_BD) + 1)
            nc.scalar.activation(seq(S.la, t), S.ps[2 * (t % 2)][:, :], ACT.Tanh, scale=0.5, bias=S.curB[:, PB_BA + t:PB_BA + t + 1])
            nc.scalar.activation(seq(S.lri, t), S.ps[2 * (t % 2) + 1][:, :], ACT.Tanh, scale=0.5,
                                 bias=S.curB[:, PB_BI + t:PB_BI + t + 1]).then_inc(S.lru_gate, 1)
        used(L, B_BD)

        for t in range(4):
            act.wait_ge(S.cl_d, L * 4 + t + 1)
            if t >= 2:
                act.wait_ge(S.cl_var, L * 4 + t - 1)
            nc.scalar.activation(S.lnsq[t % 2][:, :], seq(S.cacc, t), ACT.Square).then_inc(S.cl_sq, 1)
        act.wait_ge(S.nla_ready, L + 1)
        nc.scalar.activation(S.ls[:, :], S.la[:, :], ACT.Tanh)
        act.drain()
        nc.scalar.activation(S.la[:, :], S.la[:, :], ACT.Exp, scale=-1.0).then_inc(S.a_ready, 1)

        def hidden(kv):
            act.wait_ge(S.unit_done[(B_CMP1 + 3) % SLOTS], GB(L, B_CMP1 + 4 * kv + 3) + 1)
            nc.scalar.activation(S.wk[0][0:NB2, kv * 256:(kv + 1) * 256], S.X[kv][0:NB2, 0:256], ACT.Silu).then_inc(S.hid_act, 1)

        act.wait_ge(S.cl_var, L * 4 + 4)
        nc.scalar.activation(S.wk[3][:, :], S.ps[1][:, :], ACT.Sqrt, scale=2.0, bias=S.eps2[:, :]).then_inc(S.cl_std, 1)
        used(L, B_CMP1)
        used(L, B_CMP1 + 1)
        act.wait_ge(S.b2_ready, L + 1)
        nc.scalar.activation(S.ls[:, :], S.ls[:, :], ACT.Sqrt, bias=S.tiny[:, :]).then_inc(S.beta_ready, 1)
        used(L, B_CMP1 + 2)
        hidden(0)
        for u in range(3, 7):
            used(L, B_CMP1 + u)
        hidden(1)
        used(L, B_CMP1 + 7)
        for t in range(4):
            act.wait_ge(S.cl_y, L * 4 + t + 1)
            nc.scalar.activation(seq(S.cacc, t), seq(S.cacc, t), ACT.Silu)
            act.drain()
            nc.scalar.activation(seq(S.xh, 4 + t), seq(S.cacc, t), ACT.Copy).then_inc(S.cl_hi, 1)
        used(L, B_CMP2)
        used(L, B_CMP2 + 1)
        for h in range(2):
            act.wait_ge(S.cexp_in, L * 2 + h + 1)
            nc.scalar.activation(S.wk[4 + h][:, :], S.wk[4 + h][:, :], ACT.Exp).then_inc(S.cexp_out, 1)
        for h in range(2):
            act.wait_ge(S.cpt_ready, L * 2 + h + 1)
            nc.scalar.activation(S.wk[6 + h][:, :], S.X[2 + h][:, :], ACT.Copy).then_inc(S.cpt_copied, 1)

        def nsa_stage(tt, i):
            for e in range(2):
                r = slice(64 * e, 64 * e + 64)
                q = S.q[r, tt * SEQ:(tt + 1) * SEQ] if isinstance(i, int) else S.q[r, bass.ds(i * 2 * SEQ + tt * SEQ, SEQ)]
                nc.scalar.activation(S.wk[2 * tt + e][r, :], q, ACT.Copy).then_inc(S.q_staged, 1)

        def nsa_after(n, i):
            if n == 2:
                nsa_stage(1, i)
            if n == 20:
                nsa_stage(0, 1 - i)
            if n and n % KT == 0:
                used(L, B_OUTL + n // KT - 1, i)

        nsa_stage(0, 0)
        used(L, B_PW2)
        used(L, B_PW2 + 1)
        for t in range(4):
            act.wait_ge(S.mc_y, L * 4 + t + 1)
            nc.scalar.activation(seq(S.xh, 4 + t), seq(S.zc, t), ACT.Copy).then_inc(S.mc_hi, 1)
        with act.Fori(0, 2) as i:
            attn_act(S, act, S.nsa, L * 64 + i * 32, nsa_steps(S, L, i),
                     lambda n: nsa_after(n, i))
            used(L, B_OUTL + 3, i)
        for k in range(4):
            act.wait_ge(S.mn_y, L * 4 + k + 1)
            nc.scalar.activation(seq(S.mnh, k), seq(S.zn, k), ACT.Copy).then_inc(S.mn_hi, 1)
        for j in range(4):
            used(L, B_OUTN + j)
            for x in (2 * j, 2 * j + 1):
                rms_square(S, act, L + 1, x)
    rms_root(S, act, DEPTH)


def free_bank(S, dve, u):
    s = u % SLOTS
    S.nc.vector.memset(S.tick[:, 24 + s:25 + s], 0.0).then_inc(S.bank_free[s], 1)


def b_rope_tables(S, dve, L):
    nc = S.nc
    ang, k, r = S.wk[2][:, :], S.wk[3][:, :], S.wk[0][:, :]
    two_pi = (6.25, 0.033203125, 2 * math.pi - 6.25 - 0.033203125)
    magic = 1.5 * 2.0 ** 23
    dve.wait_ge(S.pb_landed, 16 * (L + 2))
    nc.vector.tensor_copy(ang, S.pos[:, :])
    dve.drain()
    nc.vector.tensor_scalar(ang, ang, S.prmB[:, PB_INV:PB_INV + 1], None, ALU.mult)
    dve.drain()
    nc.vector.tensor_scalar(k, ang, 1 / (2 * math.pi), magic, ALU.mult, ALU.add)
    dve.drain()
    nc.vector.tensor_scalar(k, k, magic, None, ALU.subtract)
    dve.drain()
    nc.vector.scalar_tensor_tensor(out=r, in0=k, scalar=-two_pi[0], in1=ang, op0=ALU.mult, op1=ALU.add)
    for part in two_pi[1:]:
        dve.drain()
        nc.vector.scalar_tensor_tensor(out=r, in0=k, scalar=-part, in1=r, op0=ALU.mult, op1=ALU.add)
    dve.drain()
    nc.vector.tensor_scalar(r, r, 3.1415925, -3.1415925, ALU.min, ALU.max)
    dve.drain()
    nc.vector.scalar_tensor_tensor(out=S.wk[1][:, :], in0=r, scalar=-1.0, in1=r, op0=ALU.mult, op1=ALU.max).then_inc(S.ang_ready, 1)


def b_softplus(S, dve, L):
    nc = S.nc
    e, y, y2, p, m = (t[:, :] for t in S.lam)
    lam = S.curB[:, PB_LAM:PB_LAM + 4]
    dve.wait_ge(S.lam_out, L + 1)
    nc.vector.tensor_scalar(y, e, 2.0, None, ALU.add)
    dve.drain()
    nc.vector.reciprocal(y, y)
    dve.drain()
    nc.vector.tensor_tensor(y, y, e, ALU.mult)
    dve.drain()
    nc.vector.tensor_tensor(y2, y, y, ALU.mult)
    dve.drain()
    nc.vector.tensor_scalar(p, y2, 1 / 15, None, ALU.mult)
    for k in range(13, 1, -2):
        dve.drain()
        nc.vector.scalar_tensor_tensor(out=p, in0=p, scalar=1 / k, in1=y2, op0=ALU.add, op1=ALU.mult)
    dve.drain()
    nc.vector.scalar_tensor_tensor(out=p, in0=p, scalar=1.0, in1=y, op0=ALU.add, op1=ALU.mult)
    nc.vector.tensor_scalar(m, lam, -4.0, 0.0, ALU.mult, ALU.max)
    dve.drain()
    nc.vector.scalar_tensor_tensor(out=lam, in0=p, scalar=8.0, in1=m, op0=ALU.mult, op1=ALU.add)
    dve.drain()


def b_vector(S, dve):
    nc = S.nc
    col = lambda c: S.curB[:, c:c + 1]
    stt = nc.vector.scalar_tensor_tensor
    dve.drain()
    for j in range(KT):
        nc.vector.tensor_tensor(seq(S.res, j), seq(S.xh, j).bitcast(F32), seq(S.xl, j).bitcast(F32),
                                ALU.add).then_inc(S.res_ready, 1)
    dve.wait_ge(S.pb_landed, 16)
    with dve.Fori(0, DEPTH) as L:
        nc.vector.tensor_copy(S.curB[:, :], cols(S.prmB, L, PB_N))
        for t, w, pad in ((S.uc, UC_W, CONV_K - 1), (S.up, UP_W, LRU_K - 1)):
            for j in range(4):
                nc.vector.memset(t[:, j * w:j * w + pad], 0.0)
        dve.drain()
        half = S.curB[:, PB_BG:PB_LAM]
        nc.vector.tensor_scalar(half, half, 0.5, None, ALU.mult)
        lam = S.curB[:, PB_LAM:PB_LAM + 4]
        stt(out=S.lam[0][:, :], in0=lam, scalar=-1.0, in1=lam, op0=ALU.mult, op1=ALU.min).then_inc(S.lam_in, 1)
        rms_dve(S, dve, L)
        b_rope_tables(S, dve, L)
        b_softplus(S, dve, L)
        for j in range(4):
            u = B_GB + j
            dve.wait_ge(S.bank_free[u % SLOTS], GB(L, u) + 2)
            t = S.uc[:, j * UC_W + CONV_K - 1:(j + 1) * UC_W]
            stt(out=t, in0=S.wk[6 + j % 2][:, :], scalar=1.0, in1=t, op0=ALU.add, op1=ALU.mult).then_inc(S.glu_done, 1)
        for k in range(LRU_K):
            for t in range(4):
                src, o, w = S.up[:, t * UP_W + k:t * UP_W + k + SEQ], seq(S.xc, t), col(PB_LCW + t * LRU_K + k)
                if k == 0:
                    dve.wait_ge(S.bank_free[t], GB(L, B_U + t) + 2)
                    nc.vector.tensor_scalar(o, src, w, col(PB_LCB + t), ALU.mult, ALU.add)
                else:
                    stt(out=o, in0=src, scalar=w, in1=o, op0=ALU.mult, op1=ALU.add)
            dve.drain()
        for t in range(4):
            nc.vector.tensor_scalar(seq(S.cacc, t), S.uc[:, t * UC_W:t * UC_W + SEQ], col(PB_DW + t * CONV_K), col(PB_DWB + t),
                                    ALU.mult, ALU.add)
        dve.drain()
        with dve.Fori(0, (CONV_K - 1) // 3) as i:
            for k in range(1, 4):
                for t in range(4):
                    stt(out=seq(S.cacc, t), in0=S.uc[:, bass.ds(i * 3 + (k + t * UC_W), SEQ)],
                        scalar=S.curB[:, bass.ds(i * 3 + (k + PB_DW + t * CONV_K), 1)], in1=seq(S.cacc, t), op0=ALU.mult, op1=ALU.add)
                dve.drain()
        dve.wait_ge(S.bvt_ready, L * 3 + 3)
        nc.vector.tensor_scalar(S.gate[:, :].rearrange("p (b c) -> p b c", b=QB),
                                S.X[2][:, :].rearrange("p (b c) -> p b c", b=QB)[:, :, 0:3 * B_HEADS], 1.0, 0.5,
                                ALU.add, ALU.mult).then_inc(S.gl_done, 1)
        nc.vector.memset(S.tick[:, 28:29], 0.0).then_inc(S.dw_done, 1)
        dve.wait_ge(S.tab_ready, L + 1)
        for n, t in enumerate(rope_tiles(S)):
            a, b = S.wk[4 + n % 2][:, :], S.wk[6 + n % 2][:, :]
            nc.vector.tensor_tensor(a, t, S.cos[:, :], ALU.mult)
            dve.wait_ge(S.b_rot_ready, L * NROPE + n + 1)
            nc.vector.tensor_tensor(b, S.X[n % 2][:, :], S.sin[:, :], ALU.mult)
            dve.drain()
            nc.vector.tensor_tensor(t, a, b, ALU.add).then_inc(S.b_rope_done, 1)
        dve.wait_ge(S.cl_mean, L + 1)
        for t in range(4):
            stt(out=seq(S.cacc, t), in0=S.X[2][:, :], scalar=-2.0, in1=seq(S.cacc, t), op0=ALU.mult, op1=ALU.add).then_inc(S.cl_d, 1)
        dve.wait_ge(S.unit_done[(B_BD - 1) % SLOTS], GB(L, B_BD - 1) + 1)
        for kv in range(2):
            dve.wait_ge(S.blk_raw[kv], L + 1)
            t = S.blk[kv][:, :].rearrange("p (a n) -> p a n", a=16)
            pos = S.curB[:, PB_POS + 16 * kv:PB_POS + 16 * kv + 16]
            c = (4 + 2 * kv) * SEQ
            bh, bl = S.xh[:, c:c + 16 * NB2], S.xl[:, c:c + 16 * NB2]
            nc.vector.tensor_tensor(t, t, pos.unsqueeze(2).to_broadcast([P, 16, NB2]), ALU.add)
            dve.drain()
            nc.vector.tensor_copy(bh, S.blk[kv][:, :])
            dve.drain()
            nc.vector.tensor_tensor(bl, S.blk[kv][:, :], bh.bitcast(F32), ALU.subtract).then_inc(S.blk_ready, 1)
        dve.wait_ge(S.lru_gate, L * 4 + 4)
        free_bank(S, dve, B_BD)
        for t in range(4):
            m = nc.vector.tensor_scalar(seq(S.la, t), seq(S.la, t), 1.0, col(PB_LAM + t), ALU.add, ALU.mult)
        m.then_inc(S.nla_ready, 1)
        stt(out=S.lri[:, :], in0=S.lri[:, :], scalar=1.0, in1=S.xc[:, :], op0=ALU.add, op1=ALU.mult)
        nc.vector.memset(S.kcb[:, :], 0.0)
        nc.vector.memset(S.vbd[:, :], 0.0)
        dve.drain()
        def split_hidden(kv):
            dve.wait_ge(S.hid_turned, L * 2 + kv + 1)
            for u in range(4):
                free_bank(S, dve, B_CMP1 + 4 * kv + u)
            h = S.X[2 + kv][:, 0:2 * HD].rearrange("p (m n) -> p m n", m=2)[:, :, 0:NB2]
            if kv == 0:
                hh, hl = (t[:, :].rearrange("p (m n) -> p m n", m=2) for t in (S.hkh, S.hkl))
                nc.vector.tensor_copy(hh, h)
                dve.drain()
                nc.vector.tensor_tensor(hl, h, hh.bitcast(F32), ALU.subtract).then_inc(S.hid_split, 1)
            else:
                nc.vector.memset(S.hvh[:, :].bitcast(F32), 0.0)
                nc.vector.memset(S.hvl[:, :].bitcast(F32), 0.0)
                dve.drain()
                rep = lambda x, i: x[:, i * P:(i + 1) * P].rearrange("p (j n) -> p j n", j=4)[:, :, 0:NBLK]
                one = lambda i: h[:, i // 2, (i % 2) * NBLK:(i % 2 + 1) * NBLK].unsqueeze(1).to_broadcast([P, 4, NBLK])
                for i in range(4):
                    nc.vector.tensor_copy(rep(S.hvh, i), one(i))
                dve.drain()
                for i in range(4):
                    m = nc.vector.tensor_tensor(rep(S.hvl, i), one(i), rep(S.hvh, i).bitcast(F32), ALU.subtract)
                m.then_inc(S.hid_split, 1)

        dve.wait_ge(S.a_ready, L + 1)
        nc.vector.tensor_tensor(S.lrt[:, :], S.la[:, :], S.la[:, :], ALU.mult)
        dve.drain()
        stt(out=S.ls[:, :], in0=S.lrt[:, :], scalar=1.0, in1=S.ls[:, :], op0=ALU.add, op1=ALU.mult).then_inc(S.b2_ready, 1)
        dve.wait_ge(S.cl_std, L + 1)
        nc.vector.reciprocal(S.wk[3][:, :], S.wk[3][:, :])
        dve.drain()
        for t in range(4):
            nc.vector.tensor_tensor(seq(S.cacc, t), seq(S.cacc, t), S.wk[3][:, :], ALU.mult)
        dve.drain()
        for t in range(4):
            nc.vector.tensor_scalar(seq(S.cacc, t), seq(S.cacc, t), col(PB_LNG + t), col(PB_LNB + t),
                                    ALU.mult, ALU.add).then_inc(S.cl_y, 1)
        split_hidden(0)
        split_hidden(1)
        dve.wait_ge(S.beta_ready, L + 1)
        stt(out=S.lri[:, :], in0=S.lri[:, :], scalar=0.5, in1=S.ls[:, :], op0=ALU.mult, op1=ALU.mult)
        dve.wait_ge(S.unit_done[B_CMP2 % SLOTS], GB(L, B_CMP2) + 1)
        for g in range(2):
            m = nc.vector.tensor_copy(S.kcb[64 * g:64 * g + 64, 32 * g:32 * g + NBLK],
                                      S.X[2][64 * g:64 * g + 64, P + g * NBLK:P + (g + 1) * NBLK])
        m.then_inc(S.kcb_ready, 1)
        dve.drain()
        for t in range(4):
            m = nc.vector.tensor_tensor_scan(seq(S.lrt, t), seq(S.la, t), seq(S.lri, t), 0.0, ALU.mult, ALU.add)
        m.then_inc(S.lru_scanned, 1)
        dve.wait_ge(S.unit_done[(B_CMP2 + 1) % SLOTS], GB(L, B_CMP2 + 1) + 1)
        for g in range(2):
            for t in range(4):
                m = nc.vector.tensor_copy(S.vbd[32 * t:32 * t + 32, (4 * g + t) * HD:(4 * g + t + 1) * HD],
                                          S.X[3][32 * t:32 * t + 32, P + g * HD:P + (g + 1) * HD])
        m.then_inc(S.vbd_ready, 1)
        free_bank(S, dve, B_CMP2)
        free_bank(S, dve, B_CMP2 + 1)
        for h in range(2):
            dve.wait_ge(S.cs_ready, L * 2 + h + 1)
            p4 = S.wk[4 + h][:, :].rearrange("p (b t n) -> p b t n", b=2, t=B_HEADS)
            p3 = S.wk[4 + h][:, :].rearrange("p (r n) -> p r n", n=32)
            mask = S.cmask[:, 64 * h:64 * h + 64].rearrange("p (b n) -> p b n", b=2).unsqueeze(2).to_broadcast([P, 2, B_HEADS, 32])
            mx = S.cmx[:, 16 * h:16 * h + 16]
            nc.vector.tensor_tensor(p4, S.X[h][:, :].rearrange("p (b t n) -> p b t n", b=2, t=B_HEADS), mask, ALU.add)
            dve.drain()
            nc.vector.tensor_reduce(mx, p3, AX, ALU.max)
            dve.drain()
            nc.vector.tensor_scalar(mx, mx, NEG / 10, None, ALU.max)
            dve.drain()
            nc.vector.tensor_tensor(p3, p3, mx.unsqueeze(2).to_broadcast([P, 16, 32]), ALU.subtract).then_inc(S.cexp_in, 1)
        for t in range(4):
            dve.wait_ge(S.cl_hi, L * 4 + t + 1)
            nc.vector.tensor_tensor(seq(S.xl, 4 + t), seq(S.cacc, t), seq(S.xh, 4 + t).bitcast(F32), ALU.subtract).then_inc(S.un_ready, 1)
        for h in range(2):
            dve.wait_ge(S.cexp_out, L * 2 + h + 1)
            p3 = S.wk[4 + h][:, :].rearrange("p (r n) -> p r n", n=32)
            sm = S.csum[:, 16 * h:16 * h + 16]
            nc.vector.tensor_reduce(sm, p3, AX, ALU.add)
            dve.drain()
            nc.vector.tensor_scalar(sm, sm, 1e-30, None, ALU.max)
            dve.drain()
            nc.vector.reciprocal(sm, sm)
            dve.drain()
            gate = S.gate[:, 48 * h:48 * h + 48].rearrange("p (r c) -> p r c", c=3)[:, :, 0]
            nc.vector.tensor_tensor(sm, sm, gate, ALU.mult)
            dve.drain()
            nc.vector.tensor_tensor(p3, p3, sm.unsqueeze(2).to_broadcast([P, 16, 32]), ALU.mult).then_inc(S.cp_ready, 1)
        for n in range(4):
            e = 1 - n % 2
            m = nc.vector.memset(S.wk[n][64 * e:64 * e + 64, :], 0.0)
        m.then_inc(S.q_zero, 1)
        for b in range(QB):
            dve.wait_ge(S.oc_ready, L * 4 + b + 1)
            nc.vector.tensor_copy(S.ot2[:, b * 512:(b + 1) * 512], S.X[b % 2][:, :]).then_inc(S.oc_done, 1)
        for d in range(2):
            u = B_PW2 + d
            s = u % SLOTS
            dve.wait_ge(S.unit_done[s], GB(L, u) + 1)
            nc.vector.tensor_tensor(seq(S.zc, 2 * d), seq(S.zc, 2 * d), S.ps[s][:, :], ALU.mult).then_inc(S.mc_y, 1)
            nc.vector.tensor_tensor(seq(S.zc, 2 * d + 1), seq(S.zc, 2 * d + 1), partner(S, u)[:, :], ALU.mult).then_inc(S.mc_y, 1)
            dve.drain()
            free_bank(S, dve, u)

        with dve.Fori(0, 2) as i:
            attn_dve(S, dve, S.nsa, L * 64 + i * 32, nsa_steps(S, L, i),
                     lambda n: n and n % 4 == 0 and out_add(S, dve, L, i, *divmod(n // 4 - 1, 2)))
            out_add(S, dve, L, i, 3, 1)
            dve.drain()
        for k in range(4):
            dve.wait_ge(S.bt_ready, L * 4 + k + 1)
            nc.vector.tensor_tensor(seq(S.zn, k), seq(S.zn, k), S.X[k][:, :], ALU.mult).then_inc(S.mn_y, 1)
        for k in range(4):
            dve.wait_ge(S.mn_hi, L * 4 + k + 1)
            nc.vector.tensor_tensor(seq(S.mnl, k), seq(S.zn, k), seq(S.mnh, k).bitcast(F32), ALU.subtract).then_inc(S.mn_ready, 1)
        for j in range(4):
            s = (B_OUTN + j) % SLOTS
            dve.wait_ge(S.unit_done[s], GB(L, B_OUTN + j) + 1)
            nc.vector.tensor_tensor(seq(S.res, 2 * j), seq(S.res, 2 * j), S.ps[s][:, :], ALU.add).then_inc(S.res_ready, 1)
            nc.vector.tensor_tensor(seq(S.res, 2 * j + 1), seq(S.res, 2 * j + 1), partner(S, B_OUTN + j)[:, :],
                                    ALU.add).then_inc(S.res_ready, 1)
            free_bank(S, dve, B_OUTN + j)
    dve.wait_ge(S.rms_std, DEPTH + 1)
    nc.vector.reciprocal(S.wk[3][:, :], S.wk[2][:, :])
    dve.drain()
    for j in range(KT):
        stt(out=seq(S.res, j), in0=seq(S.res, j), scalar=S.prmB[:, PB_FINAL + j:PB_FINAL + j + 1], in1=S.wk[3][:, :],
            op0=ALU.mult, op1=ALU.mult).then_inc(S.y_done, 1)


def prime(S, dve, sems):
    for n, sm in enumerate([sm for sm, times in sems for _ in range(times)]):
        S.nc.vector.memset(S.tick[:, n:n + 1], 0.0).then_inc(sm, 1)


def setup_sync(S, sp, T):
    for dst, src in ((S.con, T["con"]), (S.cos, T["cos"]), (S.sin, T["sin"]), (S.prmA, T["prm_a"]), (S.t, T["x"]), (S.cmask, T["cmask"])):
        sp.dma_start(dst[:, :], src).then_inc(S.con_landed, 16)


def setup_vector(S, dve):
    nc = S.nc
    prime(S, dve, [(b, 1) for b in S.bank_free] + [(S.stk_oev, 1), (S.first_added, 1), (S.mc_ready, 1), (S.merge_x, 2), (S.ffn_h, 2), (S.y_ready, 2),
                                                   (S.fox.out, 2), (S.dsa.out, 2), (S.nsa.out, 2)])
    nc.vector.memset(S.ones[:, :], 1.0 / D)
    nc.vector.memset(S.negones[:, :], -1.0)
    nc.vector.memset(S.eps[:, :], LN_EPS)
    nc.vector.memset(S.eps2[:, :], RMS_EPS)
    nc.vector.memset(S.halfpi[:, :], math.pi / 2)
    nc.vector.memset(S.tiny[:, :], 1e-30)
    dve.wait_ge(S.con_landed, 16 * 6)
    for dst, c in ((S.idb, C_ID), (S.causb, C_CAUS), (S.strictb, C_STRICT), (S.chunkb, C_CHUNK)):
        nc.vector.tensor_copy(dst[:, :], S.con[:, c:c + P])
    nc.vector.tensor_copy(S.xh[:, :], S.t[:, :])
    dve.drain()
    for k in range(KT):
        nc.vector.tensor_tensor(S.xl[:, k * SEQ:(k + 1) * SEQ], S.t[:, k * SEQ:(k + 1) * SEQ],
                                S.xh[:, k * SEQ:(k + 1) * SEQ].bitcast(F32), ALU.subtract).then_inc(S.x_ready, 1)


def program(nc, T, out):
    with ExitStack() as ctx:
        S = plan(nc, ctx)
        groups = T["w"].shape[0] // SLOTS
        block = ctx.enter_context(nc.Block())

        @block.sync
        def _(sp):
            setup_sync(S, sp, T)
            sp_stream(S, sp, T["w"], groups)
            for j in range(KT):
                sp.wait_ge(S.y_done, j + 1)
                sp.dma_start(out[:, j * SEQ:(j + 1) * SEQ], seq(S.res, j)).then_inc(S.out_done, 16)
            sp.wait_ge(S.out_done, 16 * KT)

        @block.gpsimd
        def _(pool):
            pool_program(S, pool)

        @block.tensor
        def _(pe):
            a_tensor(S, pe)
            b_tensor(S, pe)

        @block.scalar
        def _(act):
            a_scalar(S, act, T["p"])
            b_scalar(S, act, T)

        @block.vector
        def _(dve):
            setup_vector(S, dve)
            a_vector(S, dve)
            b_vector(S, dve)


def feature_major(a):
    n, f = a.shape
    return np.ascontiguousarray(a.reshape(n, f // P, P).transpose(2, 1, 0).reshape(P, -1))


def unit_of(w):
    return w.reshape(KT, P, P).transpose(1, 0, 2).reshape(P, KT * P)


def units_of(w):
    return [unit_of(w[:, c:c + P]) for c in range(0, w.shape[1], P)]


def units_a(a, l):
    w = np.asarray(a["w_in"][l])
    sizes = (384, 384, 384, 6, 320, 320, 320, 320, 64, 64, 512, 64, 8, 3 * D)
    at = np.cumsum((0,) + sizes)
    fq, fk, fv, ff, sq, sk, sv, dq, dk, dv, iq, ik, iw, g = (w[:, at[n]:at[n + 1]] for n in range(14))
    zero = lambda n: np.zeros((D, n), w.dtype)
    cat = lambda *x: np.concatenate(x, axis=1)
    proj = cat(fv, sv[:, :256], sv[:, 256:], dv, fq, fk, sq[:, :256], sk[:, :256],
               ik, ff, zero(2), iw, zero(16), ff, zero(26), sq[:, 256:], dq[:, 256:], sk[:, 256:], dk, dk, ik,
               dq[:, :256], iq)
    up = np.concatenate([np.asarray(a[k][l]) for k in ("w_up_fox", "w_up_sb", "w_up_dsa")], axis=0)
    fin, fout = np.asarray(a["w_ff_in"][l]), np.asarray(a["w_ff_out"][l])
    ffn = [m for q in range(4) for m in units_of(fin[:, q * D:(q + 1) * D]) + units_of(fout[q * D:(q + 1) * D])]
    ple = np.asarray(a["w_ple"][l]).reshape(2, P, 2, 4, P).transpose(2, 1, 3, 0, 4).reshape(2, P, KT * P)
    all_ = (units_of(proj) + units_of(g) + units_of(up) + units_of(np.asarray(a["w_out"][l])) + list(ple) + ffn
            + units_of(np.asarray(a["w_ple_gate"][l])))
    assert len(all_) == A_UNITS
    return all_


def units_b(a, l):
    w = np.asarray(a["w_in_2"][l])
    sizes = (512, 128, 128, 128, 128, 128, 128, 24, 512, 512, 512, 512, 512, 512)
    at = np.cumsum((0,) + sizes)
    q, kc, vc, ks, vs, kw, vw, gl, zn, ul, zl, ga, gb, zc = (w[:, at[n]:at[n + 1]] for n in range(14))
    q = q.reshape(D, 2, B_REP, HD).transpose(0, 2, 1, 3).reshape(D, 512)
    gl = np.concatenate([gl, np.zeros((D, P - 24), w.dtype)], axis=1)
    plain = units_of(np.concatenate([ga, gb, ul, kc, ks, kw, vc, vs, vw, gl, q, zl, zc, zn], axis=1))
    bd = np.zeros((KT, P, P), w.dtype)
    for t in range(4):
        for d, name in enumerate(("lru_w_a_2", "lru_w_i_2")):
            for e in range(2):
                bd[2 * t + d, 64 * e:64 * e + 64, 64 * e:64 * e + 64] = np.asarray(a[name])[l, 2 * t + e]
    w1, w2 = np.asarray(a["cmp_w1_2"][l]), np.asarray(a["cmp_w2_2"][l])
    c1 = [w1[kv, q * 4 * P:(q + 1) * 4 * P].reshape(4, P, 256).transpose(1, 0, 2).reshape(P, KT * P) for kv in range(2) for q in range(4)]
    c2 = np.zeros((2, D, P), w.dtype)
    c2[0, 0:256] = np.concatenate([w2[0], w2[0]], axis=1)
    c2[1, 0:256, 0:HD] = w2[1]

    def pairs(m):
        return [np.concatenate([unit4(m[:, c + o * P:c + (o + 1) * P]) for o in range(2)], axis=1)
                for c in range(0, m.shape[1], 2 * P)]

    def unit4(m):
        return m.reshape(4, P, P).transpose(1, 0, 2).reshape(P, 4 * P)

    wo = np.asarray(a["w_out_2"][l])
    all_ = (plain + [bd.transpose(1, 0, 2).reshape(P, KT * P)] + c1 + [unit_of(c2[0]), unit_of(c2[1])]
            + pairs(np.asarray(a["conv_w_pw2_2"][l])) + pairs(wo[512:1024]) + pairs(wo[1024:]) + pairs(wo[:512]))
    assert len(all_) == B_UNITS
    return all_


def params_b(a):
    out = np.zeros((P, SEQ), np.float32)

    def tiles(v, n):
        return np.asarray(v).reshape(n, P).T

    for l in range(DEPTH):
        c = out[:, l * PB_N:(l + 1) * PB_N]
        c[:, PB_G:PB_G + KT] = tiles(a["norm_g_2"][l], KT)
        c[0:3 * B_HEADS, PB_BG] = np.asarray(a["b_gate_2"][l])
        for at, name in ((PB_BA, "lru_b_a_2"), (PB_BI, "lru_b_i_2"), (PB_LAM, "lru_lam_2"), (PB_LCB, "lru_conv_b_2"),
                         (PB_DWB, "conv_dw_b_2"), (PB_LNG, "conv_ln_g_2"), (PB_LNB, "conv_ln_b_2")):
            c[:, at:at + 4] = tiles(a[name][l], 4)
        c[:, PB_LCW:PB_LCW + 16] = np.asarray(a["lru_conv_w_2"][l]).reshape(LRU_K, 4, P).transpose(2, 1, 0).reshape(P, -1)
        c[:, PB_DW:PB_DW + 4 * CONV_K] = np.asarray(a["conv_dw_w_2"][l]).reshape(CONV_K, 4, P).transpose(2, 1, 0).reshape(P, -1)
        c[:, PB_POS:PB_POS + 32] = np.asarray(a["cmp_pos_2"][l]).reshape(32, P).T
    out[:, PB_FINAL:PB_FINAL + KT] = tiles(a["final_g_2"], KT)
    out[:, PB_INV] = np.tile(np.float32(10000.0) ** (-np.arange(0, HD, 2, dtype=np.float32) / np.float32(HD)), 4)
    return out


def cmp_mask():
    t = np.arange(P)[:, None, None] + P * np.arange(QB)[None, :, None]
    n = np.arange(32)[None, None, :]
    return np.where((16 * n + 31 <= t) & (n < NBLK), 0.0, NEG).astype(np.float32).reshape(P, QB * 32)


def constants():
    c = np.zeros((P, C_N), np.float32)
    i, j = np.arange(P)[:, None], np.arange(P)[None, :]
    c[:, C_ID:C_ID + P] = i == j
    half, same = HD // 2, i // HD == j // HD
    c[:, C_ROT:C_ROT + P] = np.where(same & (i == j + half), -1.0, np.where(same & (i == j - half), 1.0, 0.0))
    c[:, C_TRI:C_TRI + P] = np.where(i >= j, -1.0, 0.0)
    c[:, C_CAUS:C_CAUS + P] = np.where(j > i, NEG, 0.0)
    c[:, C_STRICT:C_STRICT + P] = np.where(i >= j, NEG, 0.0)
    c[:, C_ST01:C_ST01 + P] = i < j
    c[:, C_CHUNK:C_CHUNK + P] = np.where(j // 64 > i // 64, NEG, 0.0)
    for h in range(6):
        c[96 + h, C_QA + h] = 1.0
        c[64 + h, C_QB + h] = 1.0
    c[64:96, C_KA] = -1.0
    c[96:, C_KB] = 1.0
    return c


def rope_constants():
    inv = np.float32(10000.0) ** (-np.arange(32, dtype=np.float32) / np.float32(32))
    ang = (np.arange(SEQ, dtype=np.float32)[:, None] * inv[None, :]).astype(np.float32)
    rep = lambda t: np.ascontiguousarray(np.tile(t.T, (4, 1)).astype(np.float32))
    return rep(np.cos(ang)), rep(np.sin(ang))


def arrays_of(a):
    prm = np.zeros((P, DEPTH, PA_N), np.float32)
    for l in range(DEPTH):
        for c, name in ((PA_G1, "ln1_g"), (PA_B1, "ln1_b"), (PA_G2, "ln2_g"), (PA_B2, "ln2_b")):
            prm[:, l, c:c + KT] = np.asarray(a[name][l]).reshape(KT, P).T
        prm[64:70, l, PA_BF] = np.asarray(a["b_forget"][l])
        prm[96:102, l, PA_BF] = np.asarray(a["b_forget"][l])
    cos, sin = rope_constants()
    units = [u for l in range(DEPTH) for u in units_a(a, l)] + [u for l in range(DEPTH) for u in units_b(a, l)]
    units += [np.zeros((P, KT * P), np.float32)] * SLOTS
    return {
        "x": feature_major(np.asarray(a["x"])[0]),
        "p": np.stack([feature_major(np.asarray(a["p"])[l, 0]) for l in range(DEPTH)]),
        "w": np.stack(units), "con": constants(), "cos": cos, "sin": sin, "prm_a": prm.reshape(P, -1),
        "prm_b": params_b(a), "cmask": cmp_mask(), "pos": np.asarray(a["positions_2"]),
    }


def kernel(**inputs):
    import concourse.bacc as bacc
    from concourse.bass_utils import run_bass_kernel_spmd

    nc = bacc.Bacc("TRN2", target_bir_lowering=False, num_devices=1)
    arrays = arrays_of(inputs)
    T = {k: nc.dram_tensor(k, v.shape, mybir.dt.from_np(v.dtype), kind="ExternalInput").ap() for k, v in arrays.items()}
    out = nc.dram_tensor("out", (P, KT * SEQ), F32, kind="ExternalOutput").ap()
    program(nc, T, out)
    r = run_bass_kernel_spmd(nc, [arrays], core_ids=[0])
    y = np.asarray(r.results[0]["out"]).reshape(P, KT, SEQ)
    return np.ascontiguousarray(y.transpose(2, 1, 0).reshape(1, SEQ, D))
```
